# Optimizing a Trainium2 kernel written in Bass

```python
import jax, jax.numpy as jnp
from jax import lax
import numpy as np
import math

D_MODEL = 1024
BATCH = 1
SEQ = 512
DEPTH = 2

CHUNK = 64
N_META = 16
N_EVEN = (DEPTH + 1) // 2
N_ODD = DEPTH // 2
EPS = 1e-6
D_FF = 4 * D_MODEL

HG_HEADS = 4
HG_K = 128
HG_V = (D_MODEL // 2) // HG_HEADS
HG_KW = HG_HEADS * HG_K
HG_VW = HG_HEADS * HG_V

MLA_HEADS = 4
NOPE = 128
ROPE = 64
V_DIM = (D_MODEL // 2) // MLA_HEADS
QK_DIM = NOPE + ROPE
Q_RANK = 256
KV_RANK = 256
ROPE_THETA = 10000.0
Q_BLOCK = 128

IN_SPLITS = (HG_KW, 2 * HG_KW, 2 * HG_KW + HG_VW, 2 * HG_KW + 2 * HG_VW,
             2 * HG_KW + 2 * HG_VW + Q_RANK, 2 * HG_KW + 2 * HG_VW + Q_RANK + KV_RANK)
IN_COLS = 2 * HG_KW + 2 * HG_VW + Q_RANK + KV_RANK + ROPE

POOL_WINDOWS = (2, 4, 8, 16)
POOL_GROUPS = len(POOL_WINDOWS)
POOL_G = D_MODEL // POOL_GROUPS


def rmsnorm(x, g):
    xf = x.astype(jnp.float32)
    y = xf * lax.rsqrt(jnp.mean(xf * xf, axis=-1, keepdims=True) + EPS)
    return (y * g.astype(jnp.float32)).astype(x.dtype)

def chunk_ids(L):
    p = jnp.arange(L)
    return jnp.where(p < N_META, 0, 1 + (p - N_META) // CHUNK)

def rope_tables(L):
    half = ROPE // 2
    inv = ROPE_THETA ** (-jnp.arange(half, dtype=jnp.float32) / half)
    ang = jnp.arange(L, dtype=jnp.float32)[:, None] * inv[None, :]
    return jnp.cos(ang), jnp.sin(ang)

def rope_tail(x, cos, sin):
    xn, xr = x[..., :NOPE], x[..., NOPE:]
    x1, x2 = xr[..., :ROPE // 2], xr[..., ROPE // 2:]
    c = cos[None, :, None, :].astype(x.dtype)
    s = sin[None, :, None, :].astype(x.dtype)
    return jnp.concatenate([xn, x1 * c - x2 * s, x2 * c + x1 * s], axis=-1)

def hgrn2_chunk_scan(q, k, v, log_f):
    B, L, H, K = q.shape
    lead = CHUNK - N_META
    tail = (-(L + lead)) % CHUNK
    nc = (L + lead + tail) // CHUNK

    def to_chunks(a):
        a = jnp.pad(a.astype(jnp.float32), ((0, 0), (lead, tail), (0, 0), (0, 0)))
        return a.reshape(B, nc, CHUNK, H, a.shape[-1]).transpose(1, 0, 3, 2, 4)

    qc, kc, vc, gc = to_chunks(q), to_chunks(k), to_chunks(v), to_chunks(log_f)
    tri = jnp.tril(jnp.ones((CHUNK, CHUNK), dtype=bool))[:, :, None]

    def step(S, inp):
        qi, ki, vi, gi = inp
        b = jnp.cumsum(gi, axis=2)
        o_inter = jnp.einsum('bhtk,bhkv->bhtv', qi * jnp.exp(b), S)
        diff = b[:, :, :, None, :] - b[:, :, None, :, :]
        dec = jnp.exp(jnp.where(tri, diff, -jnp.inf))
        att = jnp.einsum('bhtk,bhtsk,bhsk->bhts', qi, dec, ki)
        o_intra = jnp.einsum('bhts,bhsv->bhtv', att, vi)
        b_last = b[:, :, -1:, :]
        S_new = jnp.exp(b_last[:, :, 0, :])[..., None] * S + jnp.einsum(
            'bhsk,bhsv->bhkv', ki * jnp.exp(b_last - b), vi)
        return S_new, o_inter + o_intra

    S0 = jnp.zeros((B, H, K, v.shape[-1]), jnp.float32)
    _, o = lax.scan(step, S0, (qc, kc, vc, gc))
    o = o.transpose(1, 0, 3, 2, 4).reshape(B, nc * CHUNK, H, -1)
    return o[:, lead:lead + L]

def hgrn2_mixer(hq, hf, hi, hg, lb, out_gain):
    B, L, _ = hq.shape
    lb = lb.astype(jnp.float32)
    log_f = jnp.logaddexp(jnp.log(lb), jnp.log1p(-lb) + jax.nn.log_sigmoid(hf.astype(jnp.float32)))
    k = -jnp.expm1(log_f)
    q = jax.nn.silu(hq.astype(jnp.float32))
    o = hgrn2_chunk_scan(q.reshape(B, L, HG_HEADS, HG_K), k.reshape(B, L, HG_HEADS, HG_K),
                         hi.reshape(B, L, HG_HEADS, HG_V), log_f.reshape(B, L, HG_HEADS, HG_K))
    o = rmsnorm(o, out_gain) * jax.nn.silu(hg.reshape(B, L, HG_HEADS, HG_V).astype(jnp.float32))
    return o.reshape(B, L, HG_VW).astype(hq.dtype)

def block_causal_attention(q, k, v, cid):
    B, L, H, Dq = q.shape
    nq = -(-L // Q_BLOCK)
    pad = nq * Q_BLOCK - L
    qp = jnp.pad(q, ((0, 0), (0, pad), (0, 0), (0, 0)))
    qb = qp.reshape(B, nq, Q_BLOCK, H, Dq).transpose(1, 0, 2, 3, 4)
    qcid = jnp.pad(cid, (0, pad), constant_values=L).reshape(nq, Q_BLOCK)
    scale = Dq ** -0.5

    def one_block(args):
        qblk, qc = args
        s = jnp.einsum('bqhd,bkhd->bhqk', qblk, k).astype(jnp.float32) * scale
        mask = cid[None, :] <= qc[:, None]
        p = jax.nn.softmax(jnp.where(mask, s, -jnp.inf), axis=-1).astype(v.dtype)
        return jnp.einsum('bhqk,bkhd->bqhd', p, v)

    out = lax.map(one_block, (qb, qcid))
    out = out.transpose(1, 0, 2, 3, 4).reshape(B, nq * Q_BLOCK, H, v.shape[-1])
    return out[:, :L]

def mla_mixer(cq, ckv, kr, qa_g, kva_g, w_q_up, w_kv_up, qn_g, kn_g, cos, sin, cid):
    B, L, _ = cq.shape
    q = jnp.einsum('blr,re->ble', rmsnorm(cq, qa_g), w_q_up).reshape(B, L, MLA_HEADS, QK_DIM)
    kv = jnp.einsum('blr,re->ble', rmsnorm(ckv, kva_g), w_kv_up).reshape(B, L, MLA_HEADS, NOPE + V_DIM)
    k_nope, v = kv[..., :NOPE], kv[..., NOPE:]
    k = jnp.concatenate([k_nope, jnp.broadcast_to(kr[:, :, None, :], (B, L, MLA_HEADS, ROPE))], axis=-1)
    q = rope_tail(rmsnorm(q, qn_g), cos, sin)
    k = rope_tail(rmsnorm(k, kn_g), cos, sin)
    o = block_causal_attention(q, k, v, cid)
    return o.reshape(B, L, MLA_HEADS * V_DIM)

def multiscale_pool(h, w_groups, scale):
    B, L, D = h.shape
    hf = h.astype(jnp.float32).reshape(B, L, POOL_GROUPS, POOL_G)
    t = jnp.arange(L, dtype=jnp.float32)
    diffs = []
    for gi, w in enumerate(POOL_WINDOWS):
        c = jnp.pad(jnp.cumsum(hf[:, :, gi], axis=1), ((0, 0), (w, 0), (0, 0)))
        win = c[:, w:] - c[:, :L]
        cnt = jnp.minimum(t + 1.0, float(w))[None, :, None]
        diffs.append(win / cnt - hf[:, :, gi])
    d = jnp.stack(diffs, axis=2).astype(h.dtype)
    y = jnp.einsum('blgc,gce->blge', d, w_groups).reshape(B, L, D)
    return y * scale

def squared_relu_mlp(h, w_up, w_down):
    a = jax.nn.relu(jnp.einsum('bld,df->blf', h, w_up))
    return jnp.einsum('blf,fd->bld', a * a, w_down)

def first_inputs(seed: int = 0) -> dict:
    key = jax.random.key(seed)
    ks = jax.random.split(key, 20)
    n = jax.random.normal
    f32 = jnp.float32
    return {
        'x': n(ks[0], (BATCH, SEQ, D_MODEL), f32),
        'meta_tokens': n(ks[1], (N_META, D_MODEL), f32),
        'mix_norm': 1.0 + 0.02 * n(ks[2], (DEPTH, D_MODEL), f32),
        'mlp_norm': 1.0 + 0.02 * n(ks[3], (DEPTH, D_MODEL), f32),
        'w_mlp_up': n(ks[4], (DEPTH, D_MODEL, D_FF), f32) * D_MODEL ** -0.5,
        'w_mlp_down': n(ks[5], (DEPTH, D_FF, D_MODEL), f32) * (0.5 * D_FF ** -0.5),
        'w_in': n(ks[6], (N_EVEN, D_MODEL, IN_COLS), f32) * D_MODEL ** -0.5,
        'hgrn_lb': 0.5 * n(ks[7], (N_EVEN, HG_KW), f32),
        'hgrn_out_norm': 1.0 + 0.02 * n(ks[8], (N_EVEN, HG_V), f32),
        'mla_q_a_norm': 1.0 + 0.02 * n(ks[9], (N_EVEN, Q_RANK), f32),
        'mla_kv_a_norm': 1.0 + 0.02 * n(ks[10], (N_EVEN, KV_RANK), f32),
        'w_q_up': n(ks[11], (N_EVEN, Q_RANK, MLA_HEADS * QK_DIM), f32) * Q_RANK ** -0.5,
        'w_kv_up': n(ks[12], (N_EVEN, KV_RANK, MLA_HEADS * (NOPE + V_DIM)), f32) * KV_RANK ** -0.5,
        'q_norm': 1.0 + 0.02 * n(ks[13], (N_EVEN, QK_DIM), f32),
        'k_norm': 1.0 + 0.02 * n(ks[14], (N_EVEN, QK_DIM), f32),
        'w_out': n(ks[15], (N_EVEN, HG_VW + MLA_HEADS * V_DIM, D_MODEL), f32) * D_MODEL ** -0.5,
        'pool_w': n(ks[16], (N_ODD, POOL_GROUPS, POOL_G, POOL_G), f32) * POOL_G ** -0.5,
        'pool_scale': 1.0 + 0.1 * n(ks[17], (N_ODD, D_MODEL), f32),
    }

def first_block(x, meta_tokens, mix_norm, mlp_norm, w_mlp_up, w_mlp_down, w_in, hgrn_lb,
              hgrn_out_norm, mla_q_a_norm, mla_kv_a_norm, w_q_up, w_kv_up, q_norm, k_norm,
              w_out, pool_w, pool_scale):
    B = x.shape[0]
    meta = jnp.broadcast_to(meta_tokens[None].astype(x.dtype), (B, N_META, D_MODEL))
    h = jnp.concatenate([meta, x], axis=1)
    L = h.shape[1]
    cid = chunk_ids(L)
    cos, sin = rope_tables(L)
    lb_cum = jnp.cumsum(jax.nn.softmax(hgrn_lb.astype(jnp.float32), axis=0), axis=0)
    lower_bounds = lb_cum - lb_cum[0:1]

    for layer in range(DEPTH):
        u = rmsnorm(h, mix_norm[layer])
        if layer % 2 == 0:
            e = layer // 2
            z = jnp.einsum('bld,de->ble', u, w_in[e])
            hq, hf, hi, hg, cq, ckv, kr = jnp.split(z, IN_SPLITS, axis=-1)
            o_a = hgrn2_mixer(hq, hf, hi, hg, lower_bounds[e], hgrn_out_norm[e])
            o_b = mla_mixer(cq, ckv, kr, mla_q_a_norm[e], mla_kv_a_norm[e], w_q_up[e], w_kv_up[e],
                            q_norm[e], k_norm[e], cos, sin, cid)
            mix = jnp.einsum('ble,ed->bld', jnp.concatenate([o_a, o_b], axis=-1), w_out[e])
        else:
            o = layer // 2
            mix = multiscale_pool(u, pool_w[o], pool_scale[o])
        h = h + mix
        h = h + squared_relu_mlp(rmsnorm(h, mlp_norm[layer]), w_mlp_up[layer], w_mlp_down[layer])

    return h[:, N_META:]


DEPTH_2 = 1

A_HEADS = 8
A_HEAD_DIM = 64
A_WIDTH = A_HEADS * A_HEAD_DIM
IDX_HEADS = 8
IDX_DIM = 32
INDEX_TOPK = 256
SPARSE_Q_BLOCK = 64
N_BUCKETS = 32
MAX_DISTANCE = 128

B_HEADS = 4
B_KEY_DIM = 64
B_VAL_DIM = 128
B_KEY_WIDTH = B_HEADS * B_KEY_DIM
B_WIDTH = B_HEADS * B_VAL_DIM
GATE_RANK = 16
GATE_TEMP = 16.0
GLA_CHUNK = 64

MIX_WIDTH = A_WIDTH + B_WIDTH

PROJ_SPLITS = (A_WIDTH, A_WIDTH, A_WIDTH,
               IDX_HEADS * IDX_DIM, IDX_DIM, IDX_HEADS,
               B_KEY_WIDTH, B_KEY_WIDTH, B_WIDTH,
               GATE_RANK, B_WIDTH)
PROJ_WIDTH = 3 * A_WIDTH + IDX_HEADS * IDX_DIM + IDX_DIM + IDX_HEADS + 2 * B_KEY_WIDTH + B_WIDTH + GATE_RANK + B_WIDTH

N_GROUPS = 4
EXPERTS_PER_GROUP = 8
N_EXPERTS = N_GROUPS * EXPERTS_PER_GROUP
EXPERT_TOPK = 2
D_EXPERT = 256


def rmsnorm_2(x, g):
    xf = x.astype(jnp.float32)
    y = xf * lax.rsqrt(jnp.mean(xf * xf, axis=-1, keepdims=True) + EPS)
    return (y * g.astype(jnp.float32)).astype(x.dtype)

def t5_bucket(dist):
    max_exact = N_BUCKETS // 2
    d_f = jnp.maximum(dist, 1).astype(jnp.float32)
    large = max_exact + (jnp.log(d_f / max_exact) / math.log(MAX_DISTANCE / max_exact)
                         * (N_BUCKETS - max_exact)).astype(jnp.int32)
    large = jnp.minimum(large, N_BUCKETS - 1)
    return jnp.where(dist < max_exact, dist, large)

def dsa_attention(q, k, v, iq, ik, iw, rel_bias):
    bsz, s_len = q.shape[0], q.shape[1]
    topk = min(INDEX_TOPK, s_len // 4)
    nb = s_len // SPARSE_Q_BLOCK

    def blocks(a):
        return a.reshape(bsz, nb, SPARSE_Q_BLOCK, *a.shape[2:]).swapaxes(0, 1)

    q_pos = jnp.arange(s_len, dtype=jnp.int32).reshape(nb, SPARSE_Q_BLOCK)
    key_pos = jnp.arange(s_len, dtype=jnp.int32)
    ik_f = ik.astype(jnp.float32)
    gather = jax.vmap(lambda a, i: a[i])

    def one_block(args):
        qb, iqb, iwb, tb = args
        idx_logits = jnp.einsum('bqhd,bsd->bqhs', iqb.astype(jnp.float32), ik_f) * IDX_DIM ** -0.5
        score = jnp.einsum('bqhs,bqh->bqs', jax.nn.relu(idx_logits),
                           iwb.astype(jnp.float32) * IDX_HEADS ** -0.5)
        causal = key_pos[None, :] <= tb[:, None]
        score = jnp.where(causal[None], score, -jnp.inf)
        _, idx = lax.top_k(score, topk)
        valid = idx <= tb[None, :, None]
        k_sel = gather(k, idx)
        v_sel = gather(v, idx)
        logits = jnp.einsum('bqhd,bqkhd->bhqk', qb, k_sel).astype(jnp.float32) * A_HEAD_DIM ** -0.5
        dist = jnp.maximum(tb[None, :, None] - idx, 0)
        bias = rel_bias[t5_bucket(dist)]
        logits = logits + jnp.transpose(bias, (0, 3, 1, 2)).astype(jnp.float32)
        logits = jnp.where(valid[:, None], logits, -jnp.inf)
        p = jax.nn.softmax(logits, axis=-1).astype(v.dtype)
        return jnp.einsum('bhqk,bqkhd->bqhd', p, v_sel)

    out = lax.map(one_block, (blocks(q), blocks(iq), blocks(iw), q_pos))
    return out.swapaxes(0, 1).reshape(bsz, s_len, A_HEADS * A_HEAD_DIM)

def gla_chunked(q, k, v, log_a):
    bsz, s_len, h, dk = q.shape
    dv = v.shape[-1]
    nc = s_len // GLA_CHUNK

    def chunks(a):
        return a.reshape(bsz, nc, GLA_CHUNK, h, a.shape[-1]).transpose(1, 0, 3, 2, 4)

    tri = jnp.tril(jnp.ones((GLA_CHUNK, GLA_CHUNK), dtype=bool))

    def step(state, inp):
        qc, kc, vc, gc = inp
        b = jnp.cumsum(gc, axis=2)
        o_inter = jnp.einsum('bhcd,bhdv->bhcv', qc * jnp.exp(b), state)
        diff = b[:, :, :, None, :] - b[:, :, None, :, :]
        decay = jnp.exp(jnp.where(tri[None, None, :, :, None], diff, -jnp.inf))
        attn = jnp.einsum('bhtd,bhsd,bhtsd->bhts', qc, kc, decay)
        o_intra = jnp.einsum('bhts,bhsv->bhtv', attn, vc)
        b_last = b[:, :, -1:, :]
        state = (jnp.exp(b_last[:, :, 0, :])[..., None] * state
                 + jnp.einsum('bhsd,bhsv->bhdv', kc * jnp.exp(b_last - b), vc))
        return state, o_inter + o_intra

    init = jnp.zeros((bsz, h, dk, dv), jnp.float32)
    _, o = lax.scan(step, init, (chunks(q * dk ** -0.5), chunks(k), chunks(v), chunks(log_a)))
    return o.transpose(1, 0, 3, 2, 4).reshape(bsz, s_len, h, dv)

def hier_moe(h, w_rg, b_rg, w_re, b_re, w_g, w_u, w_d):
    bsz, s_len, d = h.shape
    hf = h.reshape(-1, d)
    g_logits = (hf @ w_rg).astype(jnp.float32) + b_rg.astype(jnp.float32)
    g_prob = jax.nn.softmax(g_logits, axis=-1)
    _, g_sel = lax.top_k(g_logits, 1)
    g_onehot = jax.nn.one_hot(g_sel[:, 0], N_GROUPS, dtype=jnp.float32)
    g_weight = jnp.sum(g_prob * g_onehot, axis=-1, keepdims=True)
    e_logits = ((hf @ w_re).astype(jnp.float32) + b_re.astype(jnp.float32)).reshape(-1, N_GROUPS, EXPERTS_PER_GROUP)
    e_logits_sel = jnp.einsum('nge,ng->ne', e_logits, g_onehot)
    top_val, top_idx = lax.top_k(e_logits_sel, EXPERT_TOPK)
    e_weight = jax.nn.softmax(top_val, axis=-1) * g_weight
    e_idx = g_sel * EXPERTS_PER_GROUP + top_idx
    gates = jnp.sum(jax.nn.one_hot(e_idx, N_EXPERTS, dtype=jnp.float32) * e_weight[..., None], axis=1)
    out = jnp.zeros(hf.shape, jnp.float32)
    for g in range(N_GROUPS):
        sl = slice(g * EXPERTS_PER_GROUP, (g + 1) * EXPERTS_PER_GROUP)
        a = jnp.einsum('nd,edf->nef', hf, w_g[sl])
        u = jnp.einsum('nd,edf->nef', hf, w_u[sl])
        hid = jax.nn.silu(a) * u * gates[:, sl, None].astype(hf.dtype)
        out = out + jnp.einsum('nef,efd->nd', hid, w_d[sl]).astype(jnp.float32)
    return out.astype(h.dtype).reshape(bsz, s_len, d)

def second_inputs(seed: int = 0) -> dict:
    key = jax.random.key(seed)
    ks = jax.random.split(key, 20)
    f32 = jnp.float32
    nrm = lambda k, shape, scale: jax.random.normal(k, shape, f32) * scale
    return {
        "x": nrm(ks[0], (BATCH, SEQ, D_MODEL), 1.0),
        "norm1_g": 1.0 + nrm(ks[1], (DEPTH_2, D_MODEL), 0.01),
        "w_in": nrm(ks[2], (DEPTH_2, D_MODEL, PROJ_WIDTH), D_MODEL ** -0.5),
        "q_norm_g": 1.0 + nrm(ks[3], (DEPTH_2, A_HEAD_DIM), 0.01),
        "k_norm_g": 1.0 + nrm(ks[4], (DEPTH_2, A_HEAD_DIM), 0.01),
        "rel_bias": nrm(ks[5], (N_BUCKETS, A_HEADS), 0.5),
        "gla_gate_w2": nrm(ks[6], (DEPTH_2, GATE_RANK, B_KEY_WIDTH), GATE_RANK ** -0.5),
        "gla_gate_b": nrm(ks[7], (DEPTH_2, B_KEY_WIDTH), 0.1),
        "gla_out_norm_g": 1.0 + nrm(ks[8], (DEPTH_2, B_VAL_DIM), 0.01),
        "w_out": nrm(ks[9], (DEPTH_2, MIX_WIDTH, D_MODEL), MIX_WIDTH ** -0.5),
        "norm2_g": 1.0 + nrm(ks[10], (DEPTH_2, D_MODEL), 0.01),
        "w_router_group": nrm(ks[11], (DEPTH_2, D_MODEL, N_GROUPS), D_MODEL ** -0.5),
        "b_router_group": nrm(ks[12], (DEPTH_2, N_GROUPS), 0.01),
        "w_router_expert": nrm(ks[13], (DEPTH_2, D_MODEL, N_EXPERTS), D_MODEL ** -0.5),
        "b_router_expert": nrm(ks[14], (DEPTH_2, N_EXPERTS), 0.01),
        "w_exp_gate": nrm(ks[15], (DEPTH_2, N_EXPERTS, D_MODEL, D_EXPERT), D_MODEL ** -0.5),
        "w_exp_up": nrm(ks[16], (DEPTH_2, N_EXPERTS, D_MODEL, D_EXPERT), D_MODEL ** -0.5),
        "w_exp_down": nrm(ks[17], (DEPTH_2, N_EXPERTS, D_EXPERT, D_MODEL), D_EXPERT ** -0.5),
    }

def second_block(x, norm1_g, w_in, q_norm_g, k_norm_g, rel_bias, gla_gate_w2, gla_gate_b,
              gla_out_norm_g, w_out, norm2_g, w_router_group, b_router_group,
              w_router_expert, b_router_expert, w_exp_gate, w_exp_up, w_exp_down):
    bsz, s_len, _ = x.shape
    split_points = np.cumsum(PROJ_SPLITS)[:-1].tolist()
    for l in range(DEPTH_2):
        h = rmsnorm_2(x, norm1_g[l])
        proj = h @ w_in[l]
        qa, ka, va, iq, ik, iw, qb, kb, vb, g_lr, r_gate = jnp.split(proj, split_points, axis=-1)

        qa = rmsnorm_2(qa.reshape(bsz, s_len, A_HEADS, A_HEAD_DIM), q_norm_g[l])
        ka = rmsnorm_2(ka.reshape(bsz, s_len, A_HEADS, A_HEAD_DIM), k_norm_g[l])
        va = va.reshape(bsz, s_len, A_HEADS, A_HEAD_DIM)
        o_a = dsa_attention(qa, ka, va, iq.reshape(bsz, s_len, IDX_HEADS, IDX_DIM), ik, iw, rel_bias)

        log_a = jax.nn.log_sigmoid((g_lr @ gla_gate_w2[l]).astype(jnp.float32)
                                   + gla_gate_b[l].astype(jnp.float32)) / GATE_TEMP
        o_b = gla_chunked(qb.reshape(bsz, s_len, B_HEADS, B_KEY_DIM).astype(jnp.float32),
                          kb.reshape(bsz, s_len, B_HEADS, B_KEY_DIM).astype(jnp.float32),
                          vb.reshape(bsz, s_len, B_HEADS, B_VAL_DIM).astype(jnp.float32),
                          log_a.reshape(bsz, s_len, B_HEADS, B_KEY_DIM))
        o_b = rmsnorm_2(o_b, gla_out_norm_g[l]).reshape(bsz, s_len, B_WIDTH).astype(x.dtype) * jax.nn.silu(r_gate)

        x = x + jnp.concatenate([o_a, o_b], axis=-1) @ w_out[l]

        x = x + hier_moe(rmsnorm_2(x, norm2_g[l]), w_router_group[l], b_router_group[l],
                         w_router_expert[l], b_router_expert[l],
                         w_exp_gate[l], w_exp_up[l], w_exp_down[l])
    return x


def setup_inputs(seed=0):
    out = dict(first_inputs(seed))
    for name, value in second_inputs(seed + 1).items():
        if name != "x":
            out[name + "_2"] = value
    return out


def reference(
    x, meta_tokens, mix_norm, mlp_norm, w_mlp_up, w_mlp_down, w_in, hgrn_lb, hgrn_out_norm,
    mla_q_a_norm, mla_kv_a_norm, w_q_up, w_kv_up, q_norm, k_norm, w_out, pool_w, pool_scale,
    norm1_g_2, w_in_2, q_norm_g_2, k_norm_g_2, rel_bias_2, gla_gate_w2_2, gla_gate_b_2,
    gla_out_norm_g_2, w_out_2, norm2_g_2, w_router_group_2, b_router_group_2, w_router_expert_2,
    b_router_expert_2, w_exp_gate_2, w_exp_up_2, w_exp_down_2,
):
    x = first_block(
        x, meta_tokens, mix_norm, mlp_norm, w_mlp_up, w_mlp_down, w_in, hgrn_lb, hgrn_out_norm,
        mla_q_a_norm, mla_kv_a_norm, w_q_up, w_kv_up, q_norm, k_norm, w_out, pool_w, pool_scale,
    )
    return second_block(
        x, norm1_g_2, w_in_2, q_norm_g_2, k_norm_g_2, rel_bias_2, gla_gate_w2_2, gla_gate_b_2,
        gla_out_norm_g_2, w_out_2, norm2_g_2, w_router_group_2, b_router_group_2,
        w_router_expert_2, b_router_expert_2, w_exp_gate_2, w_exp_up_2, w_exp_down_2,
    )


_drawn_inputs = setup_inputs


def setup_inputs(seed=0):
    import zlib

    import numpy as np

    out = dict(_drawn_inputs(seed))
    spreads = {}
    factors = {'hgrn_out_norm': 3.963,
     'mla_q_a_norm': 8.0,
     'mla_kv_a_norm': 6.273,
     'q_norm': 7.853,
     'k_norm': 8.0,
     'norm1_g_2': 4.542,
     'q_norm_g_2': 8.0,
     'k_norm_g_2': 8.0,
     'gla_gate_b_2': 3.396,
     'gla_out_norm_g_2': 6.771,
     'norm2_g_2': 5.343,
     'b_router_group_2': 8.0,
     'b_router_expert_2': 18.685}
    for name, (base, spread) in spreads.items():
        noise = np.random.default_rng([zlib.crc32(name.encode()), seed]).standard_normal(out[name].shape)
        drawn = base * np.exp(spread * noise) if base else spread * noise
        out[name] = __import__('jax').numpy.asarray(drawn.astype(out[name].dtype))
    for name, factor in factors.items():
        out[name] = (out[name] * factor).astype(out[name].dtype)
    return out
```

```python
import math

import numpy as np

P = 128
D = 1024
KT = D // P
SEQ = 512
META = 16
TOK = SEQ + META
CHUNK = 64
D_FF = 4 * D
EPS = 1e-6
HEADS = 4
HDIM = 128
NOPE, ROPE, QK = 128, 64, 192
Q_RANK = KV_RANK = 256
IN_COLS = 4 * 512 + Q_RANK + KV_RANK + ROPE
A_HEADS, A_DIM = 8, 64
IDX_HEADS, IDX_DIM = 8, 32
TOPK = min(256, SEQ // 4)
N_BUCKETS, MAX_DISTANCE = 32, 128
B_KEY = 64
GATE_RANK, GATE_TEMP = 16, 16.0
GROUPS, PER_GROUP, EXPERTS, D_EXPERT = 4, 8, 32, 256
NEG = -1e30
QT = SEQ // P
TILES = [(P * i, P) for i in range(QT)] + [(SEQ, META)]
HALF = TOK // 2
REAL = [(0, SEQ // 2), (SEQ // 2, SEQ // 2)]
HALVES = [(0, HALF), (HALF, HALF)]
LEVELS = (64, 32, 16, 8, 4, 2, 1)

O_QA, O_KA, O_VA, O_IQ = 0, 512, 1024, 1536
O_IK, O_IW, O_QB, O_KB, O_VB, O_LR, O_RG = 1792, 1824, 1832, 2088, 2344, 2856, 2872
PROJ = 3384

GAIN_ROWS = {}
for _n, _c in (("mix0", 8), ("mix1", 8), ("mlp0", 8), ("mlp1", 8), ("norm1", 8), ("norm2", 8), ("pool", 8),
               ("hgrn_out", 1), ("qa", 2), ("kva", 2), ("q_norm", 2), ("k_norm", 2), ("qn2", 1), ("kn2", 1),
               ("gate_b", 2), ("gla_out", 1)):
    GAIN_ROWS[_n] = (sum(c for _, c in GAIN_ROWS.values()), _c)
GAINS = sum(c for _, c in GAIN_ROWS.values())

CONST_COLS = {}
for _n, _c in (("ident", P), ("ones", P), ("pair", P), ("causal", P), ("cos", TOK), ("sin", TOK),
               ("rot", 64), ("eps", 1), ("one", 1), ("half_ind", P), ("neg64", 64), ("scan", TOK), 
               ("onehot", 3 * P), ("slot", CHUNK), ("tri", P), ("tokid", QT), ("eids", EXPERTS), ("down", PER_GROUP)):
    CONST_COLS[_n] = (sum(c for _, c in CONST_COLS.values()), _c)
CONSTS = sum(c for _, c in CONST_COLS.values())


def t5_buckets(n):
    d = np.arange(n)
    exact = N_BUCKETS // 2
    large = exact + (np.log(np.maximum(d, 1).astype(np.float32) / np.float32(exact))
                     / np.float32(math.log(MAX_DISTANCE / exact)) * np.float32(N_BUCKETS - exact)).astype(np.int32)
    return np.where(d < exact, d, np.minimum(large, N_BUCKETS - 1))


def constant_table():
    c = np.zeros((P, CONSTS), np.float32)

    def put(name, a):
        o, n = CONST_COLS[name]
        a = np.asarray(a, np.float32)
        c[:a.shape[0], o:o + n] = a

    i = np.arange(P)
    put("ident", np.eye(P))
    put("ones", np.ones((P, P)))
    put("pair", (i[:, None] // 64 == i[None, :] // 64))
    put("causal", np.where(i[None, :] <= i[:, None], 0.0, NEG))
    pos = np.concatenate([np.arange(SEQ) + META, np.arange(META)]).astype(np.float32)
    half = ROPE // 2
    inv = (np.float32(10000.0) ** (-np.arange(half, dtype=np.float32) / half)).astype(np.float32)
    ang = inv[:, None] * pos[None, :]
    put("cos", np.concatenate([np.cos(ang)] * 2, 0))
    put("sin", np.concatenate([np.sin(ang)] * 2, 0))
    rot = np.zeros((64, 64))
    for j in range(half):
        rot[half + j, j] = -1.0
        rot[j, half + j] = 1.0
    put("rot", rot)
    put("eps", np.full((P, 1), EPS))
    put("one", np.ones((P, 1)))
    put("half_ind", (i[None, :] < 64))
    put("neg64", np.full((1, 64), NEG))
    scan = np.ones(TOK)
    scan[[P * j for j in range(QT)] + [SEQ]] = 0.0
    put("scan", np.tile(scan, (P, 1)))
    b = t5_buckets(2 * P)[np.maximum(2 * P - 1 - np.arange(3 * P), 0)]
    put("onehot", np.arange(N_BUCKETS)[:, None] == b[None, :])
    put("slot", np.tile(np.arange(CHUNK), (P, 1)))
    put("tri", (i[:, None] < i[None, :]))
    put("tokid", i[:, None] + P * np.arange(QT)[None, :])
    put("eids", np.tile(np.arange(EXPERTS), (P, 1)))
    put("down", np.tile(PER_GROUP - np.arange(PER_GROUP), (P, 1)))
    return c


def level_masks():
    s, t = np.arange(P)[:, None], np.arange(P)[None, :]
    masks = [(s // (2 * m) == t // (2 * m)) & (s % (2 * m) < m) & (t % (2 * m) >= m) for m in LEVELS] + [s == t]
    return np.concatenate(masks, 1).astype(np.float32)


class Signal:

    def __init__(self, sem):
        self.sem, self.count = sem, 0

    def by(self, ins, n=1):
        ins.then_inc(self.sem, n)
        self.count += n
        return self.count


def program(nc, t, out):
    from contextlib import ExitStack
    from concourse import bass, mybir

    F32, FR, I32, U32 = mybir.dt.float32, mybir.dt.float32r, mybir.dt.int32, mybir.dt.uint32
    ACT, ALU, AX = mybir.ActivationFunctionType, mybir.AluOpType, mybir.AxisListType.X
    te, ve, se, ge = nc.tensor, nc.vector, nc.scalar, nc.gpsimd

    root = ExitStack()
    signals = {}

    def sig(name):
        if name not in signals:
            signals[name] = Signal(root.enter_context(nc.semaphore(name)))
        return signals[name]

    taken = {}

    def sb(stack, name, shape, dt=F32):
        taken[name] = taken.get(name, 0) + 1
        name += f"_{taken[name]}" if taken[name] > 1 else ""
        return stack.enter_context(nc.sbuf_tensor(name, shape, dt))

    def chained(engine, name):
        s = sig(name)

        def step(ins):
            engine.wait_ge(s.sem, s.by(ins))
        return step

    const = sb(root, "const", [P, CONSTS])
    level_mask = sb(root, "level_mask", [P, P * (len(LEVELS) + 1)], mybir.dt.uint8)
    gains = sb(root, "gains", [P, GAINS])
    hT = sb(root, "hT", [P, KT, TOK])
    rT = sb(root, "rT", [P, TOK])
    NW = 4
    wbuf = [sb(root, f"wbuf{i}", [P, KT, 512]) for i in range(2)] + [None, None]
    banks = root.enter_context(nc.psum_tensor("banks", [P, 8, 512], F32))
    uT = late = None

    def open_late():
        nonlocal uT, late
        late = ExitStack()
        wbuf[2:] = [sb(late, f"wbuf{i}", [P, KT, 512]) for i in (2, 3)]
        uT = sb(late, "uT", [P, KT, TOK])

    def C(name, rows=P, n=None):
        o, w = CONST_COLS[name]
        return const[0:rows, o:o + (n or w)]

    def G(name, j=0, rows=P):
        o = GAIN_ROWS[name][0] + j
        return gains[0:rows, o:o + 1]

    skipped = set()
    jobs = []
    issued = [0]
    w_loaded = [sig(f"w_loaded{i}") for i in range(NW)]
    job_done = {}

    def job(src, rows=D):
        n = src.shape[1]
        jobs.append((rows // P, n, src.rearrange("(k p) n -> p k n", p=P)))
        return len(jobs) - 1

    def issue(sp, upto):
        while issued[0] < min(upto, len(jobs)):
            j = issued[0]
            if jobs[j] is None:
                issued[0] += 1
                continue
            if j >= NW:
                before = max(i for i in range(j % NW, j, NW) if i not in skipped)
                sp.wait_ge(*job_done[before])
            k, n, src = jobs[j]
            w_loaded[j % NW].by(sp.dma_start(wbuf[j % NW][:, 0:k, 0:n], src), 16)
            issued[0] += 1

    ring_loads = [0] * NW

    def loads(j):
        return sum(i not in skipped for i in range(j % NW, j + 1, NW)) + ring_loads[j % NW]

    def weight(pe, j):
        pe.wait_ge(w_loaded[j % NW].sem, 16 * loads(j))
        return wbuf[j % NW]

    def load_input():
        ctx = ExitStack()
        grow = sb(ctx, "grow", [P, P])
        xtok = sb(ctx, "xtok", [P, QT + 1, D])
        mask_f = sb(ctx, "mask_f", [P, P * (len(LEVELS) + 1)])
        c_in, g_in = sig("const_loaded"), sig("gains_loaded")
        x_in = [sig(f"x_loaded{i}") for i in range(QT + 1)]
        g_zero, turned = sig("gains_zeroed"), sig("turned")
        moved = [sig("act_moved"), sig("dve_moved")]

        def move_input(copy, n, s):
            i, c0 = n // 2, 4 * (n % 2)
            col, w = TILES[i]
            s.by(copy(hT[:, c0:c0 + 4, col:col + w],
                      banks[:, n % 8, :].rearrange("p (k t) -> p k t", k=4)[:, :, 0:w]))

        with nc.Block() as block:
            @block.sync
            def _(sp):
                c_in.by(sp.dma_start(const[:], t["constants"]), 16)
                c_in.by(sp.dma_start(mask_f[:], t["level_masks"]), 16)
                for i in range(QT):
                    x_in[i].by(sp.dma_start(xtok[:, i, :], t["x"][0, i * P:(i + 1) * P, :]), 16)
                x_in[QT].by(sp.dma_start(xtok[0:META, QT, :], t["meta_tokens"]), 16)
                issue(sp, NW)

            @block.scalar
            def _(act):
                act.wait_ge(g_zero.sem, 1)
                rows = [("mix0", t["mix_norm"][0:1], 8), ("mix1", t["mix_norm"][1:2], 8),
                        ("mlp0", t["mlp_norm"][0:1], 8), ("mlp1", t["mlp_norm"][1:2], 8),
                        ("norm1", t["norm1_g"], 8), ("norm2", t["norm2_g"], 8), ("pool", t["pool_scale"], 8),
                        ("hgrn_out", t["hgrn_out_norm"], 1), ("qa", t["mla_q_a_norm"], 2),
                        ("kva", t["mla_kv_a_norm"], 2), ("gate_b", t["gla_gate_b"], 2),
                        ("gla_out", t["gla_out_norm_g"], 1)]
                for name, src, n in rows:
                    o = GAIN_ROWS[name][0]
                    g_in.by(act.dma_start(grow[o:o + n, :], src.rearrange("a (k p) -> (a k) p", p=P)), 16)
                for name, src in (("q_norm", t["q_norm"]), ("k_norm", t["k_norm"])):
                    o = GAIN_ROWS[name][0]
                    g_in.by(act.dma_start(grow[o:o + 1, :], src[:, 0:P]), 16)
                    g_in.by(act.dma_start(grow[o + 1:o + 2, 0:ROPE], src[:, P:QK]), 16)
                for name, src in (("qn2", t["q_norm_g"]), ("kn2", t["k_norm_g"])):
                    o = GAIN_ROWS[name][0]
                    for c in (0, A_DIM):
                        g_in.by(act.dma_start(grow[o:o + 1, c:c + A_DIM], src), 16)
                for n in range(0, QT * 2 + 2, 2):
                    act.wait_ge(turned.sem, n + 1)
                    move_input(se.copy, n, moved[0])

            @block.vector
            def _(dve):
                g_zero.by(ve.memset(grow[:], 0.0))
                for n in range(1, QT * 2 + 2, 2):
                    dve.wait_ge(turned.sem, n + 1)
                    move_input(ve.tensor_copy, n, moved[1])
                dve.wait_ge(turned.sem, 2 * QT + 3)
                moved[1].by(ve.tensor_copy(gains[:], banks[:, 2, 0:GAINS]))
                dve.wait_ge(c_in.sem, 32)
                moved[1].by(ve.tensor_copy(level_mask[:], mask_f[:]))

            @block.tensor
            def _(pe):
                pe.wait_ge(c_in.sem, 32)
                for n in range(QT * 2 + 2):
                    i, c0 = n // 2, 4 * (n % 2)
                    w = TILES[i][1]
                    pe.wait_ge(x_in[i].sem, 16)
                    if n >= 8:
                        pe.wait_ge(moved[n % 2].sem, (n - 8) // 2 + 1)
                    for k in range(4):
                        ins = te.transpose(banks[:, n % 8, k * P:k * P + w],
                                           xtok[0:w, i, (c0 + k) * P:(c0 + k + 1) * P], C("ident", w, w))
                    turned.by(ins)
                pe.wait_ge(g_in.sem, 16 * 20)
                pe.wait_ge(moved[0].sem, 2)
                turned.by(te.transpose(banks[:, 2, 0:P], grow[:], C("ident")))
        ctx.close()

    def norm(gain, cols):
        n = cols[-1][0] + cols[-1][1]
        squared, summed, factor, scaled = sig("squared"), sig("summed"), sig("factor"), sig("scaled")
        s0, m0, f0 = squared.count, summed.count, factor.count
        with nc.Block() as block:
            @block.scalar
            def _(act):
                for k in range(KT):
                    squared.by(se.activation(uT[:, k, 0:n], hT[:, k, 0:n], ACT.Square))
                step = chained(act, "act_step")
                for b, (c, w) in enumerate(cols):
                    act.wait_ge(summed.sem, m0 + b + 1)
                    step(se.activation(rT[:, c:c + w], banks[:, b, 0:w], ACT.Ln, bias=C("eps"), scale=1.0 / D))
                    factor.by(se.activation(rT[:, c:c + w], rT[:, c:c + w], ACT.Exp, scale=-0.5))

            @block.tensor
            def _(pe):
                for k in range(KT):
                    pe.wait_ge(squared.sem, s0 + k + 1)
                    for b, (c, w) in enumerate(cols):
                        ins = te.matmul(banks[:, b, 0:w], C("ones"), uT[:, k, c:c + w], start=k == 0, stop=k == KT - 1)
                        if k == KT - 1:
                            summed.by(ins)

            @block.vector
            def _(dve):
                for b, (c, w) in enumerate(cols):
                    dve.wait_ge(factor.sem, f0 + b + 1)
                    for k in range(KT):
                        scaled.by(ve.scalar_tensor_tensor(uT[:, k, c:c + w], hT[:, k, c:c + w], G(gain, k),
                                                          rT[:, c:c + w], ALU.mult, ALU.mult))

    class Banks:

        def __init__(self, owners, ends=(), ring=8):
            self.made = sig("made")
            self.emptied = {"act": sig("act_emptied"), "dve": sig("dve_emptied")}
            self.first, self.ring, self.owners = self.made.count, ring, owners
            count = {e: s.count for e, s in self.emptied.items()}
            self.when = []
            for n, e in enumerate(owners):
                count[e] += 1
                self.when.append(count[e])
            for n, j in ends:
                job_done[j] = (self.made.sem, self.first + n + 1)

        def at(self, n):
            return banks[:, n % self.ring, :]

        def wait_empty(self, pe, n):
            if n >= self.ring:
                pe.wait_ge(self.emptied[self.owners[n - self.ring]].sem, self.when[n - self.ring])

        def wait_made(self, engine, n):
            engine.wait_ge(self.made.sem, self.first + n + 1)

        def wait_emptied(self, engine, n):
            engine.wait_ge(self.emptied[self.owners[n]].sem, self.when[n])

    def project_in(q, k_, sg, cT, krT, v):
        groups, ends = [], []
        for name in ("hf", "hq", "hi", "hg", "cq", "kr"):
            if name == "hi":
                groups += [(name, J[name], 0, i) for i in range(QT + 1)]
            else:
                groups += [(name, J[name], f, b) for f in range(1 if name == "kr" else 4) for b in range(2)]
            ends.append((len(groups) - 1, J[name]))
        owners = ["act" if g[0] in ("hq", "hg") or (g[0] != "hf" and n % 2) else "dve" for n, g in enumerate(groups)]
        ring = Banks(owners, ends)

        def empty(name, engine, copy):
            for n, (kind, j, f, b) in enumerate(groups):
                if owners[n] != name:
                    continue
                ring.wait_made(engine, n)
                if kind == "hi":
                    c, w = TILES[b]
                    ins = copy(v[0:w, b, :], ring.at(n)[0:w, :])
                else:
                    c, w = HALVES[b]
                    src = ring.at(n)[:, 0:w]
                    if kind in ("hq", "hg"):
                        ins = se.activation((q if kind == "hq" else sg)[:, f, c:c + w], src, ACT.Silu)
                    elif kind == "kr":
                        ins = copy(krT[0:ROPE, c:c + w], src[0:ROPE, :])
                    else:
                        ins = copy((k_ if kind == "hf" else cT)[:, f, c:c + w], src)
                ring.emptied[name].by(ins)

        with nc.Block() as block:
            @block.sync
            def _(sp):
                issue(sp, J["kr"] + 1 + NW)

            @block.tensor
            def _(pe):
                for n, (kind, j, f, b) in enumerate(groups):
                    w_ = weight(pe, j)
                    ring.wait_empty(pe, n)
                    for k in range(KT):
                        if kind == "hi":
                            c, w = TILES[b]
                            ins = te.matmul(ring.at(n)[0:w, :], uT[:, k, c:c + w], w_[:, k, :], start=k == 0, stop=k == KT - 1)
                        else:
                            c, w = HALVES[b]
                            m = ROPE if kind == "kr" else P
                            ins = te.matmul(ring.at(n)[0:m, 0:w], w_[:, k, f * P:f * P + m], uT[:, k, c:c + w],
                                            start=k == 0, stop=k == KT - 1)
                    ring.made.by(ins)

            @block.scalar
            def _(act):
                empty("act", act, se.copy)

            @block.vector
            def _(dve):
                empty("dve", dve, ve.tensor_copy)

    class Decay:

        def __init__(self, tiles, meta, q, k_, b, diff, e, qd, kd):
            self.tiles, self.meta = tiles, meta
            self.q, self.k, self.b, self.diff, self.e, self.qd, self.kd = q, k_, b, diff, e, qd, kd
            self.signals = {s: sig("decay_" + s) for s in ("diff", "exp", "q", "k", "prod", "kept")}
            self.base = {s: x.count for s, x in self.signals.items()}

        def by(self, s, ins):
            self.signals[s].by(ins)

        def wait(self, engine, s, n):
            if n > 0:
                engine.wait_ge(self.signals[s].sem, self.base[s] + n)

        def cols(self, l):
            return TOK if self.has_meta(l) else SEQ

        def has_meta(self, l):
            return self.meta and (l == len(LEVELS) or LEVELS[l] <= META // 2)

    def decay_diffs(dve, d, l):
        m, n = LEVELS[l], d.cols(l)
        d.wait(dve, "exp", l)
        for u in range(2):
            bv, o = (x[:, :, 0:n].rearrange("p h (b u m) -> p h b u m", u=2, m=m) for x in (d.b, d.diff))
            r = bv[:, :, :, 0, m - 1:m].to_broadcast([P, d.tiles, n // (2 * m), m])
            x = bv[:, :, :, u, :]
            ins = ve.tensor_tensor(o[:, :, :, u, :], x if u else r, r if u else x, ALU.subtract)
        d.by("diff", ins)

    def decay_exp(act, d, l):
        n = d.cols(l)
        d.wait(act, "diff", l + 1)
        d.wait(act, "q", l)
        d.wait(act, "k", l)
        d.by("exp", se.activation(d.e[:, :, 0:n], d.diff[:, :, 0:n], ACT.Exp))

    def decay_scale(engine, mul, d, l, s):
        n = d.cols(l)
        x, o = (d.q, d.qd) if s == "q" else (d.k, d.kd)
        d.wait(engine, "exp", l + 1)
        d.wait(engine, "prod", l)
        d.by(s, mul(o[:, :, 0:n], x[:, :, 0:n], d.e[:, :, 0:n], ALU.mult))

    def decay_products(pe, d, l, bank0, heads_per_tile):
        last = l == len(LEVELS)
        q_, k__ = (d.q, d.k) if last else (d.qd, d.kd)
        if not last:
            d.wait(pe, "q", l + 1)
            d.wait(pe, "k", l + 1)
        d.wait(pe, "kept", l)
        rows = P // heads_per_tile
        for h in range(HEADS):
            f, r = h // heads_per_tile, rows * (h % heads_per_tile)
            for c in range(QT):
                s = slice(P * c, P * c + P)
                ins = te.matmul(banks[:, bank0 + h, P * c:P * c + P], k__[r:r + rows, f, s], q_[r:r + rows, f, s],
                                start=True, stop=True)
            if d.has_meta(l):
                s = slice(SEQ, TOK)
                ins = te.matmul(banks[0:META, bank0 + HEADS, META * h:META * h + META], k__[:, f, s], q_[:, f, s],
                                start=True, stop=True)
        d.by("prod", ins)

    def decay_keep(dve, d, l, bank0, att, att_meta):
        d.wait(dve, "prod", l + 1)
        mask = level_mask[:, P * l:P * l + P]
        ins = ve.copy_predicated(att[:], mask.unsqueeze(1).to_broadcast([P, HEADS * QT, P]),
                                 banks[:, bank0:bank0 + HEADS, :].rearrange("p h (c t) -> p (h c) t", c=QT))
        if d.has_meta(l):
            ins = ve.copy_predicated(att_meta, mask[0:META, 0:META].unsqueeze(1).to_broadcast([META, HEADS, META]),
                                     banks[0:META, bank0 + HEADS, 0:HEADS * META].rearrange("p (h t) -> p h t", h=HEADS))
        d.by("kept", ins)

    def hgrn(q, k_, sg, v, oT):
        with ExitStack() as ctx:
            b = sb(ctx, "hgrn_b", [P, HEADS, TOK])
            qd = sb(ctx, "hgrn_qd", [P, HEADS, TOK])
            kd = sb(ctx, "hgrn_kd", [P, HEADS, TOK])
            att = sb(ctx, "hgrn_att", [P, HEADS * QT, P])
            att_meta = oT[0:META, 6, 0:HEADS * META].rearrange("p (h t) -> p h t", h=HEADS)
            ktok_meta = oT[0:META, 7, 0:512]
            decay = sb(ctx, "hgrn_decay", [P, HEADS, QT + 1])
            diff, e = uT[:, 0:4, :], uT[:, 4:8, :]
            d = Decay(HEADS, True, q, k_, b, diff, e, qd, kd)
            gate = sig("hgrn_gate")
            g0 = gate.count

            with nc.Block() as block:
                @block.scalar
                def _(act):
                    step = chained(act, "act_step")
                    step(se.activation(diff, k_[:], ACT.Abs))
                    step(se.activation(diff, diff, ACT.Exp, scale=-1.0))
                    gate.by(se.activation(diff, diff, ACT.Ln, bias=C("one")))
                    act.wait_ge(gate.sem, g0 + 2)
                    gate.by(se.activation(k_[:], e, ACT.Exp))
                    for l in range(len(LEVELS)):
                        decay_exp(act, d, l)

                @block.vector
                def _(dve):
                    step = chained(dve, "dve_step")
                    ve.memset(att[:], 0.0)
                    ve.memset(att_meta, 0.0)
                    dve.wait_ge(gate.sem, g0 + 1)
                    step(ve.scalar_tensor_tensor(b[:], k_[:], 0.0, diff, ALU.min, ALU.subtract))
                    ins = ve.tensor_tensor(e, b[:], k_[:], ALU.subtract)
                    ins.then_inc(gate.sem, 1)
                    step(ve.tensor_copy(diff, b[:]))
                    for h in range(HEADS):
                        ins = ve.tensor_tensor_scan(b[:, h, :], C("scan"), diff[:, h, :], 0.0, ALU.mult, ALU.add)
                    step(ins)
                    dve.wait_ge(gate.sem, g0 + 3)
                    for l in range(len(LEVELS)):
                        decay_diffs(dve, d, l)
                        decay_scale(dve, ve.tensor_tensor, d, l, "q")
                        if l >= 1:
                            decay_keep(dve, d, l - 1, 0, att, att_meta)
                    for l in (len(LEVELS) - 1, len(LEVELS)):
                        decay_keep(dve, d, l, 0, att, att_meta)
                gate.count = g0 + 3

                @block.gpsimd
                def _(pool):
                    pool.wait_ge(gate.sem, g0 + 3)
                    for l in range(len(LEVELS)):
                        decay_scale(pool, ge.tensor_tensor, d, l, "k")

                @block.tensor
                def _(pe):
                    for l in range(len(LEVELS) + 1):
                        decay_products(pe, d, l, 0, 1)

            ktok, states = qd, diff
            ktok = qd[:].rearrange("p h n -> p (h n)")[:, 0:QT * 512].rearrange("p (c n) -> p c n", c=QT)
            states = diff.rearrange("p h n -> p (h n)")[:, 0:QT * 512].rearrange("p (c n) -> p c n", c=QT)
            squares = b
            faded, summed, grown, scaled = sig("hgrn_faded"), sig("hgrn_turned"), sig("hgrn_grown"), sig("hgrn_states")
            order = [QT] + list(range(QT))
            a = {s: sig("hgrn_" + s) for s in ("from_end", "from_end_exp", "q_decayed", "k_decayed", "turned", "ktok",
                                               "grown", "state", "out", "squared", "gated", "sums", "factor")}
            a0 = {s: x.count for s, x in a.items()}

            def wait(engine, s, n):
                engine.wait_ge(a[s].sem, a0[s] + n)

            with nc.Block() as block:
                @block.vector
                def _(dve):
                    step = chained(dve, "dve_step")
                    ends = b[:, :, 0:SEQ].rearrange("p h (c t) -> p h c t", t=P)[:, :, :, P - 1:P]
                    ve.tensor_tensor(kd[:, :, 0:SEQ].rearrange("p h (c t) -> p h c t", t=P),
                                     ends.to_broadcast([P, HEADS, QT, P]),
                                     b[:, :, 0:SEQ].rearrange("p h (c t) -> p h c t", t=P), ALU.subtract)
                    a["from_end"].by(ve.tensor_tensor(kd[:, :, SEQ:TOK], b[:, :, TOK - 1:TOK].to_broadcast([P, HEADS, META]),
                                                      b[:, :, SEQ:TOK], ALU.subtract))
                    wait(dve, "from_end_exp", 2)
                    a["k_decayed"].by(ve.tensor_tensor(kd[:], kd[:], k_[:], ALU.mult))
                    a["q_decayed"].by(ve.tensor_tensor(e, e, q[:], ALU.mult))
                    for n, c in enumerate(order):
                        wait(dve, "turned", n + 1)
                        w = TILES[c][1]
                        dst = ktok_meta if c == QT else ktok[:, c, :]
                        a["ktok"].by(ve.tensor_copy(dst, banks[0:w, n, :]))
                    for n, c in enumerate(order[:-1]):
                        wait(dve, "grown", n + 1)
                        if n == 0:
                            ins = ve.tensor_copy(states[:, 0, :], banks[:, 5, :])
                        else:
                            wait(dve, "state", n)
                            for h in range(HEADS):
                                s = slice(P * h, P * h + P)
                                ins = ve.scalar_tensor_tensor(states[:, n, s], states[:, n - 1, s],
                                                              decay[:, h, c:c + 1], banks[:, 5 + n % 2, s],
                                                              ALU.mult, ALU.add)
                        a["state"].by(ins)
                    for h in range(HEADS + 1):
                        wait(dve, "squared", h + 1)
                        if h < HEADS:
                            o, x, g = oT[:, h, 0:SEQ], banks[:, h, :], sg[:, h, 0:SEQ]
                        else:
                            o, g = oT[:, 0:HEADS, SEQ:TOK], sg[:, :, SEQ:TOK]
                            x = banks[:, 4, 0:HEADS * META].rearrange("p (h t) -> p h t", h=HEADS)
                        a["gated"].by(ve.scalar_tensor_tensor(o, x, G("hgrn_out"), g, ALU.mult, ALU.mult))
                    for h in range(HEADS):
                        wait(dve, "factor", h + 1)
                        wait(dve, "gated", HEADS + 1)
                        step(ve.tensor_tensor(oT[:, h, :], oT[:, h, :], squares[:, h, :], ALU.mult))

                @block.scalar
                def _(act):
                    a["from_end_exp"].by(se.activation(e, b[:], ACT.Exp))
                    wait(act, "from_end", 1)
                    se.activation(decay[:, :, 0:QT], b[:, :, 0:SEQ].rearrange("p h (c t) -> p h c t", t=P)[:, :, :, P - 1], ACT.Exp)
                    se.activation(decay[:, :, QT], b[:, :, TOK - 1], ACT.Exp)
                    a["from_end_exp"].by(se.activation(kd[:], kd[:], ACT.Exp))
                    for h in range(HEADS + 1):
                        wait(act, "out", h + 1)
                        wait(act, "k_decayed", 1)
                        if h < HEADS:
                            o, x = squares[:, h, 0:SEQ], banks[:, h, :]
                        else:
                            o = squares[:, :, SEQ:TOK]
                            x = banks[:, 4, 0:HEADS * META].rearrange("p (h t) -> p h t", h=HEADS)
                        a["squared"].by(se.activation(o, x, ACT.Square))
                    step = chained(act, "act_step")
                    for h in range(HEADS):
                        wait(act, "sums", h + 1)
                        x = banks[:, 2 * h:2 * h + 2, 0:HALF]
                        o = squares[:, h, :].rearrange("p (b t) -> p b t", b=2)
                        step(se.activation(o, x, ACT.Ln, bias=C("eps"), scale=1.0 / HDIM))
                        a["factor"].by(se.activation(o, o, ACT.Exp, scale=-0.5))

                @block.tensor
                def _(pe):
                    wait(pe, "k_decayed", 1)
                    for n, c in enumerate(order):
                        col, w = TILES[c]
                        for h in range(HEADS):
                            ins = te.transpose(banks[0:w, n, P * h:P * h + P], kd[:, h, col:col + w], C("ident"))
                        a["turned"].by(ins)
                    for n, c in enumerate(order[:-1]):
                        w = TILES[c][1]
                        wait(pe, "ktok", n + 1)
                        if n >= 2:
                            wait(pe, "state", n - 1)
                        for h in range(HEADS):
                            s = slice(P * h, P * h + P)
                            x = ktok_meta[:, s] if c == QT else ktok[:, c, s]
                            ins = te.matmul(banks[:, 5 + n % 2, s], x, v[0:w, c, s], start=True, stop=True)
                        a["grown"].by(ins)
                    wait(pe, "q_decayed", 1)
                    wait(pe, "ktok", QT + 1)
                    wait(pe, "state", QT)
                    for h in range(HEADS):
                        s = slice(P * h, P * h + P)
                        for c in range(QT):
                            o = banks[:, h, P * c:P * c + P]
                            te.matmul(o, v[:, c, s], att[:, QT * h + c, :], start=True, stop=False)
                            ins = te.matmul(o, states[:, c, s], e[:, h, P * c:P * c + P], start=False, stop=True)
                        a["out"].by(ins)
                    for h in range(HEADS):
                        ins = te.matmul(banks[:, 4, META * h:META * h + META], v[0:META, QT, P * h:P * h + P],
                                        att_meta[:, h, :], start=True, stop=True)
                    a["out"].by(ins)
                    wait(pe, "squared", HEADS + 1)
                    wait(pe, "gated", HEADS + 1)
                    for h in range(HEADS):
                        for b_ in range(2):
                            ins = te.matmul(banks[:, 2 * h + b_, 0:HALF], C("ones"), squares[:, h, HALF * b_:HALF * b_ + HALF],
                                            start=True, stop=True)
                        a["sums"].by(ins)

    def factors(act, step, src, rows, w, dst, width):
        step(se.activation(dst, src, ACT.Ln, bias=C("eps", rows), scale=1.0 / width))
        return se.activation(dst, dst, ACT.Exp, scale=-0.5)

    def mla_heads(q, k_, qr, kr, krT, cT, v):
        squares, fac = uT[:, 0:4, :], uT[:, 4:8, :]
        s = {x: sig("mla_" + x) for x in ("squared", "sums", "factor", "normed", "turned", "cosine", "sine", "done")}
        s0 = {x: y.count for x, y in s.items()}

        def wait(engine, x, n):
            engine.wait_ge(s[x].sem, s0[x] + n)

        with nc.Block() as block:
            @block.scalar
            def _(act):
                s["squared"].by(se.activation(squares, cT[:], ACT.Square))
                step = chained(act, "act_step")
                for j in range(2):
                    wait(act, "sums", j + 1)
                    x = banks[:, 2 * j:2 * j + 2, 0:HALF]
                    s["factor"].by(factors(act, step, x, P, TOK, fac[:, j, :].rearrange("p (b t) -> p b t", b=2), Q_RANK))

            @block.tensor
            def _(pe):
                wait(pe, "squared", 1)
                for j in range(2):
                    for b, (c, w) in enumerate(HALVES):
                        for k in range(2):
                            ins = te.matmul(banks[:, 2 * j + b, 0:w], C("ones"), squares[:, 2 * j + k, c:c + w],
                                            start=k == 0, stop=k == 1)
                    s["sums"].by(ins)

            @block.vector
            def _(dve):
                for j, g in enumerate(("qa", "kva")):
                    wait(dve, "factor", j + 1)
                    for k in range(2):
                        s["normed"].by(ve.scalar_tensor_tensor(cT[:, 2 * j + k, :], cT[:, 2 * j + k, :], G(g, k),
                                                               fac[:, j, :], ALU.mult, ALU.mult))

        groups, ends = [], []
        for h in range(HEADS):
            c = QK * h
            groups += [("q", J["q_up"][c // 512], c % 512, h, b) for b in range(2)]
            c += NOPE
            groups += [("qr", J["q_up"][c // 512], c % 512, h, b) for b in range(2)]
            if h == 2:
                ends.append((len(groups) - 3, J["q_up"][0]))
        ends.append((len(groups) - 1, J["q_up"][1]))
        for h in range(HEADS):
            groups += [("k", J["kv_up"][h // 2], 256 * (h % 2), h, b) for b in range(2)]
        groups += [("v", J["kv_up"][1], 0, 0, i) for i in range(QT + 1)]
        ends += [(len(groups) - 1, j) for j in J["kv_up"]]
        owners = [("act", "dve")[n % 2] for n in range(len(groups))]
        ring = Banks(owners, ends)

        def empty(name, engine, copy):
            for n, (kind, j, c0, h, b) in enumerate(groups):
                if owners[n] != name:
                    continue
                ring.wait_made(engine, n)
                if kind == "v":
                    ins = copy(v[0:TILES[b][1], b, :], ring.at(n)[0:TILES[b][1], :])
                else:
                    c, w = HALVES[b]
                    m = ROPE if kind == "qr" else P
                    ins = copy({"q": q, "qr": qr, "k": k_}[kind][0:m, h, c:c + w], ring.at(n)[0:m, 0:w])
                ring.emptied[name].by(ins)

        with nc.Block() as block:
            @block.sync
            def _(sp):
                issue(sp, J["out"][1] + 1)

            @block.tensor
            def _(pe):
                for n, (kind, j, c0, h, b) in enumerate(groups):
                    w_ = weight(pe, j)
                    ring.wait_empty(pe, n)
                    if kind == "v":
                        c, w = TILES[b]
                        for i, jj in enumerate(J["kv_up"]):
                            for k in range(2):
                                rhs = weight(pe, jj)[:, k, :].rearrange("p (h n) -> p h n", h=2)[:, :, NOPE:]
                                ins = te.matmul(ring.at(n)[0:w, 256 * i:256 * i + 256], cT[:, 2 + k, c:c + w], rhs,
                                                start=k == 0, stop=k == 1)
                    else:
                        c, w = HALVES[b]
                        m = ROPE if kind == "qr" else P
                        for k in range(2):
                            ins = te.matmul(ring.at(n)[0:m, 0:w], w_[:, k, c0:c0 + m],
                                            cT[:, (2 if kind == "k" else 0) + k, c:c + w], start=k == 0, stop=k == 1)
                    ring.made.by(ins)

            @block.scalar
            def _(act):
                empty("act", act, se.copy)

            @block.vector
            def _(dve):
                empty("dve", dve, ve.tensor_copy)

        s0.update({x: y.count for x, y in s.items()})
        with ExitStack() as ctx:
            sq_rope = sb(ctx, "mla_sq_rope", [ROPE, HEADS + 1, TOK])
            with nc.Block() as block:
                @block.scalar
                def _(act):
                    step = chained(act, "act_step")
                    s["squared"].by(se.activation(sq_rope[:, 0:HEADS, :], qr, ACT.Square))
                    s["squared"].by(se.activation(squares, q[:], ACT.Square))
                    s["squared"].by(se.activation(sq_rope[:, HEADS, :], krT[0:ROPE, :], ACT.Square))
                    for side in range(2):
                        for h in range(HEADS):
                            wait(act, "sums", 4 * side + h + 1)
                            if side == 1:
                                wait(act, "normed", 2 * h + 2)
                            x = banks[:, 2 * h:2 * h + 2, 0:HALF]
                            s["factor"].by(factors(act, step, x, P, TOK,
                                                   fac[:, h, :].rearrange("p (b t) -> p b t", b=2), QK))
                        if side == 0:
                            s["squared"].by(se.activation(squares, k_[:], ACT.Square))

                @block.tensor
                def _(pe):
                    for side in range(2):
                        wait(pe, "squared", 3 + side)
                        for h in range(HEADS):
                            if side == 1:
                                wait(pe, "factor", h + 1)
                            for b, (c, w) in enumerate(HALVES):
                                te.matmul(banks[:, 2 * h + b, 0:w], C("ones"), squares[:, h, c:c + w], start=True, stop=False)
                                r = sq_rope[:, h if side == 0 else HEADS, c:c + w]
                                ins = te.matmul(banks[:, 2 * h + b, 0:w], C("ones", ROPE), r, start=False, stop=True)
                            s["sums"].by(ins)

                @block.vector
                def _(dve):
                    for h in range(HEADS):
                        wait(dve, "factor", h + 1)
                        s["normed"].by(ve.scalar_tensor_tensor(q[:, h, :], q[:, h, :], G("q_norm"), fac[:, h, :],
                                                               ALU.mult, ALU.mult))
                        if h == 0:
                            wait(dve, "squared", 3)
                        s["normed"].by(ve.scalar_tensor_tensor(qr[:, h, :], qr[:, h, :], G("q_norm", 1, ROPE),
                                                               fac[0:ROPE, h, :], ALU.mult, ALU.mult))
                    ve.tensor_scalar(krT[0:ROPE, :], krT[0:ROPE, :], G("k_norm", 1, ROPE), None, ALU.mult)
                    for h in range(HEADS):
                        wait(dve, "factor", HEADS + h + 1)
                        s["normed"].by(ve.scalar_tensor_tensor(k_[:, h, :], k_[:, h, :], G("k_norm"), fac[:, h, :],
                                                               ALU.mult, ALU.mult))

            sined = sq_rope

            def source(n):
                return qr[:, n, :] if n < HEADS else krT[0:ROPE, :]

            with nc.Block() as block:
                @block.tensor
                def _(pe):
                    for n in range(HEADS + 1):
                        if n >= 4:
                            wait(pe, "sine", n - 3)
                        for b, (c, w) in enumerate(HALVES):
                            ins = te.matmul(banks[0:ROPE, 2 * (n % 4) + b, 0:w], C("rot", ROPE), source(n)[:, c:c + w],
                                            start=True, stop=True)
                        s["turned"].by(ins)

                @block.gpsimd
                def _(pool):
                    for n in range(HEADS + 1):
                        wait(pool, "turned", n + 1)
                        s["cosine"].by(ge.tensor_tensor(source(n), source(n), C("cos", ROPE), ALU.mult))

                @block.vector
                def _(dve):
                    step = chained(dve, "dve_step")
                    sin = C("sin", ROPE).rearrange("p (b t) -> p b t", b=2)
                    for n in range(HEADS + 1):
                        wait(dve, "turned", n + 1)
                        o = sined[:, n, :].rearrange("p (b t) -> p b t", b=2)
                        s["sine"].by(ve.tensor_tensor(o, banks[0:ROPE, 2 * (n % 4):2 * (n % 4) + 2, 0:HALF], sin, ALU.mult))
                    for n in range(HEADS + 1):
                        wait(dve, "cosine", n + 1)
                        wait(dve, "sine", n + 1)
                        ins = ve.tensor_tensor(source(n), source(n), sined[:, n, :], ALU.add)
                    step(ins)
                    for h in range(HEADS):
                        ve.tensor_tensor(kr[:, h, :], krT[0:ROPE, :], fac[0:ROPE, h, :], ALU.mult)

    def mla_attention(q, k_, qr, kr, v, oT):
        units = [(h, i) for h in range(HEADS) for i in range(QT)] + [(h, QT) for h in range(HEADS)]
        scale = QK ** -0.5
        with ExitStack() as ctx:
            probs = sb(ctx, "mla_probs", [P, 2, TOK])
            pT = sb(ctx, "mla_pT", [P, 2, QT + 1, P])
            stat = sb(ctx, "mla_stat", [P, 4, len(units)])
            s = {x: sig("att_" + x) for x in ("scored", "max", "exp", "probs", "turned", "moved", "out", "stored")}
            s0 = {x: y.count for x, y in s.items()}

            def wait(engine, x, n):
                if n > 0:
                    engine.wait_ge(s[x].sem, s0[x] + n)

            def shape(n):
                h, i = units[n]
                return (h, i) + TILES[i] + (0 if i == QT else P * (i + 1),)

            def scores_at(n, w, a, b):
                return banks[0:w, 2 * (n % 2):2 * (n % 2) + 2, :].rearrange("p a b -> p (a b)")[:, a:b]

            with nc.Block() as block:
                @block.tensor
                def _(pe):
                    def scores(n):
                        h, i, c, w, real = shape(n)
                        wait(pe, "exp", n - 1)
                        wait(pe, "moved", n - 1)
                        if real:
                            o = scores_at(n, w, 0, real)
                            te.matmul(o, q[:, h, c:c + w], k_[:, h, 0:real], start=True, stop=False)
                            te.matmul(o, qr[:, h, c:c + w], kr[:, h, 0:real], start=False, stop=True)
                            te.matmul(scores_at(n, w, real - CHUNK, real), C("half_ind", 1), C("neg64", 1),
                                      start=False, stop=True, skip_group_check=True)
                        o = scores_at(n, w, real, real + META)
                        te.matmul(o, q[:, h, c:c + w], k_[:, h, SEQ:TOK], start=True, stop=False, skip_group_check=True)
                        s["scored"].by(te.matmul(o, qr[:, h, c:c + w], kr[:, h, SEQ:TOK], start=False, stop=True,
                                                 skip_group_check=True))

                    def turn(n):
                        h, i, c, w, real = shape(n)
                        wait(pe, "probs", n + 1)
                        for j in range(real // P):
                            te.transpose(banks[:, 4 + n % 2, P * j:P * j + w], probs[0:w, n % 2, P * j:P * j + P],
                                         C("ident", w, w))
                        s["turned"].by(te.transpose(banks[0:META, 2 * (n % 2) + 1, P:P + w],
                                                    probs[0:w, n % 2, real:real + META], C("ident", w, w)))

                    def weigh(n):
                        h, i, c, w, real = shape(n)
                        wait(pe, "moved", n + 1)
                        wait(pe, "stored", n - 1)
                        o = banks[:, 6 + n % 2, 0:w]
                        vs = slice(P * h, P * h + P)
                        for j in range(real // P):
                            te.matmul(o, v[:, j, vs], pT[:, n % 2, j, 0:w], start=j == 0, stop=False)
                        s["out"].by(te.matmul(o, v[0:META, QT, vs], pT[0:META, n % 2, QT, 0:w], start=not real, stop=True))

                    for n in range(len(units) + 2):
                        if n < len(units):
                            scores(n)
                        if 1 <= n <= len(units):
                            turn(n - 1)
                        if n >= 2:
                            weigh(n - 2)

                @block.vector
                def _(dve):
                    step = chained(dve, "dve_step")

                    def move(n):
                        h, i, c, w, real = shape(n)
                        wait(dve, "turned", n + 1)
                        wait(dve, "out", n - 1)
                        if real:
                            ve.tensor_copy(pT[:, n % 2, 0:real // P, :],
                                           banks[:, 4 + n % 2, 0:real].rearrange("p (j t) -> p j t", t=P))
                        s["moved"].by(ve.tensor_copy(pT[0:META, n % 2, QT, 0:w], banks[0:META, 2 * (n % 2) + 1, P:P + w]))

                    def maximum(n):
                        h, i, c, w, real = shape(n)
                        wait(dve, "scored", n + 1)
                        step(ve.reduce_max(stat[0:w, 0, n:n + 1], scores_at(n, w, 0, real + META), AX))
                        s["max"].by(ve.tensor_scalar(stat[0:w, 1, n:n + 1], stat[0:w, 0, n:n + 1], -scale, None, ALU.mult))

                    def normalise(n):
                        h, i, c, w, real = shape(n)
                        wait(dve, "exp", n + 1)
                        step(ve.reciprocal(stat[0:w, 3, n:n + 1], stat[0:w, 2, n:n + 1]))
                        x = probs[0:w, n % 2, 0:real + META]
                        s["probs"].by(ve.tensor_scalar(x, x, stat[0:w, 3, n:n + 1], None, ALU.mult))

                    for n in range(len(units) + 2):
                        if n >= 2:
                            move(n - 2)
                        if n < len(units):
                            maximum(n)
                        if 1 <= n <= len(units):
                            normalise(n - 1)

                @block.scalar
                def _(act):
                    for n in range(len(units) + 2):
                        if n < len(units):
                            h, i, c, w, real = shape(n)
                            wait(act, "max", n + 1)
                            wait(act, "turned", n - 1)
                            s["exp"].by(se.activation(probs[0:w, n % 2, 0:real + META], scores_at(n, w, 0, real + META),
                                                      ACT.Exp, bias=stat[0:w, 1, n:n + 1], scale=scale,
                                                      accum_out=stat[0:w, 2, n:n + 1]))
                        if n >= 2:
                            h, i, c, w, real = shape(n - 2)
                            wait(act, "out", n - 1)
                            s["stored"].by(se.copy(oT[:, HEADS + h, c:c + w], banks[:, 6 + n % 2, 0:w]))

    def project_out(oT, pair, cols, prefetch):
        groups = [(pair[f // 4], f, b) for f in range(KT) for b in range(len(cols))]
        ring = Banks(["dve"] * len(groups), [(len(groups) // 2 - 1, pair[0]), (len(groups) - 1, pair[1])])
        with nc.Block() as block:
            @block.sync
            def _(sp):
                issue(sp, prefetch)

            @block.tensor
            def _(pe):
                for n, (j, f, b) in enumerate(groups):
                    w_ = weight(pe, j)
                    c, w = cols[b]
                    ring.wait_empty(pe, n)
                    for k in range(KT):
                        ins = te.matmul(ring.at(n)[:, 0:w], w_[:, k, P * (f % 4):P * (f % 4) + P], oT[:, k, c:c + w],
                                        start=k == 0, stop=k == KT - 1)
                    ring.made.by(ins)

            @block.vector
            def _(dve):
                for n, (j, f, b) in enumerate(groups):
                    c, w = cols[b]
                    ring.wait_made(dve, n)
                    ring.emptied["dve"].by(ve.tensor_tensor(hT[:, f, c:c + w], hT[:, f, c:c + w], ring.at(n)[:, 0:w], ALU.add))

    FC = 512
    CHUNKS = D_FF // FC

    def mlp_jobs(up):
        while len(jobs) % NW:
            skipped.add(len(jobs))
            jobs.append(None)
        first = len(jobs)
        for c in range(2):
            job(up[:, FC * c:FC * c + FC])
        skipped.update((first + 2, first + 3))
        jobs.extend([None, None])
        return first

    def split_products(o, w_hi, w_lo, x_hi, x_lo, first, last):
        te.matmul(o, w_hi, x_hi, start=first, stop=False)
        te.matmul(o, w_hi, x_lo, start=False, stop=False)
        return te.matmul(o, w_lo, x_hi, start=False, stop=last)

    def mlp(first, gain, up, down, cols):
        B, F = len(cols), FC // P
        GU, GD = F * B, KT * B
        SL = 4
        n_cols = cols[-1][0] + cols[-1][1]
        up_made, down_made, hidden = sig("up_made"), sig("down_made"), sig("hidden")
        relu, added = sig("act_emptied"), sig("dve_emptied")
        squared, a_high = sig("mlp_squared"), sig("mlp_a_high")
        high = sig("mlp_up_high"), sig("mlp_down_high")
        split = sig("mlp_up_split"), sig("mlp_down_split")
        u0, d0, a0, r0, h0, q0, g0 = (x.count for x in (up_made, down_made, hidden, relu, added, squared, a_high))
        hi0, sp0 = [x.count for x in high], [x.count for x in split]
        n_ = {x: sig("mlp_norm_" + x) for x in ("square", "sum", "factor", "scaled", "high", "split")}
        n0 = {x: y.count for x, y in n_.items()}
        assert min(r0, h0) >= GD + 4
        L = CHUNKS // 2 - 1
        late.close()
        with ExitStack() as ctx:
            relued = sb(ctx, "mlp_relu", [P, 2, HALF])
            sq = sb(ctx, "mlp_square", [P, 2, HALF])
            tmp = sb(ctx, "mlp_norm_tmp", [P, 2, TOK])
            a_hi, a_lo = (sb(ctx, "mlp_hidden_" + x, [P, 2, F, TOK], FR) for x in ("high", "low"))
            u_hi, u_lo = (sb(ctx, "mlp_u_" + x, [P, KT, TOK], FR) for x in ("high", "low"))
            w_hi, w_lo = ((sb(ctx, "mlp_up_" + x, [P, KT, FC], FR), sb(ctx, "mlp_down_" + x, [P, F, D], FR))
                          for x in ("high", "low"))

            def as_piece(d, b):
                w = wbuf[b][:]
                return w.rearrange("p a b -> p (a b)").rearrange("p (k n) -> p k n", k=F) if d else w

            loads0 = [loads(first + b) - 1 for b in range(2)]

            def raw(piece):
                d, i, par = piece
                c = 2 * i + par
                if d == 0:
                    b, n = (0, 1) if isinstance(c, int) and c == 0 else (1, c)
                else:
                    b, n = (1, CHUNKS) if isinstance(c, int) and c == CHUNKS - 1 else (0, c + 2)
                return as_piece(d, b), b, loads0[b] + n

            def cols_of(d, s):
                w = (D if d else FC) // SL
                return slice(w * s, w * s + w)

            def schedule(engine, go_up, go_down):
                go_up(0, 0, (0, 0, 1))
                with engine.Fori(0, L) as i:
                    go_up(i, 1, (1, i, 0))
                    go_down(i, 0, (0, i + 1, 0))
                    go_up(i + 1, 0, (1, i, 1))
                    go_down(i, 1, (0, i + 1, 1))
                go_up(L, 1, (1, L, 0))
                go_down(L, 0, (1, L, 1))
                go_down(L, 1, None)

            u_tmp = tmp[:].rearrange("p a n -> p (a n)").rearrange("p (a n) -> p a n", n=HALF)

            def norm_wait(engine, x, n):
                if n > 0:
                    engine.wait_ge(n_[x].sem, n0[x] + n)

            with nc.Block() as block:
                @block.sync
                def _(sp):
                    def load(d, c, b, x, n):
                        sp.wait_ge(split[x].sem, sp0[x] + n)
                        src = down[bass.ds(c * FC, FC), :] if d else up[:, bass.ds(c * FC, FC)]
                        sp.dma_start(as_piece(d, b), src.rearrange("(k p) n -> p k n", p=P)).then_inc(w_loaded[b].sem, 16)

                    issue(sp, first + 2)
                    load(1, 0, 0, 0, SL)
                    with sp.Fori(1, CHUNKS - 1) as c:
                        load(0, c + 1, 1, 0, SL * (c + 1))
                        load(1, c, 0, 1, SL * c)
                    load(1, CHUNKS - 1, 1, 0, SL * CHUNKS)
                    for b in range(2):
                        w_loaded[b].count += 16 * (CHUNKS - 1)
                        job_done[first + b] = (split[1].sem, sp0[1] + SL * (CHUNKS - 1 + b))
                    for b in range(2):
                        ring_loads[b] += CHUNKS - 1
                    issue(sp, first + NW + 2)

                @block.tensor
                def _(pe):
                    def go_up(i, par, _):
                        for g in range(GU):
                            f, (c, w) = g // B, cols[g % B]
                            if g % B == 0:
                                pe.wait_ge(split[0].sem, sp0[0] + SL * (2 * i + par) + f + 1)
                            pe.wait_ge(relu.sem, r0 + GU * (2 * i + par) + g - 3)
                            for k in range(KT):
                                if isinstance(i, int) and i == par == 0 and g < B:
                                    norm_wait(pe, "split", g * KT + k + 1)
                                m = slice(P * f, P * f + P)
                                ins = split_products(banks[:, g % 4, 0:w], w_hi[0][:, k, m], w_lo[0][:, k, m],
                                                     u_hi[:, k, c:c + w], u_lo[:, k, c:c + w], k == 0, k == KT - 1)
                            ins.then_inc(up_made.sem, 1)

                    def go_down(i, par, _):
                        pe.wait_ge(hidden.sem, a0 + GU * (2 * i + par + 1))
                        for g in range(GD):
                            f, (c, w) = g // B, cols[g % B]
                            if g % (GD // SL) == 0:
                                pe.wait_ge(split[1].sem, sp0[1] + SL * (2 * i + par) + g // (GD // SL) + 1)
                            pe.wait_ge(added.sem, h0 + GD * (2 * i + par) + g - 3)
                            for k in range(F):
                                m = slice(P * f, P * f + P)
                                ins = split_products(banks[:, 4 + g % 4, 0:w], w_hi[1][:, k, m],
                                                     w_lo[1][:, k, m], a_hi[:, par, k, c:c + w],
                                                     a_lo[:, par, k, c:c + w], k == 0, k == F - 1)
                            ins.then_inc(down_made.sem, 1)

                    for k in range(KT):
                        norm_wait(pe, "square", k + 1)
                        for b, (c, w) in enumerate(cols):
                            ins = te.matmul(banks[:, 4 + b, 0:w], C("ones"), tmp[:, k % 2, c:c + w], start=k == 0, stop=k == KT - 1)
                        n_["sum"].by(ins)
                    schedule(pe, go_up, go_down)

                @block.scalar
                def _(act):
                    def round_weights(piece, s):
                        d, m = piece[0], cols_of(piece[0], s)
                        w, b, n = raw(piece)
                        act.wait_ge(w_loaded[b].sem, 16 * n)
                        se.copy(w_hi[d][:, :, m], w[:, :, m]).then_inc(high[d].sem, 1)

                    def go_up(i, par, piece):
                        for g in range(GU):
                            f, (c, w) = g // B, cols[g % B]
                            n = GU * (2 * i + par) + g
                            act.wait_ge(up_made.sem, u0 + n + 1)
                            se.activation(relued[:, g % 2, 0:w], banks[:, g % 4, 0:w], ACT.Relu).then_inc(relu.sem, 1)
                            act.wait_ge(relu.sem, r0 + n + 1)
                            if not (isinstance(n, int) and n < 2):
                                act.wait_ge(hidden.sem, a0 + n - 1)
                            se.activation(sq[:, g % 2, 0:w], relued[:, g % 2, 0:w], ACT.Square).then_inc(squared.sem, 1)
                            act.wait_ge(squared.sem, q0 + n + 1)
                            se.copy(a_hi[:, par, f, c:c + w], sq[:, g % 2, 0:w]).then_inc(a_high.sem, 1)
                            if g % B == B - 1:
                                round_weights(piece, g // B)

                    def go_down(i, par, piece):
                        if piece:
                            for s in range(SL):
                                if piece[0]:
                                    act.wait_ge(down_made.sem, d0 + GD * (2 * i + par) + GD // SL * (s + 1))
                                round_weights(piece, s)

                    for k in range(KT):
                        norm_wait(act, "sum", k - 1)
                        n_["square"].by(se.activation(tmp[:, k % 2, 0:n_cols], hT[:, k, 0:n_cols], ACT.Square))
                    for s in range(2):
                        round_weights((0, 0, 0), s)
                    norm_wait(act, "sum", KT)
                    step = chained(act, "act_step")
                    for b, (c, w) in enumerate(cols):
                        step(se.activation(rT[:, c:c + w], banks[:, 4 + b, 0:w], ACT.Ln, bias=C("eps"), scale=1.0 / D))
                    for b, (c, w) in enumerate(cols):
                        n_["factor"].by(se.activation(rT[:, c:c + w], rT[:, c:c + w], ACT.Exp, scale=-0.5))
                    for n in range(B * KT):
                        k, (c, w) = n % KT, cols[n // KT]
                        norm_wait(act, "scaled", n + 1)
                        n_["high"].by(se.copy(u_hi[:, k, c:c + w], u_tmp[:, n % 4, 0:w]))
                    for s in range(2, SL):
                        round_weights((0, 0, 0), s)
                    schedule(act, go_up, go_down)

                @block.vector
                def _(dve):
                    def rest(o, x, hi):
                        return ve.tensor_tensor(o, x, hi.bitcast(F32), ALU.subtract)

                    def rest_of_weights(piece, s):
                        d, i, par = piece
                        m = cols_of(d, s)
                        dve.wait_ge(high[d].sem, hi0[d] + SL * (2 * i + par) + s + 1)
                        rest(w_lo[d][:, :, m], raw(piece)[0][:, :, m], w_hi[d][:, :, m]).then_inc(split[d].sem, 1)

                    def go_up(i, par, piece):
                        for g in range(GU):
                            f, (c, w) = g // B, cols[g % B]
                            n = GU * (2 * i + par) + g
                            dve.wait_ge(a_high.sem, g0 + n + 1)
                            rest(a_lo[:, par, f, c:c + w], sq[:, g % 2, 0:w], a_hi[:, par, f, c:c + w]).then_inc(hidden.sem, 1)
                            if g % B == B - 1:
                                rest_of_weights(piece, g // B)

                    def go_down(i, par, piece):
                        for g in range(GD):
                            f, (c, w) = g // B, cols[g % B]
                            dve.wait_ge(down_made.sem, d0 + GD * (2 * i + par) + g + 1)
                            dve.wait_ge(added.sem, h0 + GD * (2 * i + par - 1) + g + 1)
                            ve.tensor_tensor(hT[:, f, c:c + w], hT[:, f, c:c + w], banks[:, 4 + g % 4, 0:w], ALU.add)\
                                .then_inc(added.sem, 1)
                            if piece and g % (GD // SL) == GD // SL - 1:
                                rest_of_weights(piece, g // (GD // SL))

                    for s in range(2):
                        rest_of_weights((0, 0, 0), s)
                    for n in range(B * KT + 1):
                        if n < B * KT:
                            k, (c, w) = n % KT, cols[n // KT]
                            norm_wait(dve, "factor", n // KT + 1)
                            norm_wait(dve, "split", n - 3)
                            n_["scaled"].by(ve.scalar_tensor_tensor(u_tmp[:, n % 4, 0:w], hT[:, k, c:c + w], G(gain, k),
                                                                    rT[:, c:c + w], ALU.mult, ALU.mult))
                        if n > 0:
                            k, (c, w) = (n - 1) % KT, cols[(n - 1) // KT]
                            norm_wait(dve, "high", n)
                            n_["split"].by(rest(u_lo[:, k, c:c + w], u_tmp[:, (n - 1) % 4, 0:w], u_hi[:, k, c:c + w]))
                    for s in range(2, SL):
                        rest_of_weights((0, 0, 0), s)
                    schedule(dve, go_up, go_down)
            for x, n in ((up_made, GU), (relu, GU), (hidden, GU), (squared, GU), (a_high, GU), (down_made, GD), (added, GD),
                         (high[0], SL), (high[1], SL), (split[0], SL), (split[1], SL)):
                x.count += n * CHUNKS
        open_late()

    WINDOWS = (2, 4, 8, 16)

    def pool_mixer(prefetch):
        with ExitStack() as ctx:
            x = sb(ctx, "pool_x", [P, KT, TOK])
            sums = [x, sb(ctx, "pool_s", [P, KT, TOK])]
            groups = [(g, f) for g in range(4) for f in range(2)]
            ring = Banks(["dve"] * len(groups), [(len(groups) - 1, J["pool"])])
            placed, ready = sig("pool_placed"), sig("pool_ready")
            p0, d0 = placed.count, ready.count
            with nc.Block() as block:
                @block.sync
                def _(sp):
                    issue(sp, prefetch)

                @block.scalar
                def _(act):
                    placed.by(se.copy(x[:, :, 0:META], uT[:, :, SEQ:TOK]))
                    placed.by(se.copy(x[:, :, META:TOK], uT[:, :, 0:SEQ]))

                @block.vector
                def _(dve):
                    step = chained(dve, "dve_step")
                    dve.wait_ge(placed.sem, p0 + 2)
                    for g, w in enumerate(WINDOWS):
                        a, b_ = sums[g % 2], sums[1 - g % 2]
                        step(ve.tensor_tensor(b_[:, 2 * g:, w - 1:TOK], a[:, 2 * g:, w - 1:TOK],
                                              a[:, 2 * g:, w - 1 - w // 2:TOK - w // 2], ALU.add))
                        f = slice(2 * g, 2 * g + 2)
                        ready.by(ve.scalar_tensor_tensor(uT[:, f, 0:SEQ], b_[:, f, META:TOK], 1.0 / w, uT[:, f, 0:SEQ],
                                                         ALU.mult, ALU.subtract))
                    for n, (g, f) in enumerate(groups):
                        ring.wait_made(dve, n)
                        k = 2 * g + f
                        ring.emptied["dve"].by(ve.scalar_tensor_tensor(hT[:, k, 0:SEQ], ring.at(n), G("pool", k), hT[:, k, 0:SEQ],
                                                                       ALU.mult, ALU.add))

                @block.tensor
                def _(pe):
                    w_ = weight(pe, J["pool"])
                    for n, (g, f) in enumerate(groups):
                        pe.wait_ge(ready.sem, d0 + g + 1)
                        for k in range(2):
                            ins = te.matmul(ring.at(n), w_[:, 2 * g + k, P * f:P * f + P], uT[:, 2 * g + k, 0:SEQ],
                                            start=k == 0, stop=k == 1)
                        ring.made.by(ins)

    def project_in2(qa, ka, va, iq, ik, iw, qb, kb, vb, lr, rg, mask):
        groups, ends = [], []

        def add(kind, j, n):
            groups.extend((kind, J[j], f) for f in range(n))

        for kind, j, n in (("iq", "idx", 2), ("ik", "idx", 1), ("iw", "idx", 1), ("qb", "qkb", 2), ("kb", "qkb", 2),
                           ("lr", "lr", 1), ("vb", "vb", QT), ("rg", "rg", 4), ("qa", "qa", 4), ("ka", "ka", 4), ("va", "va", QT)):
            add(kind, j, n)
            if kind not in ("iq", "ik", "qb"):
                ends.append((len(groups) - 1, J[j]))
        first_rest = 4
        ring = Banks(["act"] * len(groups), ends, ring=4)
        place = {"iq": (iq, 0), "qb": (qb, 0), "kb": (kb, 0), "rg": (rg, 0), "qa": (qa, 0), "ka": (ka, 0)}
        column = {"iq": 0, "ik": 256, "iw": 288, "qb": 0, "kb": 256, "lr": 0, "vb": 0, "rg": 0, "qa": 0, "ka": 0, "va": 0}
        units = [(i, h) for i in range(1, QT) for h in range(IDX_HEADS)]
        s = {x: sig("idx_" + x) for x in ("made", "relu", "added", "chosen")}
        s0 = {x: y.count for x, y in s.items()}

        def wait(engine, x, n):
            if n > 0:
                engine.wait_ge(s[x].sem, s0[x] + n)

        with ExitStack() as ctx:
            relued = sb(ctx, "idx_relu", [P, 2, SEQ])
            score = sb(ctx, "idx_score", [P, SEQ])
            work = sb(ctx, "idx_work", [P, SEQ])
            top = sb(ctx, "idx_top", [P, 8])

            with nc.Block() as block:
                @block.sync
                def _(sp):
                    issue(sp, J["out2"][1] + 1)

                @block.tensor
                def _(pe):
                    def project(n):
                        kind, j, f = groups[n]
                        w_ = weight(pe, j)
                        ring.wait_empty(pe, n)
                        c = column[kind]
                        if kind == "iw":
                            for i in range(QT):
                                for k in range(KT):
                                    ins = te.matmul(ring.at(n)[:, 8 * i:8 * i + 8], uT[:, k, P * i:P * i + P],
                                                    w_[:, k, c:c + 8], start=k == 0, stop=k == KT - 1)
                        else:
                            for k in range(KT):
                                if kind in ("va", "vb"):
                                    ins = te.matmul(ring.at(n), uT[:, k, P * f:P * f + P], w_[:, k, :],
                                                    start=k == 0, stop=k == KT - 1)
                                else:
                                    m = {"ik": IDX_DIM, "lr": GATE_RANK}.get(kind, P)
                                    ins = te.matmul(ring.at(n)[0:m, :], w_[:, k, c + P * f:c + P * f + m], uT[:, k, 0:SEQ],
                                                    start=k == 0, stop=k == KT - 1)
                        ring.made.by(ins)

                    for n in range(first_rest):
                        project(n)
                    ring.wait_emptied(pe, first_rest - 1)
                    for u, (i, h) in enumerate(units):
                        wait(pe, "relu", u - 3)
                        r = slice(IDX_DIM * (h % 4), IDX_DIM * (h % 4) + IDX_DIM)
                        s["made"].by(te.matmul(banks[:, 4 + h % 4, 0:P * (i + 1)], iq[r, h // 4, P * i:P * i + P],
                                               ik[r, 0:P * (i + 1)], start=True, stop=True))
                    for n in range(first_rest, len(groups)):
                        project(n)

                @block.scalar
                def _(act):
                    def empty(n):
                        kind, j, f = groups[n]
                        ring.wait_made(act, n)
                        x = ring.at(n)
                        if kind == "ik":
                            for r in range(4):
                                ins = se.copy(ik[IDX_DIM * r:IDX_DIM * r + IDX_DIM, :], x[0:IDX_DIM, :])
                        elif kind == "iw":
                            ins = se.mul(iw[:].rearrange("p i h -> p (i h)"), x[:, 0:QT * IDX_HEADS], IDX_HEADS ** -0.5)
                        elif kind == "lr":
                            ins = se.copy(lr[0:GATE_RANK, :], x[0:GATE_RANK, :])
                        elif kind in ("va", "vb"):
                            ins = se.copy((va if kind == "va" else vb)[:, f, :], x)
                        elif kind == "qb":
                            ins = se.mul(qb[:, f, :], x, B_KEY ** -0.5)
                        elif kind == "rg":
                            ins = se.activation(rg[:, f, :], x, ACT.Silu)
                        else:
                            ins = se.copy(place[kind][0][:, f, :], x)
                        ring.emptied["act"].by(ins)

                    for n in range(first_rest):
                        empty(n)
                    for u, (i, h) in enumerate(units):
                        wait(act, "made", u + 1)
                        wait(act, "added", u - 1)
                        s["relu"].by(se.activation(relued[:, u % 2, 0:P * (i + 1)], banks[:, 4 + h % 4, 0:P * (i + 1)],
                                                   ACT.Relu, scale=IDX_DIM ** -0.5))
                    for n in range(first_rest, len(groups)):
                        empty(n)

                @block.vector
                def _(dve):
                    step = chained(dve, "dve_step")
                    ring.wait_emptied(dve, first_rest - 1)
                    for u, (i, h) in enumerate(units):
                        n = P * (i + 1)
                        wait(dve, "relu", u + 1)
                        wait(dve, "added", u)
                        x, g = relued[:, u % 2, 0:n], iw[:, i, h:h + 1]
                        if h == 0:
                            s["added"].by(ve.tensor_scalar(score[:, 0:n], x, g, None, ALU.mult))
                            continue
                        s["added"].by(ve.scalar_tensor_tensor(score[:, 0:n], x, g, score[:, 0:n], ALU.mult, ALU.add))
                        if h < IDX_HEADS - 1:
                            continue
                        wait(dve, "added", u + 1)
                        step(ve.tensor_tensor(score[:, n - P:n], score[:, n - P:n], C("causal"), ALU.add))
                        src = score
                        for _ in range(TOPK // 8):
                            step(ve.max(top[:], src[:, 0:n]))
                            step(ve.match_replace(work[:, 0:n], top[:], src[:, 0:n], -3e38))
                            src = work
                        step(ve.tensor_scalar(mask[:, i - 1, 0:n], work[:, 0:n], -2e38, 8 * NEG, ALU.is_ge, ALU.mult))

    def gla(qb, kb, vb, lr, rg, oT):
        with ExitStack() as ctx:
            b = sb(ctx, "gla_b", [P, 2, SEQ])
            diff = sb(ctx, "gla_diff", [P, 2, SEQ])
            e = sb(ctx, "gla_e", [P, 2, SEQ])
            qd = sb(ctx, "gla_qd", [P, 2, SEQ])
            kd = sb(ctx, "gla_kd", [P, 2, SEQ])
            att = sb(ctx, "gla_att", [P, HEADS * QT, P])
            decay = sb(ctx, "gla_decay", [P, 2, QT])
            w2 = sb(ctx, "gla_w2", [GATE_RANK, 2 * P])
            d = Decay(2, False, qb, kb, b, diff, e, qd, kd)
            a = {s: sig("gla_" + s) for s in ("w2", "gate", "made", "log", "keys", "from_end", "exp", "decayed", "turned",
                                              "ktok", "grown", "state", "out", "squared", "gated", "sums", "factor")}
            a0 = {s: x.count for s, x in a.items()}

            def wait(engine, s, n):
                if n > 0:
                    engine.wait_ge(a[s].sem, a0[s] + n)

            with nc.Block() as block:
                @block.sync
                def _(sp):
                    a["w2"].by(sp.dma_start(w2[:], t["gla_gate_w2"]), 16)

                @block.scalar
                def _(act):
                    step = chained(act, "act_step")
                    for f in range(2):
                        wait(act, "made", f + 1)
                        ins = se.activation(b[:, f, :], banks[:, f, :], ACT.Identity, bias=G("gate_b", f))
                    step(ins)
                    step(se.activation(diff[:], b[:], ACT.Abs))
                    step(se.activation(diff[:], diff[:], ACT.Exp, scale=-1.0))
                    a["log"].by(se.activation(diff[:], diff[:], ACT.Ln, bias=C("one")))
                    for l in range(len(LEVELS)):
                        decay_exp(act, d, l)

                @block.vector
                def _(dve):
                    step = chained(dve, "dve_step")
                    ve.memset(att[:], 0.0)
                    wait(dve, "log", 1)
                    step(ve.scalar_tensor_tensor(diff[:], b[:], 0.0, diff[:], ALU.min, ALU.subtract))
                    step(ve.tensor_scalar(diff[:], diff[:], 1.0 / GATE_TEMP, None, ALU.mult))
                    for f in range(2):
                        ins = ve.tensor_tensor_scan(b[:, f, :], C("scan")[:, 0:SEQ], diff[:, f, :], 0.0, ALU.mult, ALU.add)
                    step(ins)
                    for l in range(len(LEVELS)):
                        decay_diffs(dve, d, l)
                        decay_scale(dve, ve.tensor_tensor, d, l, "q")
                        if l >= 1:
                            decay_keep(dve, d, l - 1, 0, att, None)
                    for l in (len(LEVELS) - 1, len(LEVELS)):
                        decay_keep(dve, d, l, 0, att, None)

                @block.gpsimd
                def _(pool):
                    for l in range(len(LEVELS)):
                        decay_scale(pool, ge.tensor_tensor, d, l, "k")

                @block.tensor
                def _(pe):
                    wait(pe, "w2", 16)
                    for f in range(2):
                        a["made"].by(te.matmul(banks[:, f, :], w2[:, P * f:P * f + P], lr[0:GATE_RANK, :], start=True, stop=True))
                    for l in range(len(LEVELS) + 1):
                        decay_products(pe, d, l, 0, 2)

            ktok = diff[:].rearrange("p f n -> p (f n)").rearrange("p (c n) -> p c n", c=QT)
            states = qd[:].rearrange("p f n -> p (f n)").rearrange("p (c n) -> p c n", c=QT)
            squares = sb(ctx, "gla_squares", [P, HEADS, SEQ])
            by_chunk = lambda x: x.rearrange("p f (c t) -> p f c t", t=P)
            with nc.Block() as block:
                @block.vector
                def _(dve):
                    step = chained(dve, "dve_step")
                    ends = by_chunk(b[:])[:, :, :, P - 1:P]
                    a["from_end"].by(ve.tensor_tensor(by_chunk(kd[:]), ends.to_broadcast([P, 2, QT, P]), by_chunk(b[:]),
                                                      ALU.subtract))
                    wait(dve, "exp", 3)
                    a["decayed"].by(ve.tensor_tensor(kd[:], kd[:], kb[:], ALU.mult))
                    a["decayed"].by(ve.tensor_tensor(e[:], e[:], qb[:], ALU.mult))
                    for c in range(QT):
                        wait(dve, "turned", c + 1)
                        a["ktok"].by(ve.tensor_copy(ktok[:, c, :], banks[:, c, 0:2 * P]))
                    a["state"].by(ve.memset(states[:, 0, :], 0.0))
                    for c in range(QT - 1):
                        wait(dve, "grown", c + 1)
                        wait(dve, "state", c + 1)
                        for f in range(2):
                            s = slice(P * f, P * f + P)
                            ins = ve.scalar_tensor_tensor(states[:, c + 1, s], states[:, c, s], decay[:, f, c:c + 1],
                                                          banks[:, 4 + c % 2, s], ALU.mult, ALU.add)
                        a["state"].by(ins)
                    for h in range(HEADS):
                        wait(dve, "squared", h + 1)
                        a["gated"].by(ve.scalar_tensor_tensor(oT[:, HEADS + h, 0:SEQ], banks[:, h, :], G("gla_out"), rg[:, h, :],
                                                              ALU.mult, ALU.mult))
                    for h in range(HEADS):
                        wait(dve, "factor", h + 1)
                        wait(dve, "gated", h + 1)
                        step(ve.tensor_tensor(oT[:, HEADS + h, 0:SEQ], oT[:, HEADS + h, 0:SEQ], squares[:, h, :], ALU.mult))

                @block.scalar
                def _(act):
                    a["exp"].by(se.activation(e[:], b[:], ACT.Exp))
                    a["exp"].by(se.activation(decay[:], by_chunk(b[:])[:, :, :, P - 1], ACT.Exp))
                    wait(act, "from_end", 1)
                    a["exp"].by(se.activation(kd[:], kd[:], ACT.Exp))
                    for h in range(HEADS):
                        wait(act, "out", h + 1)
                        a["squared"].by(se.activation(squares[:, h, :], banks[:, h, :], ACT.Square))
                    step = chained(act, "act_step")
                    for h in range(HEADS):
                        wait(act, "sums", h + 1)
                        a["factor"].by(factors(act, step, banks[:, 4 + h, :], P, SEQ, squares[:, h, :], HDIM))

                @block.tensor
                def _(pe):
                    wait(pe, "decayed", 1)
                    for c in range(QT):
                        for f in range(2):
                            ins = te.transpose(banks[:, c, P * f:P * f + P], kd[:, f, P * c:P * c + P], C("ident"))
                        a["turned"].by(ins)
                    for c in range(QT - 1):
                        wait(pe, "ktok", c + 1)
                        wait(pe, "state", c)
                        for h in range(HEADS):
                            f, r = h // 2, 64 * (h % 2)
                            ins = te.matmul(banks[r:r + 64, 4 + c % 2, P * f:P * f + P], ktok[:, c, 64 * h:64 * h + 64],
                                            vb[:, c, P * h:P * h + P], start=True, stop=True)
                        a["grown"].by(ins)
                    wait(pe, "decayed", 2)
                    wait(pe, "ktok", QT)
                    wait(pe, "state", QT)
                    for h in range(HEADS):
                        f, r = h // 2, 64 * (h % 2)
                        for c in range(QT):
                            o = banks[:, h, P * c:P * c + P]
                            te.matmul(o, vb[:, c, P * h:P * h + P], att[:, QT * h + c, :], start=True, stop=False)
                            ins = te.matmul(o, states[r:r + 64, c, P * f:P * f + P], e[r:r + 64, f, P * c:P * c + P],
                                            start=False, stop=True)
                        a["out"].by(ins)
                    for h in range(HEADS):
                        wait(pe, "squared", h + 1)
                        a["sums"].by(te.matmul(banks[:, 4 + h, :], C("ones"), squares[:, h, :], start=True, stop=True))

    def sparse_attention(qa, ka, va, mask, oT):
        with ExitStack() as ctx:
            squares = sb(ctx, "dsa_squares", [P, 2, SEQ])
            bias = sb(ctx, "dsa_bias", [P, A_HEADS, 2, P])
            vec = sb(ctx, "dsa_vec", [A_HEADS, 3 * P])
            far = sb(ctx, "dsa_far", [A_HEADS, 1])
            rel = sb(ctx, "dsa_rel", [N_BUCKETS, A_HEADS])
            scratch = nc.dram_tensor("bias_by_distance", (A_HEADS, P, 3 * P), F32, kind="Internal")
            a = {s: sig("dsa_" + s) for s in ("rel", "rel_made", "vec", "kept", "bias", "squared", "sums", "factor", "normed")}
            a0 = {s: x.count for s, x in a.items()}

            def wait(engine, s, n):
                if n > 0:
                    engine.wait_ge(a[s].sem, a0[s] + n)

            both = [(x, f) for x in (qa, ka) for f in range(4)]
            with nc.Block() as block:
                @block.sync
                def _(sp):
                    a["rel"].by(sp.dma_start(rel[:], t["rel_bias"]), 16)
                    wait(sp, "vec", 1)
                    a["kept"].by(sp.dma_start(scratch.ap(), vec[:].unsqueeze(1).to_broadcast([A_HEADS, P, 3 * P])), 16)
                    wait(sp, "kept", 16)
                    for u in range(2):
                        src = bass.AP(scratch, 2 * P - 1 - P * u, [[3 * P - 1, P], [3 * P * P, A_HEADS], [1, P]])
                        a["bias"].by(sp.dma_start(bias[:, :, u, :], src), 16)

                @block.tensor
                def _(pe):
                    wait(pe, "rel", 16)
                    a["rel_made"].by(te.matmul(banks[0:A_HEADS, 7, 0:3 * P], rel[:], C("onehot", N_BUCKETS), start=True, stop=True))
                    for n in range(8):
                        wait(pe, "squared", n + 1)
                        wait(pe, "factor", n - 3)
                        a["sums"].by(te.matmul(banks[:, n % 4, :], C("pair"), squares[:, n % 2, :], start=True, stop=True))

                @block.scalar
                def _(act):
                    step = chained(act, "act_step")
                    for n, (x, f) in enumerate(both):
                        if n >= 1:
                            wait(act, "normed", n - 1)
                        a["squared"].by(se.activation(squares[:, n % 2, :], x[:, f, :], ACT.Square))
                        wait(act, "sums", n + 1)
                        a["factor"].by(factors(act, step, banks[:, n % 4, :], P, SEQ, squares[:, n % 2, :], A_DIM))

                @block.vector
                def _(dve):
                    step = chained(dve, "dve_step")
                    wait(dve, "rel_made", 1)
                    step(ve.tensor_copy(vec[:], banks[0:A_HEADS, 7, 0:3 * P]))
                    step(ve.tensor_copy(far[:], vec[:, 0:1]))
                    a["vec"].by(ve.tensor_scalar(vec[:], vec[:], far[:], 8.0, ALU.subtract, ALU.mult))
                    for n, (x, f) in enumerate(both):
                        wait(dve, "factor", n + 1)
                        a["normed"].by(ve.scalar_tensor_tensor(x[:, f, :], x[:, f, :], G("qn2" if n < 4 else "kn2"),
                                                               squares[:, n % 2, :], ALU.mult, ALU.mult))

            units = [(h, i) for h in range(A_HEADS) for i in range(QT)]
            probs = sb(ctx, "dsa_probs", [P, 2, SEQ])
            pT = sb(ctx, "dsa_pT", [P, 2, QT, P])
            stat = sb(ctx, "dsa_stat", [P, 4, len(units)])
            s = {x: sig("att_" + x) for x in ("scored", "max", "exp", "probs", "turned", "moved", "out", "stored")}
            s0 = {x: y.count for x, y in s.items()}

            def waits(engine, x, n):
                if n > 0:
                    engine.wait_ge(s[x].sem, s0[x] + n)

            with nc.Block() as block:
                @block.tensor
                def _(pe):
                    wait(pe, "bias", 32)

                    def scores(n):
                        h, i = units[n]
                        waits(pe, "max", n - 1)
                        r, f, keys = slice(64 * (h % 2), 64 * (h % 2) + 64), h // 2, P * (i + 1)
                        o = banks[:, n % 2, 0:keys]
                        te.matmul(o, qa[r, f, P * i:P * i + P], ka[r, f, 0:keys], start=True, stop=True)
                        for u in range(min(2, i + 1)):
                            c = P * (i - u)
                            ins = te.matmul(banks[:, n % 2, c:c + P], C("ident"), bias[:, h, u, :], start=False, stop=True,
                                            skip_group_check=True)
                        s["scored"].by(ins)

                    def turn(n):
                        h, i = units[n]
                        waits(pe, "probs", n + 1)
                        waits(pe, "moved", n - 1)
                        for j in range(i + 1):
                            ins = te.transpose(banks[:, 2 + n % 2, P * j:P * j + P], probs[:, n % 2, P * j:P * j + P], C("ident"))
                        s["turned"].by(ins)

                    def weigh(n):
                        h, i = units[n]
                        waits(pe, "moved", n + 1)
                        waits(pe, "stored", n - 1)
                        o = banks[64 * (h % 2):64 * (h % 2) + 64, 4 + n % 2, 0:P]
                        for j in range(i + 1):
                            ins = te.matmul(o, va[:, j, A_DIM * h:A_DIM * h + A_DIM], pT[:, n % 2, j, :], start=j == 0, stop=j == i)
                        s["out"].by(ins)

                    for n in range(len(units) + 2):
                        if n < len(units):
                            scores(n)
                        if 1 <= n <= len(units):
                            turn(n - 1)
                        if n >= 2:
                            weigh(n - 2)

                @block.vector
                def _(dve):
                    step = chained(dve, "dve_step")
                    for n in range(len(units) + 2):
                        if n >= 2:
                            h, i = units[n - 2]
                            waits(dve, "turned", n - 1)
                            waits(dve, "out", n - 3)
                            s["moved"].by(ve.tensor_copy(pT[:, n % 2, 0:i + 1, :],
                                                         banks[:, 2 + n % 2, 0:P * (i + 1)].rearrange("p (j t) -> p j t", t=P)))
                        if n < len(units):
                            h, i = units[n]
                            waits(dve, "scored", n + 1)
                            waits(dve, "turned", n - 1)
                            keys = P * (i + 1)
                            m = mask[:, i - 1, 0:keys] if i else C("causal")
                            step(ve.tensor_tensor_reduce(probs[:, n % 2, 0:keys], banks[:, n % 2, 0:keys], m, A_DIM ** -0.5,
                                                         -3e38, ALU.add, ALU.max, stat[:, 0, n:n + 1]))
                            s["max"].by(ve.tensor_scalar(stat[:, 1, n:n + 1], stat[:, 0, n:n + 1], -1.0, None, ALU.mult))
                        if 1 <= n <= len(units):
                            h, i = units[n - 1]
                            waits(dve, "exp", n)
                            step(ve.reciprocal(stat[:, 3, n - 1:n], stat[:, 2, n - 1:n]))
                            x = probs[:, (n - 1) % 2, 0:P * (i + 1)]
                            s["probs"].by(ve.tensor_scalar(x, x, stat[:, 3, n - 1:n], None, ALU.mult))

                @block.scalar
                def _(act):
                    for n in range(len(units) + 2):
                        if n < len(units):
                            h, i = units[n]
                            waits(act, "max", n + 1)
                            x = probs[:, n % 2, 0:P * (i + 1)]
                            s["exp"].by(se.activation(x, x, ACT.Exp, bias=stat[:, 1, n:n + 1], accum_out=stat[:, 2, n:n + 1]))
                        if n >= 2:
                            h, i = units[n - 2]
                            r = slice(64 * (h % 2), 64 * (h % 2) + 64)
                            waits(act, "out", n - 1)
                            s["stored"].by(se.copy(oT[r, h // 2, P * i:P * i + P], banks[r, 4 + n % 2, 0:P]))

    SLOTS = CHUNK
    PAIRS, QUADS = EXPERTS // 2, EXPERTS // 4
    PASSES = SEQ // SLOTS

    def expert_weights(sp, src, quad, slot, dst, s):
        e, rows = 4 * quad + slot, src.shape[1]
        x = src[e] if isinstance(e, int) else src.rearrange("e a b -> (e a) b")[bass.ds(e * rows, rows), :]
        sp.dma_start(dst, x.rearrange("(k p) n -> p k n", p=P)).then_inc(s[slot].sem, 16)

    def mixture():
        with ExitStack() as ctx:
            wdn = sb(ctx, "moe_down", [P, 4, 2, D])
            xtok = sb(ctx, "moe_x", [P, QT, D])
            w_r = sb(ctx, "moe_router", [P, KT, GROUPS + EXPERTS])
            b_r = sb(ctx, "moe_router_bias", [1, GROUPS + EXPERTS])
            rowi = sb(ctx, "moe_row", [P, QT, 2], I32)
            turn = sb(ctx, "moe_turn", [P, QT, 2])
            gate = sb(ctx, "moe_gate", [P, QT, 2])
            place = sb(ctx, "moe_place", [P, QT, EXPERTS])
            more = sb(ctx, "moe_more", [P, 1], I32)
            hn = nc.dram_tensor("moe_tokens", (SEQ, D), F32, kind="Internal")
            y = nc.dram_tensor("moe_results", (EXPERTS * SLOTS, D), F32, kind="Internal")
            a = {s: sig("moe_" + s) for s in ("router", "turned", "moved", "logits", "chosen", "counted", "hn_kept",
                                              "exps")}
            a0 = {s: x.count for s, x in a.items()}
            in_loaded = [sig(f"expert_in_loaded{i}") for i in range(4)]
            down_loaded = [sig(f"expert_down_loaded{i}") for i in range(4)]

            def load_in(sp, quad, slot):
                expert_weights(sp, t["w_exp_gate"], quad, slot, wbuf[slot][:, :, 0:D_EXPERT], in_loaded)
                expert_weights(sp, t["w_exp_up"], quad, slot, wbuf[slot][:, :, D_EXPERT:], in_loaded)

            def load_down(sp, quad, slot):
                expert_weights(sp, t["w_exp_down"], quad, slot, wdn[:, slot], down_loaded)

            def wait(engine, s, n):
                if n > 0:
                    engine.wait_ge(a[s].sem, a0[s] + n)

            turns = [(x, i, b_) for i in range(QT) for x in range(2) for b_ in range(2)]
            L = GROUPS + EXPERTS
            with ExitStack() as rc:
                utok = sb(rc, "moe_utok", [P, QT, D])
                lg = sb(rc, "router_logits", [P, QT, L])
                t4 = [sb(rc, f"router_g{n}", [P, QT, GROUPS]) for n in range(4)]
                t8 = [sb(rc, f"router_e{n}", [P, QT, PER_GROUP]) for n in range(4)]
                t32 = sb(rc, "router_ge", [P, QT, GROUPS, PER_GROUP])
                pick = [sb(rc, f"router_pick{n}", [P, QT, EXPERTS]) for n in range(2)]
                both = sb(rc, "router_both", [P, QT, EXPERTS])
                pos = sb(rc, "router_pos", [P, QT, EXPERTS])
                c1 = [sb(rc, f"router_c{n}", [P, QT]) for n in range(6)]
                rowf = sb(rc, "router_row", [P, QT, 2])
                count = sb(rc, "router_count", [P, EXPERTS])
                morf = sb(rc, "router_more", [P, 1])
                with nc.Block() as block:
                    @block.sync
                    def _(sp):
                        a["router"].by(sp.dma_start(w_r[:, :, 0:GROUPS], t["w_router_group"].rearrange("(k p) n -> p k n", p=P)), 16)
                        a["router"].by(sp.dma_start(w_r[:, :, GROUPS:], t["w_router_expert"].rearrange("(k p) n -> p k n", p=P)), 16)
                        a["router"].by(sp.dma_start(b_r[:, 0:GROUPS], t["b_router_group"]), 16)
                        a["router"].by(sp.dma_start(b_r[:, GROUPS:], t["b_router_expert"]), 16)
                        sp.wait_ge(*job_done[J["out2"][1]])
                        for slot in range(4):
                            load_in(sp, 0, slot)
                            load_down(sp, 0, slot)
                        for i in range(QT):
                            wait(sp, "moved", 4 * i + 4)
                            a["hn_kept"].by(sp.dma_start(hn.ap()[P * i:P * i + P, :], utok[:, i, :]), 16)
                        wait(sp, "hn_kept", 16 * QT)

                    @block.tensor
                    def _(pe):
                        wait(pe, "router", 64)
                        for i in range(QT):
                            o = banks[:, 7, L * i:L * i + L]
                            for k in range(KT):
                                te.matmul(o, uT[:, k, P * i:P * i + P], w_r[:, k, :], start=k == 0, stop=False)
                            ins = te.matmul(o, C("ones", 1), b_r[:], start=False, stop=True)
                        a["logits"].by(ins)
                        for n, (x, i, b_) in enumerate(turns):
                            wait(pe, "moved", n - 3)
                            for k in range(4):
                                ins = te.transpose(banks[:, n % 4, P * k:P * k + P], (uT, hT)[x][:, 4 * b_ + k, P * i:P * i + P],
                                                   C("ident"))
                            a["turned"].by(ins)
                        wait(pe, "chosen", 1)
                        for i in range(QT):
                            for j in range(i + 1):
                                ins = te.matmul(banks[:, 6, EXPERTS * i:EXPERTS * i + EXPERTS], C("tri") if j == i else C("ones"),
                                                both[:, j, :], start=j == 0, stop=j == i)
                        for j in range(QT):
                            ins = te.matmul(banks[:, 6, EXPERTS * QT:EXPERTS * QT + EXPERTS], C("ones"), both[:, j, :],
                                            start=j == 0, stop=j == QT - 1)
                        a["counted"].by(ins)

                    @block.scalar
                    def _(act):
                        for n, (x, i, b_) in enumerate(turns):
                            wait(act, "turned", n + 1)
                            a["moved"].by(se.copy((utok, xtok)[x][:, i, 512 * b_:512 * b_ + 512], banks[:, n % 4, :]))
                        wait(act, "chosen", 1)
                        a["exps"].by(se.activation(t4[3][:], t4[3][:], ACT.Exp))
                        a["exps"].by(se.activation(c1[4][:], c1[4][:], ACT.Exp))

                    @block.vector
                    def _(dve):
                        step = chained(dve, "dve_step")
                        tt = lambda o, x, z, op: step(ve.tensor_tensor(o, x, z, op))
                        wait(dve, "logits", 1)
                        step(ve.tensor_copy(lg[:], banks[:, 7, 0:QT * L].rearrange("p (i l) -> p i l", i=QT)))

                        def first_largest(x, ids, m, eq, one, n):
                            step(ve.tensor_reduce(m[:], x, AX, ALU.max))
                            tt(eq, x, m[:].unsqueeze(2).to_broadcast([P, QT, n]), ALU.is_equal)
                            tt(eq, eq, ids.unsqueeze(1).to_broadcast([P, QT, n]), ALU.mult)
                            step(ve.tensor_reduce(c1[5][:], eq, AX, ALU.max))
                            tt(one, eq, c1[5][:].unsqueeze(2).to_broadcast([P, QT, n]), ALU.is_equal)

                        G_, E_ = lg[:, :, 0:GROUPS], lg[:, :, GROUPS:]
                        gmax, m1, m2, x5 = c1[0], c1[1], c1[2], c1[4]
                        first_largest(G_, C("down")[:, 0:GROUPS], gmax, t4[0][:], t4[1][:], GROUPS)
                        group = t4[1]
                        tt(t4[3][:], G_, gmax[:].unsqueeze(2).to_broadcast([P, QT, GROUPS]), ALU.subtract)
                        tt(t32[:], E_.rearrange("p i (g e) -> p i g e", g=GROUPS),
                           group[:].unsqueeze(3).to_broadcast([P, QT, GROUPS, PER_GROUP]), ALU.mult)
                        step(ve.tensor_reduce(t8[0][:], t32[:].rearrange("p i g e -> p i e g"), AX, ALU.add))
                        first_largest(t8[0][:], C("down"), m1, t8[1][:], t8[2][:], PER_GROUP)
                        step(ve.scalar_tensor_tensor(t8[0][:], t8[2][:], NEG, t8[0][:], ALU.mult, ALU.add))
                        first_largest(t8[0][:], C("down"), m2, t8[1][:], t8[3][:], PER_GROUP)
                        for n, o in enumerate((t8[2], t8[3])):
                            tt(pick[n][:].rearrange("p i (g e) -> p i g e", g=GROUPS),
                               group[:].unsqueeze(3).to_broadcast([P, QT, GROUPS, PER_GROUP]),
                               o[:].unsqueeze(2).to_broadcast([P, QT, GROUPS, PER_GROUP]), ALU.mult)
                        tt(both[:], pick[0][:], pick[1][:], ALU.add)
                        a["chosen"].by(ve.tensor_tensor(x5[:], m2[:], m1[:], ALU.subtract))
                        wait(dve, "exps", 2)
                        step(ve.tensor_reduce(c1[3][:], t4[3][:], AX, ALU.add))
                        step(ve.tensor_scalar(m1[:], x5[:], 1.0, None, ALU.add))
                        tt(m1[:], m1[:], c1[3][:], ALU.mult)
                        step(ve.reciprocal(m1[:], m1[:]))
                        step(ve.tensor_copy(gate[:, :, 0], m1[:]))
                        tt(gate[:, :, 1], m1[:], x5[:], ALU.mult)
                        wait(dve, "counted", 1)
                        step(ve.tensor_copy(pos[:], banks[:, 6, 0:QT * EXPERTS].rearrange("p (i e) -> p i e", i=QT)))
                        step(ve.tensor_copy(count[:], banks[:, 6, QT * EXPERTS:(QT + 1) * EXPERTS]))
                        step(ve.scalar_tensor_tensor(place[:], pos[:], 1.0, both[:], ALU.add, ALU.mult))
                        step(ve.tensor_scalar(place[:], place[:], -1.0, None, ALU.add))
                        for n in range(2):
                            tt(both[:], pos[:], pick[n][:], ALU.mult)
                            step(ve.tensor_reduce(rowf[:, :, n], both[:], AX, ALU.add))
                            tt(pick[n][:], pick[n][:], C("eids").unsqueeze(1).to_broadcast([P, QT, EXPERTS]), ALU.mult)
                        step(ve.tensor_scalar(turn[:], rowf[:], float(SLOTS), None, ALU.is_ge))
                        for p in range(2, PASSES):
                            step(ve.scalar_tensor_tensor(turn[:], rowf[:], float(SLOTS * p), turn[:], ALU.is_ge, ALU.add))
                        step(ve.scalar_tensor_tensor(rowf[:], turn[:], -float(SLOTS), rowf[:], ALU.mult, ALU.add))
                        for n in range(2):
                            step(ve.tensor_reduce(c1[5][:], pick[n][:], AX, ALU.add))
                            step(ve.scalar_tensor_tensor(rowf[:, :, n], c1[5][:], float(SLOTS), rowf[:, :, n], ALU.mult, ALU.add))
                        step(ve.tensor_copy(rowi[:], rowf[:]))
                        step(ve.tensor_reduce(c1[5][:, 0:1], count[:], AX, ALU.max))
                        step(ve.tensor_scalar(morf[:], c1[5][:, 0:1], float(SLOTS + 1), None, ALU.is_ge))
                        for p in range(2, PASSES):
                            step(ve.scalar_tensor_tensor(morf[:], c1[5][:, 0:1], float(SLOTS * p + 1), morf[:], ALU.is_ge, ALU.add))
                        step(ve.tensor_copy(more[:], morf[:]))

            with ExitStack() as ec:
                slot_oh = sb(ec, "moe_slot_onehot", [P, EXPERTS, SLOTS])
                idx = sb(ec, "moe_idx", [P, PAIRS], I32)
                cur = sb(ec, "moe_cur", [P, 2, 1], I32)
                xg = sb(ec, "moe_gathered", [P, 2, D])
                xT = sb(ec, "moe_xT", [P, KT, P])
                sl = sb(ec, "moe_silu", [P, D_EXPERT])
                hid = sb(ec, "moe_hidden", [P, D_EXPERT])
                hT2 = sb(ec, "moe_hidden_turned", [P, 2, P])
                yt = sb(ec, "moe_y", [P, 2, D])
                held = sig("moe_held")
                gate_p = sb(ec, "moe_gate_of_pass", [P, QT, 2])
                per = {"onehot": QT, "listed": QT, "idx": 1, "cur": PAIRS, "gathered0": 8 * PAIRS,
                       "gathered1": 8 * PAIRS, "turned": 2 * PAIRS, "xT": 2 * PAIRS, "up": PAIRS, "silu": PAIRS,
                       "hidden": PAIRS, "hid_turned": PAIRS, "hid_moved": PAIRS, "down": PAIRS, "moved": 2 * PAIRS,
                       "stored0": 8 * PAIRS, "stored1": 8 * PAIRS,
                       "back0": 16 * QT, "back1": 16 * QT, "gates": 2, "shifted": 2, "added0": QT, "added": QT}
                m = {s: sig("exp_" + s) for s in per}

                tokens_in_dram = a["hn_kept"].sem, a["hn_kept"].count

                def at(engine, p, s, n):
                    engine.wait_ge(m[s].sem, p * per[s] + n)

                def inc(ins, s, n=1):
                    ins.then_inc(m[s].sem, n)

                def passes(engine, one):
                    one(0)
                    n = engine.value_load(more[0:1, 0:1], min_val=0, max_val=PASSES - 1)
                    with engine.If(n):
                        with engine.Fori(1, n + 1) as p:
                            one(p)

                with nc.Block() as block:
                    @block.sync
                    def _(sp):
                        def one(p):
                            def load(i):
                                for b in range(2):
                                    for slot in (2 * b, 2 * b + 1):
                                        at(sp, p, "up", 2 * i + b - 1)
                                        load_in(sp, i, slot)
                                    for slot in (2 * b, 2 * b + 1):
                                        at(sp, p, "down", 2 * i + b - 1)
                                        load_down(sp, i, slot)

                            if not isinstance(p, int):
                                load(0)
                            with sp.Fori(1, QUADS) as i:
                                load(i)
                        passes(sp, one)

                    @block.gpsimd
                    def _(pool):
                        def hold():
                            pool.sem_inc(held.sem, 1)

                        def one(p):
                            at(pool, p, "idx", 1)
                            hold()

                            def gather(i, b):
                                inc(ge.tensor_copy(cur[:, b, :], idx[:, bass.ds(2 * i + b, 1)]), "cur")
                                at(pool, p, "cur", 2 * i + b + 1)
                                hold()
                                g = pool.indirect_dma_start(xg[:, b, :], None, hn.ap(),
                                                            bass.IndirectOffsetOnAxis(ap=cur[:, b, :], axis=0))
                                inc(g, f"gathered{b}", 16)

                            gather(0, 0)
                            gather(0, 1)
                            with pool.Fori(1, QUADS) as i:
                                for b in range(2):
                                    at(pool, p, "turned", 4 * i + 2 * b - 2)
                                    hold()
                                    gather(i, b)
                            at(pool, p, "turned", 4 * QUADS)
                            hold()
                            for b in range(2):
                                at(pool, p, f"stored{b}", 16 + 8 * PAIRS)
                            for i in range(QT):
                                b = i % 2
                                if i >= 2:
                                    at(pool, p, "added", i - 1)
                                hold()
                                for n, o in enumerate((xg, yt)):
                                    g = pool.indirect_dma_start(o[:, b, :], None, y.ap(),
                                                                bass.IndirectOffsetOnAxis(ap=rowi[:, i, n:n + 1], axis=0))
                                    inc(g, f"back{b}", 16)
                            at(pool, p, "added", QT)
                            hold()
                        passes(pool, one)

                    @block.vector
                    def _(dve):
                        def one(p):
                            if not isinstance(p, int):
                                inc(ve.tensor_scalar(place[:], place[:], -float(SLOTS), None, ALU.add), "shifted")
                                inc(ve.tensor_scalar(turn[:], turn[:], -1.0, None, ALU.add), "shifted")
                                at(dve, p, "shifted", 0)
                            for i in range(QT):
                                if i > 0:
                                    at(dve, p, "listed", i)
                                inc(ve.tensor_tensor(slot_oh[:], C("slot").unsqueeze(1).to_broadcast([P, EXPERTS, SLOTS]),
                                                     place[:, i, :].unsqueeze(2).to_broadcast([P, EXPERTS, SLOTS]), ALU.is_equal),
                                    "onehot")
                            at(dve, p, "listed", QT)
                            inc(ve.tensor_copy(idx[:], banks[:, 7, 0:PAIRS]), "idx")
                            inc(ve.tensor_scalar(gate_p[:], turn[:], 0.0, None, ALU.is_equal), "gates")
                            at(dve, p, "gates", 1)
                            inc(ve.tensor_tensor(gate_p[:], gate_p[:], gate[:], ALU.mult), "gates")
                            with dve.Fori(0, QUADS) as i:
                                for b in range(2):
                                    for h in range(2):
                                        at(dve, p, "turned", 4 * i + 2 * b + h + 1)
                                        inc(ve.tensor_copy(xT[:, 4 * h:4 * h + 4, :],
                                                           banks[:, h, :].rearrange("p (k t) -> p k t", k=4)), "xT")
                                    at(dve, p, "silu", 2 * i + b + 1)
                                    inc(ve.tensor_tensor(hid[:], sl[:], banks[:, 2 + b, D_EXPERT:], ALU.mult), "hidden")
                                    at(dve, p, "hid_turned", 2 * i + b + 1)
                                    inc(ve.tensor_copy(hT2[:], banks[:, 6, 0:2 * P].rearrange("p (f t) -> p f t", f=2)),
                                        "hid_moved")
                            at(dve, p, "gates", 2)
                            for i in range(QT):
                                b = i % 2
                                at(dve, p, f"back{b}", 32 * (i // 2 + 1))
                                for n, (o, s) in enumerate(((xg, "added0"), (yt, "added"))):
                                    inc(ve.scalar_tensor_tensor(xtok[:, i, :], o[:, b, :], gate_p[:, i, n:n + 1],
                                                                xtok[:, i, :], ALU.mult, ALU.add), s)
                                    at(dve, p, s, i + 1)
                        passes(dve, one)

                    @block.tensor
                    def _(pe):
                        def one(p):
                            for i in range(QT):
                                at(pe, p, "onehot", i + 1)
                                for n in range(PAIRS):
                                    ins = te.matmul(banks[:, 7, n:n + 1],
                                                    slot_oh[:, 2 * n:2 * n + 2, :].rearrange("p e s -> p (e s)"),
                                                    C("tokid")[:, i:i + 1], start=i == 0 and n == 0, stop=i == QT - 1,
                                                    skip_group_check=True)
                                inc(ins, "listed")
                            with pe.Fori(0, QUADS) as i:
                                for b in range(2):
                                    at(pe, p, f"gathered{b}", 16 * i + 16)
                                    for h in range(2):
                                        for k in range(4):
                                            ins = te.transpose(banks[:, h, P * k:P * k + P],
                                                               xg[:, b, P * (4 * h + k):P * (4 * h + k) + P], C("ident"))
                                        inc(ins, "turned")
                                    at(pe, p, "xT", 4 * i + 2 * b + 2)
                                    for h in range(2):
                                        pe.wait_ge(in_loaded[2 * b + h].sem, p * 32 * QUADS + 32 * i + 32)
                                    for k in range(KT):
                                        for h in range(2):
                                            r = slice(SLOTS * h, SLOTS * h + SLOTS)
                                            ins = te.matmul(banks[r, 2 + b, :], xT[:, k, r], wbuf[2 * b + h][:, k, :],
                                                            start=k == 0, stop=k == KT - 1)
                                    inc(ins, "up")
                                    at(pe, p, "hidden", 2 * i + b + 1)
                                    for f in range(2):
                                        ins = te.transpose(banks[:, 6, P * f:P * f + P], hid[:, P * f:P * f + P], C("ident"))
                                    inc(ins, "hid_turned")
                                    at(pe, p, "hid_moved", 2 * i + b + 1)
                                    at(pe, p, "moved", 4 * i + 2 * b + 2)
                                    for h in range(2):
                                        pe.wait_ge(down_loaded[2 * b + h].sem, p * 16 * QUADS + 16 * i + 16)
                                    for f in range(2):
                                        for c in range(2):
                                            for h in range(2):
                                                r = slice(SLOTS * h, SLOTS * h + SLOTS)
                                                ins = te.matmul(banks[r, 4 + c, :], hT2[:, f, r],
                                                                wdn[:, 2 * b + h, f, 512 * c:512 * c + 512],
                                                                start=f == 0, stop=f == 1)
                                    inc(ins, "down")
                        passes(pe, one)

                    @block.scalar
                    def _(act):
                        def one(p):
                            if not isinstance(p, int):
                                at(act, p, "added", 0)
                                act.wait_ge(*tokens_in_dram)
                            with act.Fori(0, QUADS) as i:
                                for b in range(2):
                                    at(act, p, "up", 2 * i + b + 1)
                                    inc(se.activation(sl[:], banks[:, 2 + b, 0:D_EXPERT], ACT.Silu), "silu")
                                    at(act, p, "down", 2 * i + b + 1)
                                    at(act, p, f"stored{b}", 16 * i + 16)
                                    for c in range(2):
                                        inc(se.copy(yt[:, b, 512 * c:512 * c + 512], banks[:, 4 + c, :]), "moved")
                                    at(act, p, "moved", 4 * i + 2 * b + 4)
                                    inc(act.dma_start(y.ap()[bass.ds((2 * i + b) * P, P), :], yt[:, b, :]),
                                        f"stored{b}", 16)
                        for b in range(2):
                            act.sem_inc(m[f"stored{b}"].sem, 16)
                        act.sem_inc(m["moved"].sem, 2)
                        passes(act, one)

            written = sig("out_written")
            with nc.Block() as block:
                @block.sync
                def _(sp):
                    for i in range(QT):
                        written.by(sp.dma_start(out[0, P * i:P * i + P, :], xtok[:, i, :]), 16)
                    sp.wait_ge(written.sem, written.count)

    w_in, w2 = t["w_in"], t["w_in_2"]
    J = {}
    for name, c in (("hf", 512), ("hq", 0), ("hi", 1024), ("hg", 1536), ("cq", 2048)):
        J[name] = job(w_in[:, c:c + 512])
    J["kr"] = job(w_in[:, 2560:2624])
    J["q_up"] = job(t["w_q_up"][:, 0:512], Q_RANK), job(t["w_q_up"][:, 512:768], Q_RANK)
    J["kv_up"] = job(t["w_kv_up"][:, 0:512], KV_RANK), job(t["w_kv_up"][:, 512:1024], KV_RANK)
    J["out"] = job(t["w_out"][:, 0:512]), job(t["w_out"][:, 512:1024])
    J["mlp0"] = mlp_jobs(t["w_mlp_up"][0])
    J["pool"] = job(t["pool_w"].rearrange("g c e -> (g c) e"))
    J["mlp1"] = mlp_jobs(t["w_mlp_up"][1])
    for name, c, n in (("idx", O_IQ, 296), ("qkb", O_QB, 512), ("lr", O_LR, GATE_RANK), ("vb", O_VB, 512), ("rg", O_RG, 512),
                       ("qa", O_QA, 512), ("ka", O_KA, 512), ("va", O_VA, 512)):
        J[name] = job(w2[:, c:c + n])
    J["out2"] = job(t["w_out_2"][:, 0:512]), job(t["w_out_2"][:, 512:1024])

    def finish():
        with nc.Block() as block:
            @block.sync
            def _(sp):
                for s in signals.values():
                    if s.count and (s.sem.name if hasattr(s.sem, "name") else "").startswith("w_load"):
                        sp.wait_ge(s.sem, s.count)

    with root:
        open_late()
        load_input()
        norm("mix0", HALVES)
        mixer0 = ExitStack()
        q = sb(mixer0, "q", [P, HEADS, TOK])
        k_ = sb(mixer0, "k", [P, HEADS, TOK])
        sg = sb(mixer0, "sg", [P, HEADS, TOK])
        cT = sb(mixer0, "cT", [P, 4, TOK])
        krT = sb(mixer0, "krT", [ROPE, TOK])
        v = sb(mixer0, "v", [P, QT + 1, 512])
        project_in(q, k_, sg, cT, krT, v)
        oT = sb(mixer0, "oT", [P, KT, TOK])
        hgrn(q, k_, sg, v, oT)
        kr = sb(mixer0, "kr", [ROPE, HEADS, TOK])
        qr = sg[0:ROPE]
        mla_heads(q, k_, qr, kr, krT, cT, v)
        mla_attention(q, k_, qr, kr[:], v, oT)
        project_out(oT, J["out"], HALVES, J["mlp0"] + 2)
        mixer0.close()
        mlp(J["mlp0"], "mlp0", t["w_mlp_up"][0], t["w_mlp_down"][0], HALVES)
        norm("mix1", HALVES)
        pool_mixer(J["mlp1"] + 2)
        mlp(J["mlp1"], "mlp1", t["w_mlp_up"][1], t["w_mlp_down"][1], REAL)
        norm("norm1", [(0, SEQ)])
        mixer1 = ExitStack()
        qa, ka, va, vb, rg = (sb(mixer1, n, [P, 4, SEQ]) for n in ("qa", "ka", "va", "vb", "rg"))
        qb, kb = (sb(mixer1, n, [P, 2, SEQ]) for n in ("qb", "kb"))
        lr = sb(mixer1, "lr", [GATE_RANK, SEQ])
        mask = sb(mixer1, "mask", [P, QT - 1, SEQ])
        idx = ExitStack()
        iq = sb(idx, "iq", [P, 2, SEQ])
        ik = sb(idx, "ik", [P, SEQ])
        iw = sb(idx, "iw", [P, QT, IDX_HEADS])
        project_in2(qa, ka, va, iq, ik, iw, qb, kb, vb, lr, rg, mask)
        idx.close()
        gla(qb, kb, vb, lr, rg, uT)
        sparse_attention(qa, ka, va, mask, uT)
        project_out(uT, J["out2"], [(0, SEQ)], 0)
        mixer1.close()
        norm("norm2", [(0, SEQ)])
        mixture()
        finish()
        late.close()


_NAMES = ("x", "meta_tokens", "mix_norm", "mlp_norm", "w_mlp_up", "w_mlp_down", "w_in", "hgrn_lb", "hgrn_out_norm",
          "mla_q_a_norm", "mla_kv_a_norm", "w_q_up", "w_kv_up", "q_norm", "k_norm", "w_out", "pool_w", "pool_scale",
          "norm1_g_2", "w_in_2", "q_norm_g_2", "k_norm_g_2", "rel_bias_2", "gla_gate_w2_2", "gla_gate_b_2",
          "gla_out_norm_g_2", "w_out_2", "norm2_g_2", "w_router_group_2", "b_router_group_2", "w_router_expert_2",
          "b_router_expert_2", "w_exp_gate_2", "w_exp_up_2", "w_exp_down_2")
_LEADING_ONE = ("w_in", "w_q_up", "w_kv_up", "w_out", "pool_w", "w_in_2", "gla_gate_w2_2", "w_out_2",
                "w_router_group_2", "w_router_expert_2", "w_exp_gate_2", "w_exp_up_2", "w_exp_down_2")
_KEEP_SUFFIX = ("w_in_2", "w_out_2")


def kernel(**inputs):
    import concourse.bacc as bacc
    from concourse import mybir
    from concourse.bass_utils import run_bass_kernel_spmd

    nc = bacc.Bacc("TRN2", target_bir_lowering=False, num_devices=1)
    arrays, t = {}, {}
    for name in _NAMES:
        a = np.ascontiguousarray(inputs[name])
        arrays["in_" + name] = a
        ap = nc.dram_tensor("in_" + name, a.shape, mybir.dt.from_np(a.dtype), kind="ExternalInput").ap()
        if name in _LEADING_ONE:
            ap = ap[0]
        t[name if name in _KEEP_SUFFIX else name.removesuffix("_2")] = ap
    arrays["constants"] = constant_table()
    t["constants"] = nc.dram_tensor("constants", (P, CONSTS), mybir.dt.float32, kind="ExternalInput").ap()
    arrays["level_masks"] = level_masks()
    t["level_masks"] = nc.dram_tensor("level_masks", (P, P * 8), mybir.dt.float32, kind="ExternalInput").ap()
    out = nc.dram_tensor("out", (1, SEQ, D), mybir.dt.float32, kind="ExternalOutput").ap()
    program(nc, t, out)
    r = run_bass_kernel_spmd(nc, [arrays], core_ids=[0])
    return r.results[0]["out"]
```

```python
import math

import numpy as np

P = 128
D = 1024
KT = D // P
SEQ = 512
META = 16
TOK = SEQ + META
CHUNK = 64
D_FF = 4 * D
EPS = 1e-6
HEADS = 4
HDIM = 128
NOPE, ROPE, QK = 128, 64, 192
Q_RANK = KV_RANK = 256
IN_COLS = 4 * 512 + Q_RANK + KV_RANK + ROPE
A_HEADS, A_DIM = 8, 64
IDX_HEADS, IDX_DIM = 8, 32
TOPK = min(256, SEQ // 4)
N_BUCKETS, MAX_DISTANCE = 32, 128
B_KEY = 64
GATE_RANK, GATE_TEMP = 16, 16.0
GROUPS, PER_GROUP, EXPERTS, D_EXPERT = 4, 8, 32, 256
NEG = -1e30
QT = SEQ // P
TILES = [(P * i, P) for i in range(QT)] + [(SEQ, META)]
HALF = TOK // 2
REAL = [(0, SEQ // 2), (SEQ // 2, SEQ // 2)]
HALVES = [(0, HALF), (HALF, HALF)]
LEVELS = (64, 32, 16, 8, 4, 2, 1)

O_QA, O_KA, O_VA, O_IQ = 0, 512, 1024, 1536
O_IK, O_IW, O_QB, O_KB, O_VB, O_LR, O_RG = 1792, 1824, 1832, 2088, 2344, 2856, 2872
PROJ = 3384

GAIN_ROWS = {}
for _n, _c in (("mix0", 8), ("mix1", 8), ("mlp0", 8), ("mlp1", 8), ("norm1", 8), ("norm2", 8), ("pool", 8),
               ("hgrn_out", 1), ("qa", 2), ("kva", 2), ("q_norm", 2), ("k_norm", 2), ("qn2", 1), ("kn2", 1),
               ("gate_b", 2), ("gla_out", 1)):
    GAIN_ROWS[_n] = (sum(c for _, c in GAIN_ROWS.values()), _c)
GAINS = sum(c for _, c in GAIN_ROWS.values())

CONST_COLS = {}
for _n, _c in (("ident", P), ("ones", P), ("pair", P), ("causal", P), ("cos", TOK), ("sin", TOK),
               ("rot", 64), ("eps", 1), ("one", 1), ("half_ind", P), ("neg64", 64), ("scan", TOK), 
               ("onehot", 3 * P), ("slot", CHUNK), ("tri", P), ("tokid", QT), ("eids", EXPERTS), ("down", PER_GROUP)):
    CONST_COLS[_n] = (sum(c for _, c in CONST_COLS.values()), _c)
CONSTS = sum(c for _, c in CONST_COLS.values())


def t5_buckets(n):
    d = np.arange(n)
    exact = N_BUCKETS // 2
    large = exact + (np.log(np.maximum(d, 1).astype(np.float32) / np.float32(exact))
                     / np.float32(math.log(MAX_DISTANCE / exact)) * np.float32(N_BUCKETS - exact)).astype(np.int32)
    return np.where(d < exact, d, np.minimum(large, N_BUCKETS - 1))


def constant_table():
    c = np.zeros((P, CONSTS), np.float32)

    def put(name, a):
        o, n = CONST_COLS[name]
        a = np.asarray(a, np.float32)
        c[:a.shape[0], o:o + n] = a

    i = np.arange(P)
    put("ident", np.eye(P))
    put("ones", np.ones((P, P)))
    put("pair", (i[:, None] // 64 == i[None, :] // 64))
    put("causal", np.where(i[None, :] <= i[:, None], 0.0, NEG))
    pos = np.concatenate([np.arange(SEQ) + META, np.arange(META)]).astype(np.float32)
    half = ROPE // 2
    inv = (np.float32(10000.0) ** (-np.arange(half, dtype=np.float32) / half)).astype(np.float32)
    ang = inv[:, None] * pos[None, :]
    put("cos", np.concatenate([np.cos(ang)] * 2, 0))
    put("sin", np.concatenate([np.sin(ang)] * 2, 0))
    rot = np.zeros((64, 64))
    for j in range(half):
        rot[half + j, j] = -1.0
        rot[j, half + j] = 1.0
    put("rot", rot)
    put("eps", np.full((P, 1), EPS))
    put("one", np.ones((P, 1)))
    put("half_ind", (i[None, :] < 64))
    put("neg64", np.full((1, 64), NEG))
    scan = np.ones(TOK)
    scan[[P * j for j in range(QT)] + [SEQ]] = 0.0
    put("scan", np.tile(scan, (P, 1)))
    b = t5_buckets(2 * P)[np.maximum(2 * P - 1 - np.arange(3 * P), 0)]
    put("onehot", np.arange(N_BUCKETS)[:, None] == b[None, :])
    put("slot", np.tile(np.arange(CHUNK), (P, 1)))
    put("tri", (i[:, None] < i[None, :]))
    put("tokid", i[:, None] + P * np.arange(QT)[None, :])
    put("eids", np.tile(np.arange(EXPERTS), (P, 1)))
    put("down", np.tile(PER_GROUP - np.arange(PER_GROUP), (P, 1)))
    return c


def level_masks():
    s, t = np.arange(P)[:, None], np.arange(P)[None, :]
    masks = [(s // (2 * m) == t // (2 * m)) & (s % (2 * m) < m) & (t % (2 * m) >= m) for m in LEVELS] + [s == t]
    return np.concatenate(masks, 1).astype(np.float32)


class Signal:

    def __init__(self, sem):
        self.sem, self.count = sem, 0

    def by(self, ins, n=1):
        ins.then_inc(self.sem, n)
        self.count += n
        return self.count


def program(nc, t, out):
    from contextlib import ExitStack
    from concourse import bass, mybir

    F32, FR, I32, U32 = mybir.dt.float32, mybir.dt.float32r, mybir.dt.int32, mybir.dt.uint32
    ACT, ALU, AX = mybir.ActivationFunctionType, mybir.AluOpType, mybir.AxisListType.X
    te, ve, se, ge = nc.tensor, nc.vector, nc.scalar, nc.gpsimd

    root = ExitStack()
    signals = {}

    def sig(name):
        if name not in signals:
            signals[name] = Signal(root.enter_context(nc.semaphore(name)))
        return signals[name]

    taken = {}

    def sb(stack, name, shape, dt=F32):
        taken[name] = taken.get(name, 0) + 1
        name += f"_{taken[name]}" if taken[name] > 1 else ""
        return stack.enter_context(nc.sbuf_tensor(name, shape, dt))

    def chained(engine, name):
        s = sig(name)

        def step(ins):
            engine.wait_ge(s.sem, s.by(ins))
        return step

    const = sb(root, "const", [P, CONSTS])
    level_mask = sb(root, "level_mask", [P, P * (len(LEVELS) + 1)], mybir.dt.uint8)
    gains = sb(root, "gains", [P, GAINS])
    hT = sb(root, "hT", [P, KT, TOK])
    rT = sb(root, "rT", [P, TOK])
    NW = 4
    wbuf = [sb(root, f"wbuf{i}", [P, KT, 512]) for i in range(2)] + [None, None]
    banks = root.enter_context(nc.psum_tensor("banks", [P, 8, 512], F32))
    uT = late = None

    def open_late():
        nonlocal uT, late
        late = ExitStack()
        wbuf[2:] = [sb(late, f"wbuf{i}", [P, KT, 512]) for i in (2, 3)]
        uT = sb(late, "uT", [P, KT, TOK])

    def C(name, rows=P, n=None):
        o, w = CONST_COLS[name]
        return const[0:rows, o:o + (n or w)]

    def G(name, j=0, rows=P):
        o = GAIN_ROWS[name][0] + j
        return gains[0:rows, o:o + 1]

    skipped = set()
    jobs = []
    issued = [0]
    w_loaded = [sig(f"w_loaded{i}") for i in range(NW)]
    job_done = {}

    def job(src, rows=D):
        n = src.shape[1]
        jobs.append((rows // P, n, src.rearrange("(k p) n -> p k n", p=P)))
        return len(jobs) - 1

    def issue(sp, upto):
        while issued[0] < min(upto, len(jobs)):
            j = issued[0]
            if jobs[j] is None:
                issued[0] += 1
                continue
            if j >= NW:
                before = max(i for i in range(j % NW, j, NW) if i not in skipped)
                sp.wait_ge(*job_done[before])
            k, n, src = jobs[j]
            w_loaded[j % NW].by(sp.dma_start(wbuf[j % NW][:, 0:k, 0:n], src), 16)
            issued[0] += 1

    ring_loads = [0] * NW

    def loads(j):
        return sum(i not in skipped for i in range(j % NW, j + 1, NW)) + ring_loads[j % NW]

    def weight(pe, j):
        pe.wait_ge(w_loaded[j % NW].sem, 16 * loads(j))
        return wbuf[j % NW]

    def load_input():
        ctx = ExitStack()
        grow = sb(ctx, "grow", [P, P])
        xtok = sb(ctx, "xtok", [P, QT + 1, D])
        mask_f = sb(ctx, "mask_f", [P, P * (len(LEVELS) + 1)])
        c_in, g_in = sig("const_loaded"), sig("gains_loaded")
        x_in = [sig(f"x_loaded{i}") for i in range(QT + 1)]
        g_zero, turned = sig("gains_zeroed"), sig("turned")
        moved = [sig("act_moved"), sig("dve_moved")]

        def move_input(copy, n, s):
            i, c0 = n // 2, 4 * (n % 2)
            col, w = TILES[i]
            s.by(copy(hT[:, c0:c0 + 4, col:col + w],
                      banks[:, n % 8, :].rearrange("p (k t) -> p k t", k=4)[:, :, 0:w]))

        with nc.Block() as block:
            @block.sync
            def _(sp):
                c_in.by(sp.dma_start(const[:], t["constants"]), 16)
                c_in.by(sp.dma_start(mask_f[:], t["level_masks"]), 16)
                for i in range(QT):
                    x_in[i].by(sp.dma_start(xtok[:, i, :], t["x"][0, i * P:(i + 1) * P, :]), 16)
                x_in[QT].by(sp.dma_start(xtok[0:META, QT, :], t["meta_tokens"]), 16)
                sp.wait_ge(g_in.sem, 16 * 20)
                issue(sp, NW)

            @block.scalar
            def _(act):
                act.wait_ge(g_zero.sem, 1)
                rows = [("mix0", t["mix_norm"][0:1], 8), ("mix1", t["mix_norm"][1:2], 8),
                        ("mlp0", t["mlp_norm"][0:1], 8), ("mlp1", t["mlp_norm"][1:2], 8),
                        ("norm1", t["norm1_g"], 8), ("norm2", t["norm2_g"], 8), ("pool", t["pool_scale"], 8),
                        ("hgrn_out", t["hgrn_out_norm"], 1), ("qa", t["mla_q_a_norm"], 2),
                        ("kva", t["mla_kv_a_norm"], 2), ("gate_b", t["gla_gate_b"], 2),
                        ("gla_out", t["gla_out_norm_g"], 1)]
                for name, src, n in rows:
                    o = GAIN_ROWS[name][0]
                    g_in.by(act.dma_start(grow[o:o + n, :], src.rearrange("a (k p) -> (a k) p", p=P)), 16)
                for name, src in (("q_norm", t["q_norm"]), ("k_norm", t["k_norm"])):
                    o = GAIN_ROWS[name][0]
                    g_in.by(act.dma_start(grow[o:o + 1, :], src[:, 0:P]), 16)
                    g_in.by(act.dma_start(grow[o + 1:o + 2, 0:ROPE], src[:, P:QK]), 16)
                for name, src in (("qn2", t["q_norm_g"]), ("kn2", t["k_norm_g"])):
                    o = GAIN_ROWS[name][0]
                    for c in (0, A_DIM):
                        g_in.by(act.dma_start(grow[o:o + 1, c:c + A_DIM], src), 16)
                for n in range(0, QT * 2 + 2, 2):
                    act.wait_ge(turned.sem, n + 1)
                    move_input(se.copy, n, moved[0])

            @block.vector
            def _(dve):
                g_zero.by(ve.memset(grow[:], 0.0))
                for n in range(1, QT * 2 + 2, 2):
                    dve.wait_ge(turned.sem, n + 1)
                    move_input(ve.tensor_copy, n, moved[1])
                dve.wait_ge(turned.sem, 2 * QT + 3)
                moved[1].by(ve.tensor_copy(gains[:], banks[:, 2, 0:GAINS]))
                dve.wait_ge(c_in.sem, 32)
                moved[1].by(ve.tensor_copy(level_mask[:], mask_f[:]))

            @block.tensor
            def _(pe):
                pe.wait_ge(c_in.sem, 32)
                for n in range(QT * 2 + 2):
                    i, c0 = n // 2, 4 * (n % 2)
                    w = TILES[i][1]
                    pe.wait_ge(x_in[i].sem, 16)
                    if n >= 8:
                        pe.wait_ge(moved[n % 2].sem, (n - 8) // 2 + 1)
                    for k in range(4):
                        ins = te.transpose(banks[:, n % 8, k * P:k * P + w],
                                           xtok[0:w, i, (c0 + k) * P:(c0 + k + 1) * P], C("ident", w, w))
                    turned.by(ins)
                pe.wait_ge(g_in.sem, 16 * 20)
                pe.wait_ge(moved[0].sem, 2)
                turned.by(te.transpose(banks[:, 2, 0:P], grow[:], C("ident")))
        ctx.close()

    def norm(gain, cols, load=None):
        n = cols[-1][0] + cols[-1][1]
        squared, summed, factor, scaled = sig("squared"), sig("summed"), sig("factor"), sig("scaled")
        s0, m0, f0 = squared.count, summed.count, factor.count
        with nc.Block() as block:
            @block.sync
            def _(sp):
                if load:
                    load(sp)

            @block.scalar
            def _(act):
                for k in range(KT):
                    squared.by(se.activation(uT[:, k, 0:n], hT[:, k, 0:n], ACT.Square))
                step = chained(act, "act_step")
                for b, (c, w) in enumerate(cols):
                    act.wait_ge(summed.sem, m0 + b + 1)
                    step(se.activation(rT[:, c:c + w], banks[:, b, 0:w], ACT.Ln, bias=C("eps"), scale=1.0 / D))
                for c, w in cols:
                    factor.by(se.activation(rT[:, c:c + w], rT[:, c:c + w], ACT.Exp, scale=-0.5))

            @block.tensor
            def _(pe):
                for k in range(KT):
                    pe.wait_ge(squared.sem, s0 + k + 1)
                    for b, (c, w) in enumerate(cols):
                        ins = te.matmul(banks[:, b, 0:w], C("ones"), uT[:, k, c:c + w], start=k == 0, stop=k == KT - 1)
                        if k == KT - 1:
                            summed.by(ins)

            @block.vector
            def _(dve):
                for b, (c, w) in enumerate(cols):
                    dve.wait_ge(factor.sem, f0 + b + 1)
                    for k in range(KT):
                        scaled.by(ve.scalar_tensor_tensor(uT[:, k, c:c + w], hT[:, k, c:c + w], G(gain, k),
                                                          rT[:, c:c + w], ALU.mult, ALU.mult))

    class Banks:

        def __init__(self, owners, ends=(), ring=8, base=0):
            self.made = sig("made")
            self.emptied = {"act": sig("act_emptied"), "dve": sig("dve_emptied")}
            self.first, self.ring, self.owners, self.base = self.made.count, ring, owners, base
            count = {e: s.count for e, s in self.emptied.items()}
            self.when = []
            for n, e in enumerate(owners):
                count[e] += 1
                self.when.append(count[e])
            for n, j in ends:
                job_done[j] = (self.made.sem, self.first + n + 1)

        def at(self, n):
            return banks[:, self.base + n % self.ring, :]

        def wait_empty(self, pe, n):
            if n >= self.ring:
                pe.wait_ge(self.emptied[self.owners[n - self.ring]].sem, self.when[n - self.ring])

        def wait_made(self, engine, n):
            engine.wait_ge(self.made.sem, self.first + n + 1)

        def wait_emptied(self, engine, n):
            engine.wait_ge(self.emptied[self.owners[n]].sem, self.when[n])

    class Decay:

        def __init__(self, tiles, meta, q, k_, b, e, qd, kd):
            self.tiles, self.meta = tiles, meta
            self.q, self.k, self.b, self.e, self.qd, self.kd = q, k_, b, e, qd, kd
            self.signals = {s: sig("decay_" + s) for s in ("diff", "exp", "q", "k", "prod", "kept")}
            self.base = {s: x.count for s, x in self.signals.items()}

        def by(self, s, ins):
            self.signals[s].by(ins)

        def wait(self, engine, s, n):
            if n > 0:
                engine.wait_ge(self.signals[s].sem, self.base[s] + n)

        def cols(self, l):
            return TOK if self.has_meta(l) else SEQ

        def has_meta(self, l):
            return self.meta and (l == len(LEVELS) or LEVELS[l] <= META // 2)

    def decay_diffs(dve, d, l):
        m, n = LEVELS[l], d.cols(l)
        d.wait(dve, "q", d.tiles * (l - 1))
        d.wait(dve, "k", d.tiles * (l - 1))
        for u in range(2):
            bv, o = (x[:, :, 0:n].rearrange("p h (b u m) -> p h b u m", u=2, m=m) for x in (d.b, d.e[l % 2]))
            r = bv[:, :, :, 0, m - 1:m].to_broadcast([P, d.tiles, n // (2 * m), m])
            x = bv[:, :, :, u, :]
            ins = ve.tensor_tensor(o[:, :, :, u, :], x if u else r, r if u else x, ALU.subtract)
        d.by("diff", ins)

    def decay_exp(act, d, l):
        n = d.cols(l)
        d.wait(act, "diff", l + 1)
        e = d.e[l % 2][:, :, 0:n]
        d.by("exp", se.activation(e, e, ACT.Exp))

    def decay_scale(engine, mul, d, l, s):
        n = d.cols(l)
        x, o = (d.q, d.qd) if s == "q" else (d.k, d.kd)
        d.wait(engine, "exp", l + 1)
        for f in range(d.tiles):
            d.wait(engine, "prod", d.tiles * (l - 1) + f + 1)
            d.by(s, mul(o[:, f, 0:n], x[:, f, 0:n], d.e[l % 2][:, f, 0:n], ALU.mult))

    def decay_products(pe, d, l, bank0, heads_per_tile):
        last = l == len(LEVELS)
        q_, k__ = (d.q, d.k) if last else (d.qd, d.kd)
        rows = P // heads_per_tile
        for h in range(HEADS):
            f, r = h // heads_per_tile, rows * (h % heads_per_tile)
            if not last:
                d.wait(pe, "q", d.tiles * l + f + 1)
                d.wait(pe, "k", d.tiles * l + f + 1)
            d.wait(pe, "kept", HEADS * (l - 1) + h + 1)
            for c in range(QT):
                s = slice(P * c, P * c + P)
                ins = te.matmul(banks[:, bank0 + h, P * c:P * c + P], k__[r:r + rows, f, s], q_[r:r + rows, f, s],
                                start=True, stop=True)
            if d.has_meta(l):
                if h == 0:
                    d.wait(pe, "kept", HEADS * l)
                s = slice(SEQ, TOK)
                ins = te.matmul(banks[0:META, bank0 + HEADS, META * h:META * h + META], k__[:, f, s], q_[:, f, s],
                                start=True, stop=True)
            if h % heads_per_tile == heads_per_tile - 1:
                d.by("prod", ins)

    def decay_keep(dve, d, l, bank0, att, att_meta):
        mask = level_mask[:, P * l:P * l + P]
        for h in range(HEADS):
            d.wait(dve, "prod", d.tiles * l + h * d.tiles // HEADS + 1)
            ins = ve.copy_predicated(att[:, QT * h:QT * h + QT, :], mask.unsqueeze(1).to_broadcast([P, QT, P]),
                                     banks[:, bank0 + h, :].rearrange("p (c t) -> p c t", c=QT))
            if d.has_meta(l) and h == HEADS - 1:
                ins = ve.copy_predicated(att_meta, mask[0:META, 0:META].unsqueeze(1).to_broadcast([META, HEADS, META]),
                                         banks[0:META, bank0 + HEADS, 0:HEADS * META].rearrange("p (h t) -> p h t", h=HEADS))
            d.by("kept", ins)

    def decay_dve(dve, d, bank0, att, att_meta):
        n = len(LEVELS)
        decay_diffs(dve, d, 0)
        for l in range(n):
            if l + 1 < n:
                decay_diffs(dve, d, l + 1)
            decay_scale(dve, ve.tensor_tensor, d, l, "q")
            if l >= 1:
                decay_keep(dve, d, l - 1, bank0, att, att_meta)
        for l in (n - 1, n):
            decay_keep(dve, d, l, bank0, att, att_meta)

    def project_in(q, k_, sg, cT, krT, v, b, qd, kd, att, att_meta, oT):
        diff, e = oT[:, 0:4, :], oT[:, 4:8, :]
        d = Decay(HEADS, True, q, k_, b, (diff, e), qd, kd)
        gate = sig("hgrn_gate")
        g0 = gate.count
        groups, ends = [], []
        for name in ("hq", "hf", "hi", "hg", "cq", "kr"):
            if name == "hi":
                groups += [(name, J[name], 0, i) for i in range(QT + 1)]
            else:
                groups += [(name, J[name], f, b_) for f in range(1 if name == "kr" else 4) for b_ in range(2)]
            ends.append((len(groups) - 1, J[name]))
        owners = ["dve" if g[0] == "hf" else "act" for g in groups]
        ring = Banks(owners, ends, ring=3, base=5)
        hf_end = 15
        assert groups[hf_end][0] == "hf" and groups[hf_end + 1][0] == "hi"
        events = [("group", n) for n in range(hf_end + 1, len(groups))]
        for l in range(len(LEVELS) + 1):
            events.insert(8 + 3 * l, ("level", l))

        def empty(n, engine):
            kind, j, f, b_ = groups[n]
            ring.wait_made(engine, n)
            c, w = TILES[b_] if kind == "hi" else HALVES[b_]
            src = ring.at(n)[:, 0:w]
            if kind == "hi":
                ins = se.copy(v[0:w, b_, :], ring.at(n)[0:w, :])
            elif kind == "hq":
                ins = se.activation(q[:, f, c:c + w], src, ACT.Silu)
            elif kind == "hf":
                ins = ve.tensor_copy(k_[:, f, c:c + w], src)
            elif kind == "kr":
                ins = se.copy(krT[0:ROPE, c:c + w], src[0:ROPE, :])
            else:
                ins = se.copy((sg if kind == "hg" else cT)[:, f, c:c + w], src)
            ring.emptied[owners[n]].by(ins)

        with nc.Block() as block:
            @block.sync
            def _(sp):
                issue(sp, J["kr"] + 1 + NW)

            @block.tensor
            def _(pe):
                def project(n):
                    kind, j, f, b_ = groups[n]
                    w_ = weight(pe, j)
                    ring.wait_empty(pe, n)
                    for k in range(KT):
                        if kind == "hi":
                            c, w = TILES[b_]
                            ins = te.matmul(ring.at(n)[0:w, :], uT[:, k, c:c + w], w_[:, k, :], start=k == 0, stop=k == KT - 1)
                        else:
                            c, w = HALVES[b_]
                            m = ROPE if kind == "kr" else P
                            ins = te.matmul(ring.at(n)[0:m, 0:w], w_[:, k, f * P:f * P + m], uT[:, k, c:c + w],
                                            start=k == 0, stop=k == KT - 1)
                    ring.made.by(ins)

                for n in range(hf_end + 1):
                    project(n)
                for what, n in events:
                    if what == "group":
                        project(n)
                    else:
                        decay_products(pe, d, n, 0, 1)

            @block.scalar
            def _(act):
                for n in range(8):
                    empty(n, act)
                ring.wait_emptied(act, hf_end)
                step = chained(act, "act_step")
                step(se.activation(diff, k_[:], ACT.Abs))
                step(se.activation(diff, diff, ACT.Exp, scale=-1.0))
                gate.by(se.activation(diff, diff, ACT.Ln, bias=C("one")))
                act.wait_ge(gate.sem, g0 + 2)
                gate.by(se.activation(k_[:], e, ACT.Exp))
                for l in range(2):
                    decay_exp(act, d, l)
                for what, n in events:
                    if what == "group":
                        empty(n, act)
                    elif n + 2 < len(LEVELS):
                        decay_exp(act, d, n + 2)
                ring.wait_emptied(act, len(groups) - 1)
                step(se.activation(sg[:], sg[:], ACT.Silu))

            @block.vector
            def _(dve):
                step = chained(dve, "dve_step")
                ve.memset(att[:], 0.0)
                ve.memset(att_meta, 0.0)
                for n in range(8, hf_end + 1):
                    empty(n, dve)
                dve.wait_ge(gate.sem, g0 + 1)
                step(ve.scalar_tensor_tensor(b[:], k_[:], 0.0, diff, ALU.min, ALU.subtract))
                ins = ve.tensor_tensor(e, b[:], k_[:], ALU.subtract)
                ins.then_inc(gate.sem, 1)
                step(ve.tensor_copy(diff, b[:]))
                for h in range(HEADS):
                    ins = ve.tensor_tensor_scan(b[:, h, :], C("scan"), diff[:, h, :], 0.0, ALU.mult, ALU.add)
                step(ins)
                dve.wait_ge(gate.sem, g0 + 3)
                decay_dve(dve, d, 0, att, att_meta)
            gate.count = g0 + 3

            @block.gpsimd
            def _(pool):
                pool.wait_ge(gate.sem, g0 + 3)
                for l in range(len(LEVELS)):
                    decay_scale(pool, ge.tensor_tensor, d, l, "k")

    def hgrn(q, k_, sg, v, b, qd, kd, att, att_meta, oT):
        with ExitStack() as ctx:
            ktok_meta = oT[0:META, 7, 0:512]
            decay = sb(ctx, "hgrn_decay", [P, HEADS, QT + 1])
            diff, e = uT[:, 0:4, :], uT[:, 4:8, :]
            ktok, states = qd, diff
            ktok = qd[:].rearrange("p h n -> p (h n)")[:, 0:QT * 512].rearrange("p (c n) -> p c n", c=QT)
            states = diff.rearrange("p h n -> p (h n)")[:, 0:QT * 512].rearrange("p (c n) -> p c n", c=QT)
            squares = b
            faded, summed, grown, scaled = sig("hgrn_faded"), sig("hgrn_turned"), sig("hgrn_grown"), sig("hgrn_states")
            order = [QT] + list(range(QT))
            a = {s: sig("hgrn_" + s) for s in ("from_end", "from_end_exp", "q_decayed", "k_decayed", "turned", "ktok",
                                               "grown", "state", "out", "squared", "gated", "sums", "factor")}
            a0 = {s: x.count for s, x in a.items()}

            def wait(engine, s, n):
                engine.wait_ge(a[s].sem, a0[s] + n)

            with nc.Block() as block:
                @block.vector
                def _(dve):
                    step = chained(dve, "dve_step")
                    ends = b[:, :, 0:SEQ].rearrange("p h (c t) -> p h c t", t=P)[:, :, :, P - 1:P]
                    ve.tensor_tensor(kd[:, :, 0:SEQ].rearrange("p h (c t) -> p h c t", t=P),
                                     ends.to_broadcast([P, HEADS, QT, P]),
                                     b[:, :, 0:SEQ].rearrange("p h (c t) -> p h c t", t=P), ALU.subtract)
                    a["from_end"].by(ve.tensor_tensor(kd[:, :, SEQ:TOK], b[:, :, TOK - 1:TOK].to_broadcast([P, HEADS, META]),
                                                      b[:, :, SEQ:TOK], ALU.subtract))
                    wait(dve, "from_end_exp", 2)
                    a["k_decayed"].by(ve.tensor_tensor(kd[:], kd[:], k_[:], ALU.mult))
                    a["q_decayed"].by(ve.tensor_tensor(e, e, q[:], ALU.mult))
                    for n, c in enumerate(order):
                        wait(dve, "turned", n + 1)
                        w = TILES[c][1]
                        dst = ktok_meta if c == QT else ktok[:, c, :]
                        a["ktok"].by(ve.tensor_copy(dst, banks[0:w, n, :]))
                    for n, c in enumerate(order[:-1]):
                        wait(dve, "grown", n + 1)
                        if n == 0:
                            ins = ve.tensor_copy(states[:, 0, :], banks[:, 5, :])
                        else:
                            wait(dve, "state", n)
                            for h in range(HEADS):
                                s = slice(P * h, P * h + P)
                                ins = ve.scalar_tensor_tensor(states[:, n, s], states[:, n - 1, s],
                                                              decay[:, h, c:c + 1], banks[:, 5 + n % 2, s],
                                                              ALU.mult, ALU.add)
                        a["state"].by(ins)
                    for h in range(HEADS + 1):
                        wait(dve, "squared", h + 1)
                        if h < HEADS:
                            o, x, g = oT[:, h, 0:SEQ], banks[:, h, :], sg[:, h, 0:SEQ]
                        else:
                            o, g = oT[:, 0:HEADS, SEQ:TOK], sg[:, :, SEQ:TOK]
                            x = banks[:, 4, 0:HEADS * META].rearrange("p (h t) -> p h t", h=HEADS)
                        a["gated"].by(ve.scalar_tensor_tensor(o, x, G("hgrn_out"), g, ALU.mult, ALU.mult))
                    for h in range(HEADS):
                        wait(dve, "factor", h + 1)
                        wait(dve, "gated", HEADS + 1)
                        step(ve.tensor_tensor(oT[:, h, :], oT[:, h, :], squares[:, h, :], ALU.mult))

                @block.scalar
                def _(act):
                    a["from_end_exp"].by(se.activation(e, b[:], ACT.Exp))
                    wait(act, "from_end", 1)
                    se.activation(decay[:, :, 0:QT], b[:, :, 0:SEQ].rearrange("p h (c t) -> p h c t", t=P)[:, :, :, P - 1], ACT.Exp)
                    se.activation(decay[:, :, QT], b[:, :, TOK - 1], ACT.Exp)
                    a["from_end_exp"].by(se.activation(kd[:], kd[:], ACT.Exp))
                    for h in range(HEADS + 1):
                        wait(act, "out", h + 1)
                        wait(act, "k_decayed", 1)
                        if h < HEADS:
                            o, x = squares[:, h, 0:SEQ], banks[:, h, :]
                        else:
                            o = squares[:, :, SEQ:TOK]
                            x = banks[:, 4, 0:HEADS * META].rearrange("p (h t) -> p h t", h=HEADS)
                        a["squared"].by(se.activation(o, x, ACT.Square))
                    step = chained(act, "act_step")
                    for h in range(HEADS):
                        wait(act, "sums", h + 1)
                        log_mean(step, squares[:, h, :].rearrange("p (b t) -> p b t", b=2), banks[:, 2 * h:2 * h + 2, 0:HALF], HDIM)
                    for h in range(HEADS):
                        a["factor"].by(factor_of(squares[:, h, :]))

                @block.tensor
                def _(pe):
                    wait(pe, "k_decayed", 1)
                    for n, c in enumerate(order):
                        col, w = TILES[c]
                        for h in range(HEADS):
                            ins = te.transpose(banks[0:w, n, P * h:P * h + P], kd[:, h, col:col + w], C("ident"))
                        a["turned"].by(ins)
                    for n, c in enumerate(order[:-1]):
                        w = TILES[c][1]
                        wait(pe, "ktok", n + 1)
                        if n >= 2:
                            wait(pe, "state", n - 1)
                        for h in range(HEADS):
                            s = slice(P * h, P * h + P)
                            x = ktok_meta[:, s] if c == QT else ktok[:, c, s]
                            ins = te.matmul(banks[:, 5 + n % 2, s], x, v[0:w, c, s], start=True, stop=True)
                        a["grown"].by(ins)
                    wait(pe, "q_decayed", 1)
                    wait(pe, "ktok", QT + 1)
                    wait(pe, "state", QT)
                    for h in range(HEADS):
                        s = slice(P * h, P * h + P)
                        for c in range(QT):
                            o = banks[:, h, P * c:P * c + P]
                            te.matmul(o, v[:, c, s], att[:, QT * h + c, :], start=True, stop=False)
                            ins = te.matmul(o, states[:, c, s], e[:, h, P * c:P * c + P], start=False, stop=True)
                        a["out"].by(ins)
                    for h in range(HEADS):
                        ins = te.matmul(banks[:, 4, META * h:META * h + META], v[0:META, QT, P * h:P * h + P],
                                        att_meta[:, h, :], start=True, stop=True)
                    a["out"].by(ins)
                    wait(pe, "squared", HEADS + 1)
                    wait(pe, "gated", HEADS + 1)
                    for h in range(HEADS):
                        for b_ in range(2):
                            ins = te.matmul(banks[:, 2 * h + b_, 0:HALF], C("ones"), squares[:, h, HALF * b_:HALF * b_ + HALF],
                                            start=True, stop=True)
                        a["sums"].by(ins)

    def log_mean(step, dst, src, width):
        step(se.activation(dst, src, ACT.Ln, bias=C("eps"), scale=1.0 / width))

    def factor_of(x):
        return se.activation(x, x, ACT.Exp, scale=-0.5)

    def mla_heads(q, k_, qr, kr, krT, cT, v):
        squares, fac = uT[:, 0:4, :], uT[:, 4:8, :]
        s = {x: sig("mla_" + x) for x in ("squared", "sums", "factor", "normed", "turned", "cosine", "sine", "done")}
        s0 = {x: y.count for x, y in s.items()}

        def wait(engine, x, n):
            engine.wait_ge(s[x].sem, s0[x] + n)

        with nc.Block() as block:
            @block.scalar
            def _(act):
                s["squared"].by(se.activation(squares, cT[:], ACT.Square))
                step = chained(act, "act_step")
                for j in range(2):
                    wait(act, "sums", j + 1)
                    log_mean(step, fac[:, j, :].rearrange("p (b t) -> p b t", b=2), banks[:, 2 * j:2 * j + 2, 0:HALF], Q_RANK)
                for j in range(2):
                    s["factor"].by(factor_of(fac[:, j, :]))

            @block.tensor
            def _(pe):
                wait(pe, "squared", 1)
                for j in range(2):
                    for b, (c, w) in enumerate(HALVES):
                        for k in range(2):
                            ins = te.matmul(banks[:, 2 * j + b, 0:w], C("ones"), squares[:, 2 * j + k, c:c + w],
                                            start=k == 0, stop=k == 1)
                    s["sums"].by(ins)

            @block.vector
            def _(dve):
                for j, g in enumerate(("qa", "kva")):
                    wait(dve, "factor", j + 1)
                    for k in range(2):
                        s["normed"].by(ve.scalar_tensor_tensor(cT[:, 2 * j + k, :], cT[:, 2 * j + k, :], G(g, k),
                                                               fac[:, j, :], ALU.mult, ALU.mult))

        groups, ends = [], []
        for h in range(HEADS):
            c = QK * h
            groups += [("q", J["q_up"][c // 512], c % 512, h, b) for b in range(2)]
            c += NOPE
            groups += [("qr", J["q_up"][c // 512], c % 512, h, b) for b in range(2)]
            if h == 2:
                ends.append((len(groups) - 3, J["q_up"][0]))
        ends.append((len(groups) - 1, J["q_up"][1]))
        for h in range(HEADS):
            groups += [("k", J["kv_up"][h // 2], 256 * (h % 2), h, b) for b in range(2)]
        groups += [("v", J["kv_up"][1], 0, 0, i) for i in range(QT + 1)]
        ends += [(len(groups) - 1, j) for j in J["kv_up"]]
        owners = [("act", "dve")[n % 2] for n in range(len(groups))]
        ring = Banks(owners, ends)

        def empty(name, engine, copy):
            for n, (kind, j, c0, h, b) in enumerate(groups):
                if owners[n] != name:
                    continue
                ring.wait_made(engine, n)
                if kind == "v":
                    ins = copy(v[0:TILES[b][1], b, :], ring.at(n)[0:TILES[b][1], :])
                else:
                    c, w = HALVES[b]
                    m = ROPE if kind == "qr" else P
                    ins = copy({"q": q, "qr": qr, "k": k_}[kind][0:m, h, c:c + w], ring.at(n)[0:m, 0:w])
                ring.emptied[name].by(ins)

        with nc.Block() as block:
            @block.sync
            def _(sp):
                issue(sp, J["out"][1] + 1)

            @block.tensor
            def _(pe):
                for n, (kind, j, c0, h, b) in enumerate(groups):
                    w_ = weight(pe, j)
                    ring.wait_empty(pe, n)
                    if kind == "v":
                        c, w = TILES[b]
                        for i, jj in enumerate(J["kv_up"]):
                            for k in range(2):
                                rhs = weight(pe, jj)[:, k, :].rearrange("p (h n) -> p h n", h=2)[:, :, NOPE:]
                                ins = te.matmul(ring.at(n)[0:w, 256 * i:256 * i + 256], cT[:, 2 + k, c:c + w], rhs,
                                                start=k == 0, stop=k == 1)
                    else:
                        c, w = HALVES[b]
                        m = ROPE if kind == "qr" else P
                        for k in range(2):
                            ins = te.matmul(ring.at(n)[0:m, 0:w], w_[:, k, c0:c0 + m],
                                            cT[:, (2 if kind == "k" else 0) + k, c:c + w], start=k == 0, stop=k == 1)
                    ring.made.by(ins)

            @block.scalar
            def _(act):
                empty("act", act, se.copy)

            @block.vector
            def _(dve):
                empty("dve", dve, ve.tensor_copy)

        s0.update({x: y.count for x, y in s.items()})
        with ExitStack() as ctx:
            sq_rope = sb(ctx, "mla_sq_rope", [ROPE, HEADS + 1, TOK])
            with nc.Block() as block:
                @block.scalar
                def _(act):
                    step = chained(act, "act_step")
                    s["squared"].by(se.activation(sq_rope[:, 0:HEADS, :], qr, ACT.Square))
                    s["squared"].by(se.activation(squares, q[:], ACT.Square))
                    s["squared"].by(se.activation(sq_rope[:, HEADS, :], krT[0:ROPE, :], ACT.Square))
                    for side in range(2):
                        for h in range(HEADS):
                            wait(act, "sums", 4 * side + h + 1)
                            if side == 1:
                                wait(act, "normed", 2 * h + 2)
                            log_mean(step, fac[:, h, :].rearrange("p (b t) -> p b t", b=2), banks[:, 2 * h:2 * h + 2, 0:HALF], QK)
                        for h in range(HEADS):
                            s["factor"].by(factor_of(fac[:, h, :]))
                        if side == 0:
                            s["squared"].by(se.activation(squares, k_[:], ACT.Square))

                @block.tensor
                def _(pe):
                    for side in range(2):
                        wait(pe, "squared", 3 + side)
                        for h in range(HEADS):
                            if side == 1:
                                wait(pe, "factor", h + 1)
                            for b, (c, w) in enumerate(HALVES):
                                te.matmul(banks[:, 2 * h + b, 0:w], C("ones"), squares[:, h, c:c + w], start=True, stop=False)
                                r = sq_rope[:, h if side == 0 else HEADS, c:c + w]
                                ins = te.matmul(banks[:, 2 * h + b, 0:w], C("ones", ROPE), r, start=False, stop=True)
                            s["sums"].by(ins)

                @block.vector
                def _(dve):
                    for h in range(HEADS):
                        wait(dve, "factor", h + 1)
                        s["normed"].by(ve.scalar_tensor_tensor(q[:, h, :], q[:, h, :], G("q_norm"), fac[:, h, :],
                                                               ALU.mult, ALU.mult))
                        if h == 0:
                            wait(dve, "squared", 3)
                        s["normed"].by(ve.scalar_tensor_tensor(qr[:, h, :], qr[:, h, :], G("q_norm", 1, ROPE),
                                                               fac[0:ROPE, h, :], ALU.mult, ALU.mult))
                    ve.tensor_scalar(krT[0:ROPE, :], krT[0:ROPE, :], G("k_norm", 1, ROPE), None, ALU.mult)
                    for h in range(HEADS):
                        wait(dve, "factor", HEADS + h + 1)
                        s["normed"].by(ve.scalar_tensor_tensor(k_[:, h, :], k_[:, h, :], G("k_norm"), fac[:, h, :],
                                                               ALU.mult, ALU.mult))

            sined = sq_rope

            def source(n):
                return qr[:, n, :] if n < HEADS else krT[0:ROPE, :]

            with nc.Block() as block:
                @block.tensor
                def _(pe):
                    for n in range(HEADS + 1):
                        if n >= 4:
                            wait(pe, "sine", n - 3)
                        for b, (c, w) in enumerate(HALVES):
                            ins = te.matmul(banks[0:ROPE, 2 * (n % 4) + b, 0:w], C("rot", ROPE), source(n)[:, c:c + w],
                                            start=True, stop=True)
                        s["turned"].by(ins)

                @block.gpsimd
                def _(pool):
                    for n in range(HEADS + 1):
                        wait(pool, "turned", n + 1)
                        s["cosine"].by(ge.tensor_tensor(source(n), source(n), C("cos", ROPE), ALU.mult))

                @block.vector
                def _(dve):
                    step = chained(dve, "dve_step")
                    sin = C("sin", ROPE).rearrange("p (b t) -> p b t", b=2)
                    for n in range(HEADS + 1):
                        wait(dve, "turned", n + 1)
                        o = sined[:, n, :].rearrange("p (b t) -> p b t", b=2)
                        s["sine"].by(ve.tensor_tensor(o, banks[0:ROPE, 2 * (n % 4):2 * (n % 4) + 2, 0:HALF], sin, ALU.mult))
                    for n in range(HEADS + 1):
                        wait(dve, "cosine", n + 1)
                        wait(dve, "sine", n + 1)
                        ins = ve.tensor_tensor(source(n), source(n), sined[:, n, :], ALU.add)
                    step(ins)
                    for h in range(HEADS):
                        ve.tensor_tensor(kr[:, h, :], krT[0:ROPE, :], fac[0:ROPE, h, :], ALU.mult)

    def mla_attention(q, k_, qr, kr, v, oT):
        units = [(h, i) for h in range(HEADS) for i in range(QT)] + [(h, QT) for h in range(HEADS)]
        scale = QK ** -0.5
        with ExitStack() as ctx:
            probs = sb(ctx, "mla_probs", [P, 2, TOK])
            pT = sb(ctx, "mla_pT", [P, 2, QT + 1, P])
            stat = sb(ctx, "mla_stat", [P, 4, len(units)])
            s = {x: sig("att_" + x) for x in ("scored", "max", "exp", "probs", "turned", "moved", "out", "stored")}
            s0 = {x: y.count for x, y in s.items()}

            def wait(engine, x, n):
                if n > 0:
                    engine.wait_ge(s[x].sem, s0[x] + n)

            def shape(n):
                h, i = units[n]
                return (h, i) + TILES[i] + (0 if i == QT else P * (i + 1),)

            def scores_at(n, w, a, b):
                return banks[0:w, 2 * (n % 2):2 * (n % 2) + 2, :].rearrange("p a b -> p (a b)")[:, a:b]

            with nc.Block() as block:
                @block.tensor
                def _(pe):
                    def scores(n):
                        h, i, c, w, real = shape(n)
                        wait(pe, "exp", n - 1)
                        if real:
                            o = scores_at(n, w, 0, real)
                            te.matmul(o, q[:, h, c:c + w], k_[:, h, 0:real], start=True, stop=False)
                            te.matmul(o, qr[:, h, c:c + w], kr[:, h, 0:real], start=False, stop=True)
                            te.matmul(scores_at(n, w, real - CHUNK, real), C("half_ind", 1), C("neg64", 1),
                                      start=False, stop=True, skip_group_check=True)
                        o = scores_at(n, w, real, real + META)
                        te.matmul(o, q[:, h, c:c + w], k_[:, h, SEQ:TOK], start=True, stop=False, skip_group_check=True)
                        s["scored"].by(te.matmul(o, qr[:, h, c:c + w], kr[:, h, SEQ:TOK], start=False, stop=True,
                                                 skip_group_check=True))

                    def turn(n):
                        h, i, c, w, real = shape(n)
                        wait(pe, "probs", n + 1)
                        for j in range(real // P):
                            te.transpose(banks[:, 4 + n % 2, P * j:P * j + w], probs[0:w, n % 2, P * j:P * j + P],
                                         C("ident", w, w))
                        wait(pe, "stored", n - 1)
                        s["turned"].by(te.transpose(banks[0:META, 6 + n % 2, P:P + w],
                                                    probs[0:w, n % 2, real:real + META], C("ident", w, w)))

                    def weigh(n):
                        h, i, c, w, real = shape(n)
                        wait(pe, "moved", n + 1)
                        wait(pe, "stored", n - 1)
                        o = banks[:, 6 + n % 2, 0:w]
                        vs = slice(P * h, P * h + P)
                        for j in range(real // P):
                            te.matmul(o, v[:, j, vs], pT[:, n % 2, j, 0:w], start=j == 0, stop=False)
                        s["out"].by(te.matmul(o, v[0:META, QT, vs], pT[0:META, n % 2, QT, 0:w], start=not real, stop=True))

                    for n in range(len(units) + 2):
                        if n < len(units):
                            scores(n)
                        if n >= 2:
                            weigh(n - 2)
                        if 1 <= n <= len(units):
                            turn(n - 1)

                @block.vector
                def _(dve):
                    step = chained(dve, "dve_step")

                    def move(n):
                        h, i, c, w, real = shape(n)
                        wait(dve, "turned", n + 1)
                        wait(dve, "out", n - 1)
                        if real:
                            ve.tensor_copy(pT[:, n % 2, 0:real // P, :],
                                           banks[:, 4 + n % 2, 0:real].rearrange("p (j t) -> p j t", t=P))
                        s["moved"].by(ve.tensor_copy(pT[0:META, n % 2, QT, 0:w], banks[0:META, 6 + n % 2, P:P + w]))

                    def maximum(n):
                        h, i, c, w, real = shape(n)
                        wait(dve, "scored", n + 1)
                        step(ve.reduce_max(stat[0:w, 0, n:n + 1], scores_at(n, w, 0, real + META), AX))
                        s["max"].by(ve.tensor_scalar(stat[0:w, 1, n:n + 1], stat[0:w, 0, n:n + 1], -scale, None, ALU.mult))

                    def normalise(n):
                        h, i, c, w, real = shape(n)
                        wait(dve, "exp", n + 1)
                        step(ve.reciprocal(stat[0:w, 3, n:n + 1], stat[0:w, 2, n:n + 1]))
                        x = probs[0:w, n % 2, 0:real + META]
                        s["probs"].by(ve.tensor_scalar(x, x, stat[0:w, 3, n:n + 1], None, ALU.mult))

                    for n in range(len(units) + 2):
                        if n >= 2:
                            move(n - 2)
                        if 1 <= n <= len(units):
                            normalise(n - 1)
                        if n < len(units):
                            maximum(n)

                @block.scalar
                def _(act):
                    for n in range(len(units) + 2):
                        if n < len(units):
                            h, i, c, w, real = shape(n)
                            wait(act, "max", n + 1)
                            wait(act, "turned", n - 1)
                            s["exp"].by(se.activation(probs[0:w, n % 2, 0:real + META], scores_at(n, w, 0, real + META),
                                                      ACT.Exp, bias=stat[0:w, 1, n:n + 1], scale=scale,
                                                      accum_out=stat[0:w, 2, n:n + 1]))
                        if n >= 2:
                            h, i, c, w, real = shape(n - 2)
                            wait(act, "out", n - 1)
                            s["stored"].by(se.copy(oT[:, HEADS + h, c:c + w], banks[:, 6 + n % 2, 0:w]))

    def split_products(o, w_hi, w_lo, x_hi, x_lo, first, last):
        te.matmul(o, w_hi, x_hi, start=first, stop=False)
        te.matmul(o, w_hi, x_lo, start=False, stop=False)
        return te.matmul(o, w_lo, x_hi, start=False, stop=last)

    def project_out(oT, pair, cols, prefetch):
        B, n_cols = len(cols), cols[-1][0] + cols[-1][1]
        groups = [(f, b) for f in range(KT) for b in range(B)]
        ring = Banks(["dve"] * len(groups))
        high, split = sig("weights_high"), sig("weights_split")
        o_high, o_split = sig("operand_high"), sig("operand_split")
        hi0, sp0, oh0, os0 = (x.count for x in (high, split, o_high, o_split))
        for n, j in enumerate(pair):
            job_done[j] = (split.sem, sp0 + 4 * n + 4)
        with ExitStack() as ctx:
            o_hi, o_lo = (sb(ctx, "out_o_" + x, [P, KT, TOK], FR) for x in ("high", "low"))
            w_hi, w_lo = (sb(ctx, "out_w_" + x, [P, KT, 512], FR) for x in ("high", "low"))
            with nc.Block() as block:
                @block.sync
                def _(sp):
                    issue(sp, prefetch)

                @block.tensor
                def _(pe):
                    for n, (f, b) in enumerate(groups):
                        c, w = cols[b]
                        ring.wait_empty(pe, n)
                        if b == 0:
                            pe.wait_ge(split.sem, sp0 + f + 1)
                        m = slice(P * (f % 4), P * (f % 4) + P)
                        for k in range(KT):
                            if n == 0:
                                pe.wait_ge(o_split.sem, os0 + k + 1)
                            ins = split_products(ring.at(n)[:, 0:w], w_hi[:, k, m], w_lo[:, k, m], o_hi[:, k, c:c + w],
                                                 o_lo[:, k, c:c + w], k == 0, k == KT - 1)
                        ring.made.by(ins)

                @block.scalar
                def _(act):
                    def round_weights(f):
                        w_ = weight(act, pair[f // 4])
                        m = slice(P * (f % 4), P * (f % 4) + P)
                        if f >= 4:
                            ring.wait_made(act, B * (f - 4) + B - 1)
                        high.by(se.copy(w_hi[:, :, m], w_[:, :, m]))

                    round_weights(0)
                    for k in range(KT):
                        o_high.by(se.copy(o_hi[:, k, 0:n_cols], oT[:, k, 0:n_cols]))
                    for f in range(1, KT):
                        round_weights(f)

                @block.vector
                def _(dve):
                    def rest_of_weights(f):
                        dve.wait_ge(high.sem, hi0 + f + 1)
                        m = slice(P * (f % 4), P * (f % 4) + P)
                        split.by(ve.tensor_tensor(w_lo[:, :, m], wbuf[pair[f // 4] % NW][:, :, m], w_hi[:, :, m].bitcast(F32),
                                                  ALU.subtract))

                    rest_of_weights(0)
                    for k in range(KT):
                        dve.wait_ge(o_high.sem, oh0 + k + 1)
                        o_split.by(ve.tensor_tensor(o_lo[:, k, 0:n_cols], oT[:, k, 0:n_cols], o_hi[:, k, 0:n_cols].bitcast(F32),
                                                    ALU.subtract))
                    for f in range(1, 4):
                        rest_of_weights(f)
                    for n, (f, b) in enumerate(groups):
                        c, w = cols[b]
                        ring.wait_made(dve, n)
                        ring.emptied["dve"].by(ve.tensor_tensor(hT[:, f, c:c + w], hT[:, f, c:c + w], ring.at(n)[:, 0:w], ALU.add))
                        if b == B - 1 and f + 4 < KT:
                            rest_of_weights(f + 4)

    FC = 512
    CHUNKS = D_FF // FC

    def mlp_jobs(up):
        while len(jobs) % NW:
            skipped.add(len(jobs))
            jobs.append(None)
        first = len(jobs)
        for c in range(2):
            job(up[:, FC * c:FC * c + FC])
        skipped.update((first + 2, first + 3))
        jobs.extend([None, None])
        return first

    def mlp(first, gain, up, down, cols):
        B, F = len(cols), FC // P
        GU, GD = F * B, KT * B
        SL = 4
        n_cols = cols[-1][0] + cols[-1][1]
        up_made, down_made, hidden = sig("up_made"), sig("down_made"), sig("hidden")
        relu, added = sig("act_emptied"), sig("dve_emptied")
        squared, a_high = sig("mlp_squared"), sig("mlp_a_high")
        high = sig("weights_high"), sig("mlp_down_high")
        split = sig("weights_split"), sig("mlp_down_split")
        u0, d0, a0, r0, h0, q0, g0 = (x.count for x in (up_made, down_made, hidden, relu, added, squared, a_high))
        hi0, sp0 = [x.count for x in high], [x.count for x in split]
        n_ = {x: sig("operand_" + x) for x in ("square", "sum", "factor", "scaled", "high", "split")}
        n0 = {x: y.count for x, y in n_.items()}
        assert min(r0, h0) >= GD + 4
        L = CHUNKS // 2 - 1
        late.close()
        with ExitStack() as ctx:
            relued = sb(ctx, "mlp_relu", [P, 2, HALF])
            sq = sb(ctx, "mlp_square", [P, 2, HALF])
            tmp = sb(ctx, "mlp_norm_tmp", [P, 2, TOK])
            a_hi, a_lo = (sb(ctx, "mlp_hidden_" + x, [P, 2, F, TOK], FR) for x in ("high", "low"))
            u_hi, u_lo = (sb(ctx, "mlp_u_" + x, [P, KT, TOK], FR) for x in ("high", "low"))
            w_hi, w_lo = ((sb(ctx, "mlp_up_" + x, [P, KT, FC], FR), sb(ctx, "mlp_down_" + x, [P, F, D], FR))
                          for x in ("high", "low"))

            def as_piece(d, b):
                w = wbuf[b][:]
                return w.rearrange("p a b -> p (a b)").rearrange("p (k n) -> p k n", k=F) if d else w

            loads0 = [loads(first + b) - 1 for b in range(2)]

            def raw(piece):
                d, i, par = piece
                c = 2 * i + par
                if d == 0:
                    b, n = (0, 1) if isinstance(c, int) and c == 0 else (1, c)
                else:
                    b, n = (1, CHUNKS) if isinstance(c, int) and c == CHUNKS - 1 else (0, c + 2)
                return as_piece(d, b), b, loads0[b] + n

            def cols_of(d, s):
                w = (D if d else FC) // SL
                return slice(w * s, w * s + w)

            def schedule(engine, go_up, go_down):
                go_up(0, 0, (0, 0, 1))
                with engine.Fori(0, L) as i:
                    go_up(i, 1, (1, i, 0))
                    go_down(i, 0, (0, i + 1, 0))
                    go_up(i + 1, 0, (1, i, 1))
                    go_down(i, 1, (0, i + 1, 1))
                go_up(L, 1, (1, L, 0))
                go_down(L, 0, (1, L, 1))
                go_down(L, 1, None)

            u_tmp = tmp[:].rearrange("p a n -> p (a n)").rearrange("p (a n) -> p a n", n=HALF)

            def norm_wait(engine, x, n):
                if n > 0:
                    engine.wait_ge(n_[x].sem, n0[x] + n)

            with nc.Block() as block:
                @block.sync
                def _(sp):
                    def load(d, c, b, x, n):
                        sp.wait_ge(split[x].sem, sp0[x] + n)
                        src = down[bass.ds(c * FC, FC), :] if d else up[:, bass.ds(c * FC, FC)]
                        sp.dma_start(as_piece(d, b), src.rearrange("(k p) n -> p k n", p=P)).then_inc(w_loaded[b].sem, 16)

                    issue(sp, first + 2)
                    load(1, 0, 0, 0, SL)
                    with sp.Fori(1, CHUNKS - 1) as c:
                        load(0, c + 1, 1, 0, SL * (c + 1))
                        load(1, c, 0, 1, SL * c)
                    load(1, CHUNKS - 1, 1, 0, SL * CHUNKS)
                    for b in range(2):
                        w_loaded[b].count += 16 * (CHUNKS - 1)
                        job_done[first + b] = (split[1].sem, sp0[1] + SL * (CHUNKS - 1 + b))
                    for b in range(2):
                        ring_loads[b] += CHUNKS - 1
                    issue(sp, first + NW + 2)

                @block.tensor
                def _(pe):
                    def go_up(i, par, _):
                        for g in range(GU):
                            f, (c, w) = g // B, cols[g % B]
                            if g % B == 0:
                                pe.wait_ge(split[0].sem, sp0[0] + SL * (2 * i + par) + f + 1)
                            pe.wait_ge(relu.sem, r0 + GU * (2 * i + par) + g - 3)
                            for k in range(KT):
                                if isinstance(i, int) and i == par == 0 and g < B:
                                    norm_wait(pe, "split", g * KT + k + 1)
                                m = slice(P * f, P * f + P)
                                ins = split_products(banks[:, g % 4, 0:w], w_hi[0][:, k, m], w_lo[0][:, k, m],
                                                     u_hi[:, k, c:c + w], u_lo[:, k, c:c + w], k == 0, k == KT - 1)
                            ins.then_inc(up_made.sem, 1)

                    def go_down(i, par, _):
                        pe.wait_ge(hidden.sem, a0 + GU * (2 * i + par + 1))
                        for g in range(GD):
                            f, (c, w) = g // B, cols[g % B]
                            if g % (GD // SL) == 0:
                                pe.wait_ge(split[1].sem, sp0[1] + SL * (2 * i + par) + g // (GD // SL) + 1)
                            pe.wait_ge(added.sem, h0 + GD * (2 * i + par) + g - 3)
                            for k in range(F):
                                m = slice(P * f, P * f + P)
                                ins = split_products(banks[:, 4 + g % 4, 0:w], w_hi[1][:, k, m],
                                                     w_lo[1][:, k, m], a_hi[:, par, k, c:c + w],
                                                     a_lo[:, par, k, c:c + w], k == 0, k == F - 1)
                            ins.then_inc(down_made.sem, 1)

                    for k in range(KT):
                        norm_wait(pe, "square", k + 1)
                        for b, (c, w) in enumerate(cols):
                            ins = te.matmul(banks[:, 4 + b, 0:w], C("ones"), tmp[:, k % 2, c:c + w], start=k == 0, stop=k == KT - 1)
                        n_["sum"].by(ins)
                    schedule(pe, go_up, go_down)

                @block.scalar
                def _(act):
                    def round_weights(piece, s):
                        d, m = piece[0], cols_of(piece[0], s)
                        w, b, n = raw(piece)
                        act.wait_ge(w_loaded[b].sem, 16 * n)
                        se.copy(w_hi[d][:, :, m], w[:, :, m]).then_inc(high[d].sem, 1)

                    def go_up(i, par, piece):
                        for g in range(GU):
                            f, (c, w) = g // B, cols[g % B]
                            n = GU * (2 * i + par) + g
                            act.wait_ge(up_made.sem, u0 + n + 1)
                            se.activation(relued[:, g % 2, 0:w], banks[:, g % 4, 0:w], ACT.Relu).then_inc(relu.sem, 1)
                            act.wait_ge(relu.sem, r0 + n + 1)
                            if not (isinstance(n, int) and n < 2):
                                act.wait_ge(hidden.sem, a0 + n - 1)
                            se.activation(sq[:, g % 2, 0:w], relued[:, g % 2, 0:w], ACT.Square).then_inc(squared.sem, 1)
                            act.wait_ge(squared.sem, q0 + n + 1)
                            se.copy(a_hi[:, par, f, c:c + w], sq[:, g % 2, 0:w]).then_inc(a_high.sem, 1)
                            if g % B == B - 1:
                                round_weights(piece, g // B)

                    def go_down(i, par, piece):
                        if piece:
                            for s in range(SL):
                                if piece[0]:
                                    act.wait_ge(down_made.sem, d0 + GD * (2 * i + par) + GD // SL * (s + 1))
                                round_weights(piece, s)

                    for k in range(KT):
                        norm_wait(act, "sum", k - 1)
                        n_["square"].by(se.activation(tmp[:, k % 2, 0:n_cols], hT[:, k, 0:n_cols], ACT.Square))
                    for s in range(2):
                        round_weights((0, 0, 0), s)
                    norm_wait(act, "sum", KT)
                    step = chained(act, "act_step")
                    for b, (c, w) in enumerate(cols):
                        step(se.activation(rT[:, c:c + w], banks[:, 4 + b, 0:w], ACT.Ln, bias=C("eps"), scale=1.0 / D))
                    for b, (c, w) in enumerate(cols):
                        n_["factor"].by(se.activation(rT[:, c:c + w], rT[:, c:c + w], ACT.Exp, scale=-0.5))
                    for n in range(B * KT):
                        k, (c, w) = n % KT, cols[n // KT]
                        norm_wait(act, "scaled", n + 1)
                        n_["high"].by(se.copy(u_hi[:, k, c:c + w], u_tmp[:, n % 4, 0:w]))
                    for s in range(2, SL):
                        round_weights((0, 0, 0), s)
                    schedule(act, go_up, go_down)

                @block.vector
                def _(dve):
                    def rest(o, x, hi):
                        return ve.tensor_tensor(o, x, hi.bitcast(F32), ALU.subtract)

                    def rest_of_weights(piece, s):
                        d, i, par = piece
                        m = cols_of(d, s)
                        dve.wait_ge(high[d].sem, hi0[d] + SL * (2 * i + par) + s + 1)
                        rest(w_lo[d][:, :, m], raw(piece)[0][:, :, m], w_hi[d][:, :, m]).then_inc(split[d].sem, 1)

                    def go_up(i, par, piece):
                        for g in range(GU):
                            f, (c, w) = g // B, cols[g % B]
                            n = GU * (2 * i + par) + g
                            dve.wait_ge(a_high.sem, g0 + n + 1)
                            rest(a_lo[:, par, f, c:c + w], sq[:, g % 2, 0:w], a_hi[:, par, f, c:c + w]).then_inc(hidden.sem, 1)
                            if g % B == B - 1:
                                rest_of_weights(piece, g // B)

                    def go_down(i, par, piece):
                        for g in range(GD):
                            f, (c, w) = g // B, cols[g % B]
                            dve.wait_ge(down_made.sem, d0 + GD * (2 * i + par) + g + 1)
                            dve.wait_ge(added.sem, h0 + GD * (2 * i + par - 1) + g + 1)
                            ve.tensor_tensor(hT[:, f, c:c + w], hT[:, f, c:c + w], banks[:, 4 + g % 4, 0:w], ALU.add)\
                                .then_inc(added.sem, 1)
                            if piece and g % (GD // SL) == GD // SL - 1:
                                rest_of_weights(piece, g // (GD // SL))

                    for s in range(2):
                        rest_of_weights((0, 0, 0), s)
                    for n in range(B * KT + 1):
                        if n < B * KT:
                            k, (c, w) = n % KT, cols[n // KT]
                            norm_wait(dve, "factor", n // KT + 1)
                            norm_wait(dve, "split", n - 3)
                            n_["scaled"].by(ve.scalar_tensor_tensor(u_tmp[:, n % 4, 0:w], hT[:, k, c:c + w], G(gain, k),
                                                                    rT[:, c:c + w], ALU.mult, ALU.mult))
                        if n > 0:
                            k, (c, w) = (n - 1) % KT, cols[(n - 1) // KT]
                            norm_wait(dve, "high", n)
                            n_["split"].by(rest(u_lo[:, k, c:c + w], u_tmp[:, (n - 1) % 4, 0:w], u_hi[:, k, c:c + w]))
                    for s in range(2, SL):
                        rest_of_weights((0, 0, 0), s)
                    schedule(dve, go_up, go_down)
            for x, n in ((up_made, GU), (relu, GU), (hidden, GU), (squared, GU), (a_high, GU), (down_made, GD), (added, GD),
                         (high[0], SL), (high[1], SL), (split[0], SL), (split[1], SL)):
                x.count += n * CHUNKS
        open_late()

    WINDOWS = (2, 4, 8, 16)

    def pool_mixer(prefetch):
        with ExitStack() as ctx:
            x = sb(ctx, "pool_x", [P, KT, TOK])
            sums = [x, sb(ctx, "pool_s", [P, KT, TOK])]
            groups = [(g, f) for g in range(4) for f in range(2)]
            ring = Banks(["dve"] * len(groups), [(len(groups) - 1, J["pool"])])
            placed, ready = sig("pool_placed"), sig("pool_ready")
            p0, d0 = placed.count, ready.count
            with nc.Block() as block:
                @block.sync
                def _(sp):
                    issue(sp, prefetch)

                @block.scalar
                def _(act):
                    placed.by(se.copy(x[:, :, 0:META], uT[:, :, SEQ:TOK]))
                    placed.by(se.copy(x[:, :, META:TOK], uT[:, :, 0:SEQ]))

                @block.vector
                def _(dve):
                    step = chained(dve, "dve_step")
                    dve.wait_ge(placed.sem, p0 + 2)
                    for g, w in enumerate(WINDOWS):
                        a, b_ = sums[g % 2], sums[1 - g % 2]
                        step(ve.tensor_tensor(b_[:, 2 * g:, w - 1:TOK], a[:, 2 * g:, w - 1:TOK],
                                              a[:, 2 * g:, w - 1 - w // 2:TOK - w // 2], ALU.add))
                        f = slice(2 * g, 2 * g + 2)
                        ready.by(ve.scalar_tensor_tensor(uT[:, f, 0:SEQ], b_[:, f, META:TOK], 1.0 / w, uT[:, f, 0:SEQ],
                                                         ALU.mult, ALU.subtract))
                    for n, (g, f) in enumerate(groups):
                        ring.wait_made(dve, n)
                        k = 2 * g + f
                        ring.emptied["dve"].by(ve.scalar_tensor_tensor(hT[:, k, 0:SEQ], ring.at(n), G("pool", k), hT[:, k, 0:SEQ],
                                                                       ALU.mult, ALU.add))

                @block.tensor
                def _(pe):
                    w_ = weight(pe, J["pool"])
                    for n, (g, f) in enumerate(groups):
                        pe.wait_ge(ready.sem, d0 + g + 1)
                        for k in range(2):
                            ins = te.matmul(ring.at(n), w_[:, 2 * g + k, P * f:P * f + P], uT[:, 2 * g + k, 0:SEQ],
                                            start=k == 0, stop=k == 1)
                        ring.made.by(ins)

    def project_in2(qa, ka, va, iq, ik, iw, qb, kb, vb, lr, rg, mask, b, diff, e, qd, kd, att):
        d = Decay(2, False, qb, kb, b, (diff, e), qd, kd)
        gates = {x: sig("gla_" + x) for x in ("w2", "made", "log")}
        gates0 = {x: y.count for x, y in gates.items()}
        groups, ends = [], []

        def add(kind, j, n):
            groups.extend((kind, J[j], f) for f in range(n))

        for kind, j, n in (("iq", "idx", 2), ("ik", "idx", 1), ("iw", "idx", 1), ("qb", "qkb", 2), ("kb", "qkb", 2),
                           ("lr", "lr", 1), ("vb", "vb", QT), ("rg", "rg", 4), ("qa", "qa", 4), ("ka", "ka", 4), ("va", "va", QT)):
            add(kind, j, n)
            if kind not in ("iq", "ik", "qb"):
                ends.append((len(groups) - 1, J[j]))
        first_rest = 4
        ring = Banks(["act"] * len(groups), ends, ring=4)
        place = {"iq": (iq, 0), "qb": (qb, 0), "kb": (kb, 0), "rg": (rg, 0), "qa": (qa, 0), "ka": (ka, 0)}
        column = {"iq": 0, "ik": 256, "iw": 288, "qb": 0, "kb": 256, "lr": 0, "vb": 0, "rg": 0, "qa": 0, "ka": 0, "va": 0}
        units = [(i, h) for i in range(1, QT) for h in range(IDX_HEADS)]
        events, left = [], len(groups) - first_rest
        for g in range(left):
            events.append(("group", first_rest + g))
            events += [("scores", u) for u in range(3 * g, min(3 * g + 3, len(units)))]
            if g == len(units) // 3:
                events.append(("gates", 0))
            if g >= left - 3 - len(LEVELS) and g < left - 2:
                events.append(("level", g - (left - 3 - len(LEVELS))))
        s = {x: sig("idx_" + x) for x in ("made", "relu", "added", "chosen")}
        s0 = {x: y.count for x, y in s.items()}

        def wait(engine, x, n):
            if n > 0:
                engine.wait_ge(s[x].sem, s0[x] + n)

        with ExitStack() as ctx:
            relued, score, work = kd, qd[:, 0, :], qd[:, 1, :]
            top = sb(ctx, "idx_top", [P, 8])
            w2 = sb(ctx, "gla_w2", [GATE_RANK, 2 * P])

            with nc.Block() as block:
                @block.sync
                def _(sp):
                    gates["w2"].by(sp.dma_start(w2[:], t["gla_gate_w2"]), 16)
                    issue(sp, J["out2"][1] + 1)

                @block.tensor
                def _(pe):
                    def project(n):
                        kind, j, f = groups[n]
                        w_ = weight(pe, j)
                        ring.wait_empty(pe, n)
                        c = column[kind]
                        if kind == "iw":
                            for i in range(QT):
                                for k in range(KT):
                                    ins = te.matmul(ring.at(n)[:, 8 * i:8 * i + 8], uT[:, k, P * i:P * i + P],
                                                    w_[:, k, c:c + 8], start=k == 0, stop=k == KT - 1)
                        else:
                            for k in range(KT):
                                if kind in ("va", "vb"):
                                    ins = te.matmul(ring.at(n), uT[:, k, P * f:P * f + P], w_[:, k, :],
                                                    start=k == 0, stop=k == KT - 1)
                                else:
                                    m = {"ik": IDX_DIM, "lr": GATE_RANK}.get(kind, P)
                                    ins = te.matmul(ring.at(n)[0:m, :], w_[:, k, c + P * f:c + P * f + m], uT[:, k, 0:SEQ],
                                                    start=k == 0, stop=k == KT - 1)
                        ring.made.by(ins)

                    for n in range(first_rest):
                        project(n)
                    ring.wait_emptied(pe, first_rest - 1)
                    for what, n in events:
                        if what == "group":
                            project(n)
                        elif what == "scores":
                            i, h = units[n]
                            wait(pe, "relu", n - 3)
                            r = slice(IDX_DIM * (h % 4), IDX_DIM * (h % 4) + IDX_DIM)
                            s["made"].by(te.matmul(banks[:, 4 + h % 4, 0:P * (i + 1)], iq[r, h // 4, P * i:P * i + P],
                                                   ik[r, 0:P * (i + 1)], start=True, stop=True))
                        elif what == "gates":
                            pe.wait_ge(gates["w2"].sem, gates0["w2"] + 16)
                            ring.wait_emptied(pe, [g[0] for g in groups].index("lr"))
                            wait(pe, "relu", len(units))
                            for f in range(2):
                                gates["made"].by(te.matmul(banks[:, 4 + f, :], w2[:, P * f:P * f + P], lr[0:GATE_RANK, :],
                                                           start=True, stop=True))
                        else:
                            decay_products(pe, d, n, 4, 2)

                @block.scalar
                def _(act):
                    def empty(n):
                        kind, j, f = groups[n]
                        ring.wait_made(act, n)
                        x = ring.at(n)
                        if kind == "ik":
                            for r in range(4):
                                ins = se.copy(ik[IDX_DIM * r:IDX_DIM * r + IDX_DIM, :], x[0:IDX_DIM, :])
                        elif kind == "iw":
                            ins = se.mul(iw[:].rearrange("p i h -> p (i h)"), x[:, 0:QT * IDX_HEADS], IDX_HEADS ** -0.5)
                        elif kind == "lr":
                            ins = se.copy(lr[0:GATE_RANK, :], x[0:GATE_RANK, :])
                        elif kind in ("va", "vb"):
                            ins = se.copy((va if kind == "va" else vb)[:, f, :], x)
                        elif kind == "qb":
                            ins = se.mul(qb[:, f, :], x, B_KEY ** -0.5)
                        elif kind == "rg":
                            ins = se.activation(rg[:, f, :], x, ACT.Silu)
                        else:
                            ins = se.copy(place[kind][0][:, f, :], x)
                        ring.emptied["act"].by(ins)

                    for n in range(first_rest):
                        empty(n)
                    step = chained(act, "act_step")
                    for what, n in events:
                        if what == "group":
                            empty(n)
                        elif what == "scores":
                            i, h = units[n]
                            wait(act, "made", n + 1)
                            wait(act, "added", n - 1)
                            s["relu"].by(se.activation(relued[:, n % 2, 0:P * (i + 1)], banks[:, 4 + h % 4, 0:P * (i + 1)],
                                                       ACT.Relu, scale=IDX_DIM ** -0.5))
                        elif what == "gates":
                            for f in range(2):
                                act.wait_ge(gates["made"].sem, gates0["made"] + f + 1)
                                ins = se.activation(b[:, f, :], banks[:, 4 + f, :], ACT.Identity, bias=G("gate_b", f))
                            step(ins)
                            step(se.activation(diff[:], b[:], ACT.Abs))
                            step(se.activation(diff[:], diff[:], ACT.Exp, scale=-1.0))
                            gates["log"].by(se.activation(diff[:], diff[:], ACT.Ln, bias=C("one")))
                        else:
                            for l in (0, 1, 2) if n == 0 else (n + 2,):
                                if l < len(LEVELS):
                                    decay_exp(act, d, l)

                @block.vector
                def _(dve):
                    step = chained(dve, "dve_step")
                    ring.wait_emptied(dve, first_rest - 1)
                    for u, (i, h) in enumerate(units):
                        n = P * (i + 1)
                        wait(dve, "relu", u + 1)
                        wait(dve, "added", u)
                        x, g = relued[:, u % 2, 0:n], iw[:, i, h:h + 1]
                        if h == 0:
                            s["added"].by(ve.tensor_scalar(score[:, 0:n], x, g, None, ALU.mult))
                            continue
                        s["added"].by(ve.scalar_tensor_tensor(score[:, 0:n], x, g, score[:, 0:n], ALU.mult, ALU.add))
                        if h < IDX_HEADS - 1:
                            continue
                        wait(dve, "added", u + 1)
                        step(ve.tensor_tensor(score[:, n - P:n], score[:, n - P:n], C("causal"), ALU.add))
                        src = score
                        for _ in range(TOPK // 8):
                            step(ve.max(top[:], src[:, 0:n]))
                            step(ve.match_replace(work[:, 0:n], top[:], src[:, 0:n], -3e38))
                            src = work
                        step(ve.tensor_scalar(mask[:, i - 1, 0:n], work[:, 0:n], -2e38, 8 * NEG, ALU.is_ge, ALU.mult))
                    ve.memset(att[:], 0.0)
                    dve.wait_ge(gates["log"].sem, gates0["log"] + 1)
                    step(ve.scalar_tensor_tensor(diff[:], b[:], 0.0, diff[:], ALU.min, ALU.subtract))
                    step(ve.tensor_scalar(diff[:], diff[:], 1.0 / GATE_TEMP, None, ALU.mult))
                    for f in range(2):
                        ins = ve.tensor_tensor_scan(b[:, f, :], C("scan")[:, 0:SEQ], diff[:, f, :], 0.0, ALU.mult, ALU.add)
                    step(ins)
                    decay_dve(dve, d, 4, att, None)

                @block.gpsimd
                def _(pool):
                    for l in range(len(LEVELS)):
                        decay_scale(pool, ge.tensor_tensor, d, l, "k")

    def gla(qb, kb, vb, rg, b, diff, e, qd, kd, att, oT):
        with ExitStack() as ctx:
            decay = sb(ctx, "gla_decay", [P, 2, QT])
            a = {s: sig("gla_" + s) for s in ("from_end", "exp", "decayed", "turned", "ktok", "grown", "state", "out",
                                              "squared", "gated", "sums", "factor")}
            a0 = {s: x.count for s, x in a.items()}

            def wait(engine, s, n):
                if n > 0:
                    engine.wait_ge(a[s].sem, a0[s] + n)

            ktok = diff[:].rearrange("p f n -> p (f n)").rearrange("p (c n) -> p c n", c=QT)
            states = qd[:].rearrange("p f n -> p (f n)").rearrange("p (c n) -> p c n", c=QT)
            squares = sb(ctx, "gla_squares", [P, HEADS, SEQ])
            by_chunk = lambda x: x.rearrange("p f (c t) -> p f c t", t=P)
            with nc.Block() as block:
                @block.vector
                def _(dve):
                    step = chained(dve, "dve_step")
                    ends = by_chunk(b[:])[:, :, :, P - 1:P]
                    a["from_end"].by(ve.tensor_tensor(by_chunk(kd[:]), ends.to_broadcast([P, 2, QT, P]), by_chunk(b[:]),
                                                      ALU.subtract))
                    wait(dve, "exp", 3)
                    a["decayed"].by(ve.tensor_tensor(kd[:], kd[:], kb[:], ALU.mult))
                    a["decayed"].by(ve.tensor_tensor(e[:], e[:], qb[:], ALU.mult))
                    for c in range(QT):
                        wait(dve, "turned", c + 1)
                        a["ktok"].by(ve.tensor_copy(ktok[:, c, :], banks[:, c, 0:2 * P]))
                    a["state"].by(ve.memset(states[:, 0, :], 0.0))
                    for c in range(QT - 1):
                        wait(dve, "grown", c + 1)
                        wait(dve, "state", c + 1)
                        for f in range(2):
                            s = slice(P * f, P * f + P)
                            ins = ve.scalar_tensor_tensor(states[:, c + 1, s], states[:, c, s], decay[:, f, c:c + 1],
                                                          banks[:, 4 + c % 2, s], ALU.mult, ALU.add)
                        a["state"].by(ins)
                    for h in range(HEADS):
                        wait(dve, "squared", h + 1)
                        a["gated"].by(ve.scalar_tensor_tensor(oT[:, HEADS + h, 0:SEQ], banks[:, h, :], G("gla_out"), rg[:, h, :],
                                                              ALU.mult, ALU.mult))
                    for h in range(HEADS):
                        wait(dve, "factor", h + 1)
                        wait(dve, "gated", h + 1)
                        step(ve.tensor_tensor(oT[:, HEADS + h, 0:SEQ], oT[:, HEADS + h, 0:SEQ], squares[:, h, :], ALU.mult))

                @block.scalar
                def _(act):
                    a["exp"].by(se.activation(e[:], b[:], ACT.Exp))
                    a["exp"].by(se.activation(decay[:], by_chunk(b[:])[:, :, :, P - 1], ACT.Exp))
                    wait(act, "from_end", 1)
                    a["exp"].by(se.activation(kd[:], kd[:], ACT.Exp))
                    for h in range(HEADS):
                        wait(act, "out", h + 1)
                        a["squared"].by(se.activation(squares[:, h, :], banks[:, h, :], ACT.Square))
                    step = chained(act, "act_step")
                    for h in range(HEADS):
                        wait(act, "sums", h + 1)
                        log_mean(step, squares[:, h, :], banks[:, 4 + h, :], HDIM)
                    for h in range(HEADS):
                        a["factor"].by(factor_of(squares[:, h, :]))

                @block.tensor
                def _(pe):
                    wait(pe, "decayed", 1)
                    for c in range(QT):
                        for f in range(2):
                            ins = te.transpose(banks[:, c, P * f:P * f + P], kd[:, f, P * c:P * c + P], C("ident"))
                        a["turned"].by(ins)
                    for c in range(QT - 1):
                        wait(pe, "ktok", c + 1)
                        wait(pe, "state", c)
                        for h in range(HEADS):
                            f, r = h // 2, 64 * (h % 2)
                            ins = te.matmul(banks[r:r + 64, 4 + c % 2, P * f:P * f + P], ktok[:, c, 64 * h:64 * h + 64],
                                            vb[:, c, P * h:P * h + P], start=True, stop=True)
                        a["grown"].by(ins)
                    wait(pe, "decayed", 2)
                    wait(pe, "ktok", QT)
                    wait(pe, "state", QT)
                    for h in range(HEADS):
                        f, r = h // 2, 64 * (h % 2)
                        for c in range(QT):
                            o = banks[:, h, P * c:P * c + P]
                            te.matmul(o, vb[:, c, P * h:P * h + P], att[:, QT * h + c, :], start=True, stop=False)
                            ins = te.matmul(o, states[r:r + 64, c, P * f:P * f + P], e[r:r + 64, f, P * c:P * c + P],
                                            start=False, stop=True)
                        a["out"].by(ins)
                    for h in range(HEADS):
                        wait(pe, "squared", h + 1)
                        a["sums"].by(te.matmul(banks[:, 4 + h, :], C("ones"), squares[:, h, :], start=True, stop=True))

    def sparse_attention(qa, ka, va, mask, oT):
        with ExitStack() as ctx:
            squares = sb(ctx, "dsa_squares", [P, 8, SEQ])
            bias = sb(ctx, "dsa_bias", [P, A_HEADS, 2, P])
            vec = sb(ctx, "dsa_vec", [A_HEADS, 3 * P])
            far = sb(ctx, "dsa_far", [A_HEADS, 1])
            rel = sb(ctx, "dsa_rel", [N_BUCKETS, A_HEADS])
            scratch = nc.dram_tensor("bias_by_distance", (A_HEADS, P, 3 * P), F32, kind="Internal")
            a = {s: sig("dsa_" + s) for s in ("rel", "rel_made", "vec", "kept", "bias", "squared", "sums", "logged", "factor", "normed")}
            a0 = {s: x.count for s, x in a.items()}

            def wait(engine, s, n):
                if n > 0:
                    engine.wait_ge(a[s].sem, a0[s] + n)

            both = [(x, f) for x in (qa, ka) for f in range(4)]
            with nc.Block() as block:
                @block.sync
                def _(sp):
                    a["rel"].by(sp.dma_start(rel[:], t["rel_bias"]), 16)
                    wait(sp, "vec", 1)
                    a["kept"].by(sp.dma_start(scratch.ap(), vec[:].unsqueeze(1).to_broadcast([A_HEADS, P, 3 * P])), 16)
                    wait(sp, "kept", 16)
                    for u in range(2):
                        src = bass.AP(scratch, 2 * P - 1 - P * u, [[3 * P - 1, P], [3 * P * P, A_HEADS], [1, P]])
                        a["bias"].by(sp.dma_start(bias[:, :, u, :], src), 16)

                @block.tensor
                def _(pe):
                    wait(pe, "rel", 16)
                    a["rel_made"].by(te.matmul(banks[0:A_HEADS, 7, 0:3 * P], rel[:], C("onehot", N_BUCKETS), start=True, stop=True))
                    for n in range(8):
                        wait(pe, "squared", n + 1)
                        wait(pe, "logged", n - 3)
                        a["sums"].by(te.matmul(banks[:, n % 4, :], C("pair"), squares[:, n, :], start=True, stop=True))

                @block.scalar
                def _(act):
                    for n, (x, f) in enumerate(both):
                        a["squared"].by(se.activation(squares[:, n, :], x[:, f, :], ACT.Square))
                    for n in range(8):
                        wait(act, "sums", n + 1)
                        a["logged"].by(se.activation(squares[:, n, :], banks[:, n % 4, :], ACT.Ln, bias=C("eps"),
                                                     scale=1.0 / A_DIM))
                    for n in range(8):
                        wait(act, "logged", 8)
                        a["factor"].by(factor_of(squares[:, n, :]))

                @block.vector
                def _(dve):
                    step = chained(dve, "dve_step")
                    wait(dve, "rel_made", 1)
                    step(ve.tensor_copy(vec[:], banks[0:A_HEADS, 7, 0:3 * P]))
                    step(ve.tensor_copy(far[:], vec[:, 0:1]))
                    a["vec"].by(ve.tensor_scalar(vec[:], vec[:], far[:], 8.0, ALU.subtract, ALU.mult))
                    for n, (x, f) in enumerate(both):
                        wait(dve, "factor", n + 1)
                        a["normed"].by(ve.scalar_tensor_tensor(x[:, f, :], x[:, f, :], G("qn2" if n < 4 else "kn2"),
                                                               squares[:, n, :], ALU.mult, ALU.mult))

            units = [(h, i) for h in range(A_HEADS) for i in range(QT)]
            probs = sb(ctx, "dsa_probs", [P, 2, SEQ])
            pT = sb(ctx, "dsa_pT", [P, 2, QT, P])
            stat = sb(ctx, "dsa_stat", [P, 4, len(units)])
            s = {x: sig("att_" + x) for x in ("scored", "max", "exp", "probs", "turned", "moved", "out", "stored")}
            s0 = {x: y.count for x, y in s.items()}

            def waits(engine, x, n):
                if n > 0:
                    engine.wait_ge(s[x].sem, s0[x] + n)

            with nc.Block() as block:
                @block.tensor
                def _(pe):
                    wait(pe, "bias", 32)

                    def scores(n):
                        h, i = units[n]
                        waits(pe, "max", n - 1)
                        r, f, keys = slice(64 * (h % 2), 64 * (h % 2) + 64), h // 2, P * (i + 1)
                        o = banks[:, n % 2, 0:keys]
                        te.matmul(o, qa[r, f, P * i:P * i + P], ka[r, f, 0:keys], start=True, stop=True)
                        for u in range(min(2, i + 1)):
                            c = P * (i - u)
                            ins = te.matmul(banks[:, n % 2, c:c + P], C("ident"), bias[:, h, u, :], start=False, stop=True,
                                            skip_group_check=True)
                        s["scored"].by(ins)

                    def turn(n):
                        h, i = units[n]
                        waits(pe, "probs", n + 1)
                        waits(pe, "moved", n - 1)
                        for j in range(i + 1):
                            ins = te.transpose(banks[:, 2 + n % 2, P * j:P * j + P], probs[:, n % 2, P * j:P * j + P], C("ident"))
                        s["turned"].by(ins)

                    def weigh(n):
                        h, i = units[n]
                        waits(pe, "moved", n + 1)
                        waits(pe, "stored", n - 1)
                        o = banks[64 * (h % 2):64 * (h % 2) + 64, 4 + n % 2, 0:P]
                        for j in range(i + 1):
                            ins = te.matmul(o, va[:, j, A_DIM * h:A_DIM * h + A_DIM], pT[:, n % 2, j, :], start=j == 0, stop=j == i)
                        s["out"].by(ins)

                    for n in range(len(units) + 2):
                        if n < len(units):
                            scores(n)
                        if n >= 2:
                            weigh(n - 2)
                        if 1 <= n <= len(units):
                            turn(n - 1)

                @block.vector
                def _(dve):
                    step = chained(dve, "dve_step")
                    for n in range(len(units) + 2):
                        if n >= 2:
                            h, i = units[n - 2]
                            waits(dve, "turned", n - 1)
                            waits(dve, "out", n - 3)
                            s["moved"].by(ve.tensor_copy(pT[:, n % 2, 0:i + 1, :],
                                                         banks[:, 2 + n % 2, 0:P * (i + 1)].rearrange("p (j t) -> p j t", t=P)))
                        if 1 <= n <= len(units):
                            h, i = units[n - 1]
                            waits(dve, "exp", n)
                            step(ve.reciprocal(stat[:, 3, n - 1:n], stat[:, 2, n - 1:n]))
                            x = probs[:, (n - 1) % 2, 0:P * (i + 1)]
                            s["probs"].by(ve.tensor_scalar(x, x, stat[:, 3, n - 1:n], None, ALU.mult))
                        if n < len(units):
                            h, i = units[n]
                            waits(dve, "scored", n + 1)
                            waits(dve, "turned", n - 1)
                            keys = P * (i + 1)
                            m = mask[:, i - 1, 0:keys] if i else C("causal")
                            step(ve.tensor_tensor_reduce(probs[:, n % 2, 0:keys], banks[:, n % 2, 0:keys], m, A_DIM ** -0.5,
                                                         -3e38, ALU.add, ALU.max, stat[:, 0, n:n + 1]))
                            s["max"].by(ve.tensor_scalar(stat[:, 1, n:n + 1], stat[:, 0, n:n + 1], -1.0, None, ALU.mult))

                @block.scalar
                def _(act):
                    for n in range(len(units) + 2):
                        if n < len(units):
                            h, i = units[n]
                            waits(act, "max", n + 1)
                            x = probs[:, n % 2, 0:P * (i + 1)]
                            s["exp"].by(se.activation(x, x, ACT.Exp, bias=stat[:, 1, n:n + 1], accum_out=stat[:, 2, n:n + 1]))
                        if n >= 2:
                            h, i = units[n - 2]
                            r = slice(64 * (h % 2), 64 * (h % 2) + 64)
                            waits(act, "out", n - 1)
                            s["stored"].by(se.copy(oT[r, h // 2, P * i:P * i + P], banks[r, 4 + n % 2, 0:P]))

    SLOTS = CHUNK
    PAIRS, QUADS = EXPERTS // 2, EXPERTS // 4
    PASSES = SEQ // SLOTS

    def expert_weights(sp, src, quad, slot, dst, s):
        e, rows = 4 * quad + slot, src.shape[1]
        x = src[e] if isinstance(e, int) else src.rearrange("e a b -> (e a) b")[bass.ds(e * rows, rows), :]
        sp.dma_start(dst, x.rearrange("(k p) n -> p k n", p=P)).then_inc(s[slot].sem, 16)

    def mixture():
        with ExitStack() as ctx:
            wdn = sb(ctx, "moe_down", [P, 4, 2, D])
            xtok = sb(ctx, "moe_x", [P, QT, D])
            w_r = sb(ctx, "moe_router", [P, KT, GROUPS + EXPERTS])
            b_r = sb(ctx, "moe_router_bias", [GROUPS + EXPERTS, 1])
            router_in = sig("moe_router")

            def load_router(sp):
                for c, w, b in ((slice(0, GROUPS), t["w_router_group"], t["b_router_group"]),
                                (slice(GROUPS, None), t["w_router_expert"], t["b_router_expert"])):
                    router_in.by(sp.dma_start(w_r[:, :, c], w.rearrange("(k p) n -> p k n", p=P)), 16)
                    router_in.by(sp.dma_start(b_r[c, :], b.rearrange("a n -> n a")), 16)

            norm("norm2", [(0, SEQ)], load_router)
            pick = [sb(ctx, f"router_pick{n}", [P, QT, EXPERTS]) for n in range(2)]
            both = sb(ctx, "router_both", [P, QT, EXPERTS])
            pos = sb(ctx, "router_pos", [P, QT, EXPERTS])
            count = sb(ctx, "router_count", [P, EXPERTS])
            rowf = sb(ctx, "router_row", [P, QT, 2])
            rowt = sb(ctx, "router_row_tmp", [P, QT])
            morf = sb(ctx, "router_more", [P, 1])
            rowi = sb(ctx, "moe_row", [P, QT, 2], I32)
            turn = sb(ctx, "moe_turn", [P, QT, 2])
            gate = sb(ctx, "moe_gate", [P, QT, 2])
            place = sb(ctx, "moe_place", [P, QT, EXPERTS])
            more = sb(ctx, "moe_more", [P, 1], I32)
            hn = nc.dram_tensor("moe_tokens", (SEQ, D), F32, kind="Internal")
            y = nc.dram_tensor("moe_results", (EXPERTS * SLOTS, D), F32, kind="Internal")
            a = {s: sig("moe_" + s) for s in ("turned", "moved", "scored", "biased", "logits", "chosen", "counted", "hn_kept",
                                              "exps")}
            a0 = {s: x.count for s, x in a.items()}
            in_loaded = [sig(f"expert_in_loaded{i}") for i in range(4)]
            down_loaded = [sig(f"expert_down_loaded{i}") for i in range(4)]

            def load_in(sp, quad, slot):
                expert_weights(sp, t["w_exp_gate"], quad, slot, wbuf[slot][:, :, 0:D_EXPERT], in_loaded)
                expert_weights(sp, t["w_exp_up"], quad, slot, wbuf[slot][:, :, D_EXPERT:], in_loaded)

            def load_down(sp, quad, slot):
                expert_weights(sp, t["w_exp_down"], quad, slot, wdn[:, slot], down_loaded)

            def wait(engine, s, n):
                if n > 0:
                    engine.wait_ge(a[s].sem, a0[s] + n)

            turns = [(x, i, b_) for x in range(2) for i in range(QT) for b_ in range(2)]
            L = GROUPS + EXPERTS
            with ExitStack() as rc:
                utok = sb(rc, "moe_utok", [P, QT, D])
                lgT = sb(rc, "router_logits_T", [L, SEQ])
                lg = sb(rc, "router_logits", [P, QT, L])
                t4 = [sb(rc, f"router_g{n}", [P, QT, GROUPS]) for n in range(4)]
                t8 = [sb(rc, f"router_e{n}", [P, QT, PER_GROUP]) for n in range(4)]
                t32 = sb(rc, "router_ge", [P, QT, GROUPS, PER_GROUP])
                c1 = [sb(rc, f"router_c{n}", [P, QT]) for n in range(6)]
                with nc.Block() as block:
                    @block.sync
                    def _(sp):
                        sp.wait_ge(*job_done[J["out2"][1]])
                        for slot in range(4):
                            if slot == 2:
                                wait(sp, "moved", 2 * QT + 1)
                            load_in(sp, 0, slot)
                            load_down(sp, 0, slot)
                        wait(sp, "hn_kept", 16 * QT)

                    @block.tensor
                    def _(pe):
                        pe.wait_ge(router_in.sem, router_in.count)
                        for k in range(KT):
                            ins = te.matmul(banks[0:L, 7, :], w_r[:, k, :], uT[:, k, 0:SEQ], start=k == 0, stop=k == KT - 1)
                        a["scored"].by(ins)

                        def turn_tiles(some):
                            for n in some:
                                x, i, b_ = turns[n]
                                wait(pe, "moved", n - 3)
                                for k in range(4):
                                    ins = te.transpose(banks[:, n % 4, P * k:P * k + P],
                                                       (uT, hT)[x][:, 4 * b_ + k, P * i:P * i + P], C("ident"))
                                a["turned"].by(ins)

                        turn_tiles(range(2))
                        wait(pe, "biased", 1)
                        for i in range(QT):
                            ins = te.transpose(banks[:, 5, L * i:L * i + L], lgT[:, P * i:P * i + P], C("ident", L, L))
                        a["logits"].by(ins)
                        turn_tiles(range(2, 2 * QT))
                        wait(pe, "chosen", 1)
                        for i in range(QT):
                            for j in range(i + 1):
                                ins = te.matmul(banks[:, 6, EXPERTS * i:EXPERTS * i + EXPERTS], C("tri") if j == i else C("ones"),
                                                both[:, j, :], start=j == 0, stop=j == i)
                        for j in range(QT):
                            ins = te.matmul(banks[:, 6, EXPERTS * QT:EXPERTS * QT + EXPERTS], C("ones"), both[:, j, :],
                                            start=j == 0, stop=j == QT - 1)
                        a["counted"].by(ins)
                        turn_tiles(range(2 * QT, 4 * QT))

                    @block.scalar
                    def _(act):
                        wait(act, "scored", 1)
                        a["biased"].by(se.activation(lgT[:], banks[0:L, 7, :], ACT.Identity, bias=b_r[:]))
                        for n, (x, i, b_) in enumerate(turns):
                            if n == 2 * QT:
                                wait(act, "chosen", 1)
                                a["exps"].by(se.activation(t4[3][:], t4[3][:], ACT.Exp))
                                a["exps"].by(se.activation(c1[4][:], c1[4][:], ACT.Exp))
                            wait(act, "turned", n + 1)
                            a["moved"].by(se.copy((utok, xtok)[x][:, i, 512 * b_:512 * b_ + 512], banks[:, n % 4, :]))
                            if (x, b_) == (0, 1):
                                wait(act, "moved", n + 1)
                                a["hn_kept"].by(act.dma_start(hn.ap()[P * i:P * i + P, :], utok[:, i, :]), 16)

                    @block.vector
                    def _(dve):
                        step = chained(dve, "dve_step")
                        tt = lambda o, x, z, op: step(ve.tensor_tensor(o, x, z, op))
                        wait(dve, "logits", 1)
                        step(ve.tensor_copy(lg[:], banks[:, 5, 0:QT * L].rearrange("p (i l) -> p i l", i=QT)))

                        def first_largest(x, ids, m, eq, one, n):
                            step(ve.tensor_reduce(m[:], x, AX, ALU.max))
                            tt(eq, x, m[:].unsqueeze(2).to_broadcast([P, QT, n]), ALU.is_equal)
                            tt(eq, eq, ids.unsqueeze(1).to_broadcast([P, QT, n]), ALU.mult)
                            step(ve.tensor_reduce(c1[5][:], eq, AX, ALU.max))
                            tt(one, eq, c1[5][:].unsqueeze(2).to_broadcast([P, QT, n]), ALU.is_equal)

                        G_, E_ = lg[:, :, 0:GROUPS], lg[:, :, GROUPS:]
                        gmax, m1, m2, x5 = c1[0], c1[1], c1[2], c1[4]
                        first_largest(G_, C("down")[:, 0:GROUPS], gmax, t4[0][:], t4[1][:], GROUPS)
                        group = t4[1]
                        tt(t4[3][:], G_, gmax[:].unsqueeze(2).to_broadcast([P, QT, GROUPS]), ALU.subtract)
                        tt(t32[:], E_.rearrange("p i (g e) -> p i g e", g=GROUPS),
                           group[:].unsqueeze(3).to_broadcast([P, QT, GROUPS, PER_GROUP]), ALU.mult)
                        step(ve.tensor_reduce(t8[0][:], t32[:].rearrange("p i g e -> p i e g"), AX, ALU.add))
                        first_largest(t8[0][:], C("down"), m1, t8[1][:], t8[2][:], PER_GROUP)
                        step(ve.scalar_tensor_tensor(t8[0][:], t8[2][:], NEG, t8[0][:], ALU.mult, ALU.add))
                        first_largest(t8[0][:], C("down"), m2, t8[1][:], t8[3][:], PER_GROUP)
                        for n, o in enumerate((t8[2], t8[3])):
                            tt(pick[n][:].rearrange("p i (g e) -> p i g e", g=GROUPS),
                               group[:].unsqueeze(3).to_broadcast([P, QT, GROUPS, PER_GROUP]),
                               o[:].unsqueeze(2).to_broadcast([P, QT, GROUPS, PER_GROUP]), ALU.mult)
                        tt(both[:], pick[0][:], pick[1][:], ALU.add)
                        a["chosen"].by(ve.tensor_tensor(x5[:], m2[:], m1[:], ALU.subtract))
                        wait(dve, "exps", 2)
                        step(ve.tensor_reduce(c1[3][:], t4[3][:], AX, ALU.add))
                        step(ve.tensor_scalar(m1[:], x5[:], 1.0, None, ALU.add))
                        tt(m1[:], m1[:], c1[3][:], ALU.mult)
                        step(ve.reciprocal(m1[:], m1[:]))
                        step(ve.tensor_copy(gate[:, :, 0], m1[:]))
                        tt(gate[:, :, 1], m1[:], x5[:], ALU.mult)
                        wait(dve, "counted", 1)
                        step(ve.tensor_copy(pos[:], banks[:, 6, 0:QT * EXPERTS].rearrange("p (i e) -> p i e", i=QT)))
                        step(ve.tensor_copy(count[:], banks[:, 6, QT * EXPERTS:(QT + 1) * EXPERTS]))
                        step(ve.scalar_tensor_tensor(place[:], pos[:], 1.0, both[:], ALU.add, ALU.mult))
                        step(ve.tensor_scalar(place[:], place[:], -1.0, None, ALU.add))

            with ExitStack() as ec:
                slot_oh = sb(ec, "moe_slot_onehot", [P, 2, EXPERTS, SLOTS], FR)
                tokid = sb(ec, "moe_token", [P, QT, 2], FR)
                idx = sb(ec, "moe_idx", [P, PAIRS], I32)
                cur = sb(ec, "moe_cur", [P, 2, 1], I32)
                xg = sb(ec, "moe_gathered", [P, 2, D])
                xT = sb(ec, "moe_xT", [P, KT, P])
                sl = sb(ec, "moe_silu", [P, D_EXPERT])
                hid = sb(ec, "moe_hidden", [P, D_EXPERT])
                hT2 = sb(ec, "moe_hidden_turned", [P, 2, P])
                yt = sb(ec, "moe_y", [P, 2, D])
                held = sig("moe_held")
                gate_p = sb(ec, "moe_gate_of_pass", [P, QT, 2])
                per = {"onehot": QT, "listed": QT, "idx": 1, "cur": PAIRS, "gathered0": 8 * PAIRS,
                       "gathered1": 8 * PAIRS, "turned": 2 * PAIRS, "xT": 2 * PAIRS, "up": PAIRS, "silu": PAIRS,
                       "hidden": PAIRS, "hid_turned": PAIRS, "hid_moved": PAIRS, "down": PAIRS, "moved": 2 * PAIRS,
                       "stored0": 8 * PAIRS, "stored1": 8 * PAIRS,
                       "back0": 16 * QT, "back1": 16 * QT, "gates": 2, "shifted": 2, "added0": QT, "added": QT, "numbered": 0,
                       "rows": 0}
                m = {s: sig("exp_" + s) for s in per}

                written = sig("out_written")
                tokens_in_dram = a["hn_kept"].sem, a["hn_kept"].count

                def at(engine, p, s, n):
                    engine.wait_ge(m[s].sem, p * per[s] + n)

                def inc(ins, s, n=1):
                    ins.then_inc(m[s].sem, n)

                def passes(engine, one):
                    one(0)
                    engine.wait_ge(m["rows"].sem, 1)
                    n = engine.value_load(more[0:1, 0:1], min_val=0, max_val=PASSES - 1)
                    with engine.If(n):
                        with engine.Fori(1, n + 1) as p:
                            one(p)
                    return n

                with nc.Block() as block:
                    @block.sync
                    def _(sp):
                        def one(p):
                            def load(i):
                                for b in range(2):
                                    for slot in (2 * b, 2 * b + 1):
                                        at(sp, p, "up", 2 * i + b - 1)
                                        load_in(sp, i, slot)
                                    for slot in (2 * b, 2 * b + 1):
                                        at(sp, p, "down", 2 * i + b - 1)
                                        load_down(sp, i, slot)

                            if not isinstance(p, int):
                                load(0)
                            with sp.Fori(1, QUADS) as i:
                                load(i)
                        last = passes(sp, one)
                        for i in range(QT):
                            at(sp, last, "added", i + 1)
                            written.by(sp.dma_start(out[0, P * i:P * i + P, :], xtok[:, i, :]), 16)
                        sp.wait_ge(written.sem, written.count)

                    @block.gpsimd
                    def _(pool):
                        def hold():
                            pool.sem_inc(held.sem, 1)

                        def one(p):
                            at(pool, p, "idx", 1)
                            hold()

                            def gather(i, b):
                                inc(ge.tensor_copy(cur[:, b, :], idx[:, bass.ds(2 * i + b, 1)]), "cur")
                                at(pool, p, "cur", 2 * i + b + 1)
                                hold()
                                g = pool.indirect_dma_start(xg[:, b, :], None, hn.ap(),
                                                            bass.IndirectOffsetOnAxis(ap=cur[:, b, :], axis=0))
                                inc(g, f"gathered{b}", 16)

                            gather(0, 0)
                            gather(0, 1)
                            with pool.Fori(1, QUADS) as i:
                                for b in range(2):
                                    at(pool, p, "turned", 4 * i + 2 * b - 2)
                                    hold()
                                    gather(i, b)
                            at(pool, p, "turned", 4 * QUADS)
                            hold()
                            pool.wait_ge(m["rows"].sem, 1)
                            for b in range(2):
                                at(pool, p, f"stored{b}", 16 + 8 * PAIRS)
                            for i in range(QT):
                                b = i % 2
                                if i >= 2:
                                    at(pool, p, "added", i - 1)
                                hold()
                                for n, o in enumerate((xg, yt)):
                                    g = pool.indirect_dma_start(o[:, b, :], None, y.ap(),
                                                                bass.IndirectOffsetOnAxis(ap=rowi[:, i, n:n + 1], axis=0))
                                    inc(g, f"back{b}", 16)
                            at(pool, p, "added", QT)
                            hold()
                        passes(pool, one)

                    @block.vector
                    def _(dve):
                        step = chained(dve, "dve_step")
                        tt = lambda o, x, z, op: step(ve.tensor_tensor(o, x, z, op))

                        def rows():
                            for n in range(2):
                                tt(both[:], pos[:], pick[n][:], ALU.mult)
                                step(ve.tensor_reduce(rowf[:, :, n], both[:], AX, ALU.add))
                                tt(pick[n][:], pick[n][:], C("eids").unsqueeze(1).to_broadcast([P, QT, EXPERTS]), ALU.mult)
                            step(ve.tensor_scalar(turn[:], rowf[:], float(SLOTS), None, ALU.is_ge))
                            for p in range(2, PASSES):
                                step(ve.scalar_tensor_tensor(turn[:], rowf[:], float(SLOTS * p), turn[:], ALU.is_ge, ALU.add))
                            step(ve.scalar_tensor_tensor(rowf[:], turn[:], -float(SLOTS), rowf[:], ALU.mult, ALU.add))
                            for n in range(2):
                                step(ve.tensor_reduce(rowt[:], pick[n][:], AX, ALU.add))
                                step(ve.scalar_tensor_tensor(rowf[:, :, n], rowt[:], float(SLOTS), rowf[:, :, n], ALU.mult, ALU.add))
                            step(ve.tensor_copy(rowi[:], rowf[:]))
                            step(ve.tensor_reduce(rowt[:, 0:1], count[:], AX, ALU.max))
                            step(ve.tensor_scalar(morf[:], rowt[:, 0:1], float(SLOTS + 1), None, ALU.is_ge))
                            for p in range(2, PASSES):
                                step(ve.scalar_tensor_tensor(morf[:], rowt[:, 0:1], float(SLOTS * p + 1), morf[:], ALU.is_ge, ALU.add))
                            inc(ve.tensor_copy(more[:], morf[:]), "rows")

                        def one(p):
                            if not isinstance(p, int):
                                inc(ve.tensor_scalar(place[:], place[:], -float(SLOTS), None, ALU.add), "shifted")
                                inc(ve.tensor_scalar(turn[:], turn[:], -1.0, None, ALU.add), "shifted")
                                at(dve, p, "shifted", 0)
                            for i in range(QT):
                                if i > 1:
                                    at(dve, p, "listed", i - 1)
                                inc(ve.tensor_tensor(slot_oh[:, i % 2], C("slot").unsqueeze(1).to_broadcast([P, EXPERTS, SLOTS]),
                                                     place[:, i, :].unsqueeze(2).to_broadcast([P, EXPERTS, SLOTS]), ALU.is_equal),
                                    "onehot")
                            at(dve, p, "listed", QT)
                            inc(ve.tensor_copy(idx[:], banks[:, 7, 0:2 * PAIRS].rearrange("p (n u) -> p n u", u=2)[:, :, 0]), "idx")
                            if isinstance(p, int):
                                rows()
                            inc(ve.tensor_scalar(gate_p[:], turn[:], 0.0, None, ALU.is_equal), "gates")
                            at(dve, p, "gates", 1)
                            inc(ve.tensor_tensor(gate_p[:], gate_p[:], gate[:], ALU.mult), "gates")
                            with dve.Fori(0, QUADS) as i:
                                for b in range(2):
                                    for h in range(2):
                                        at(dve, p, "turned", 4 * i + 2 * b + h + 1)
                                        inc(ve.tensor_copy(xT[:, 4 * h:4 * h + 4, :],
                                                           banks[:, h, :].rearrange("p (k t) -> p k t", k=4)), "xT")
                                    at(dve, p, "silu", 2 * i + b + 1)
                                    inc(ve.tensor_tensor(hid[:], sl[:], banks[:, 2 + b, D_EXPERT:], ALU.mult), "hidden")
                                    at(dve, p, "hid_turned", 2 * i + b + 1)
                                    inc(ve.tensor_copy(hT2[:], banks[:, 6, 0:2 * P].rearrange("p (f t) -> p f t", f=2)),
                                        "hid_moved")
                            at(dve, p, "gates", 2)
                            for i in range(QT):
                                b = i % 2
                                at(dve, p, f"back{b}", 32 * (i // 2 + 1))
                                for n, (o, s) in enumerate(((xg, "added0"), (yt, "added"))):
                                    inc(ve.scalar_tensor_tensor(xtok[:, i, :], o[:, b, :], gate_p[:, i, n:n + 1],
                                                                xtok[:, i, :], ALU.mult, ALU.add), s)
                                    at(dve, p, s, i + 1)
                        inc(ve.tensor_copy(tokid[:], C("tokid").unsqueeze(2).to_broadcast([P, QT, 2])), "numbered")
                        passes(dve, one)

                    @block.tensor
                    def _(pe):
                        def one(p):
                            for i in range(QT):
                                at(pe, p, "onehot", i + 1)
                                for n in range(PAIRS):
                                    ins = te.matmul(banks[:, 7, 2 * n:2 * n + 2],
                                                    slot_oh[:, i % 2, 2 * n:2 * n + 2, :].rearrange("p e s -> p (e s)"),
                                                    tokid[:, i, :], start=i == 0 and n == 0, stop=i == QT - 1,
                                                    skip_group_check=True)
                                inc(ins, "listed")
                            with pe.Fori(0, QUADS) as i:
                                for b in range(2):
                                    at(pe, p, f"gathered{b}", 16 * i + 16)
                                    for h in range(2):
                                        for k in range(4):
                                            ins = te.transpose(banks[:, h, P * k:P * k + P],
                                                               xg[:, b, P * (4 * h + k):P * (4 * h + k) + P], C("ident"))
                                        inc(ins, "turned")
                                    at(pe, p, "xT", 4 * i + 2 * b + 2)
                                    for h in range(2):
                                        pe.wait_ge(in_loaded[2 * b + h].sem, p * 32 * QUADS + 32 * i + 32)
                                    for k in range(KT):
                                        for h in range(2):
                                            r = slice(SLOTS * h, SLOTS * h + SLOTS)
                                            ins = te.matmul(banks[r, 2 + b, :], xT[:, k, r], wbuf[2 * b + h][:, k, :],
                                                            start=k == 0, stop=k == KT - 1)
                                    inc(ins, "up")
                                    at(pe, p, "hidden", 2 * i + b + 1)
                                    for f in range(2):
                                        ins = te.transpose(banks[:, 6, P * f:P * f + P], hid[:, P * f:P * f + P], C("ident"))
                                    inc(ins, "hid_turned")
                                    at(pe, p, "hid_moved", 2 * i + b + 1)
                                    at(pe, p, "moved", 4 * i + 2 * b + 2)
                                    for h in range(2):
                                        pe.wait_ge(down_loaded[2 * b + h].sem, p * 16 * QUADS + 16 * i + 16)
                                    for f in range(2):
                                        for c in range(2):
                                            for h in range(2):
                                                r = slice(SLOTS * h, SLOTS * h + SLOTS)
                                                ins = te.matmul(banks[r, 4 + c, :], hT2[:, f, r],
                                                                wdn[:, 2 * b + h, f, 512 * c:512 * c + 512],
                                                                start=f == 0, stop=f == 1)
                                    inc(ins, "down")
                        pe.wait_ge(m["numbered"].sem, 1)
                        passes(pe, one)

                    @block.scalar
                    def _(act):
                        def one(p):
                            if not isinstance(p, int):
                                at(act, p, "added", 0)
                                act.wait_ge(*tokens_in_dram)
                            with act.Fori(0, QUADS) as i:
                                for b in range(2):
                                    at(act, p, "up", 2 * i + b + 1)
                                    inc(se.activation(sl[:], banks[:, 2 + b, 0:D_EXPERT], ACT.Silu), "silu")
                                    at(act, p, "down", 2 * i + b + 1)
                                    at(act, p, f"stored{b}", 16 * i + 16)
                                    for c in range(2):
                                        inc(se.copy(yt[:, b, 512 * c:512 * c + 512], banks[:, 4 + c, :]), "moved")
                                    at(act, p, "moved", 4 * i + 2 * b + 4)
                                    inc(act.dma_start(y.ap()[bass.ds((2 * i + b) * P, P), :], yt[:, b, :]),
                                        f"stored{b}", 16)
                        for b in range(2):
                            act.sem_inc(m[f"stored{b}"].sem, 16)
                        act.sem_inc(m["moved"].sem, 2)
                        passes(act, one)

    w_in, w2 = t["w_in"], t["w_in_2"]
    J = {}
    for name, c in (("hq", 0), ("hf", 512), ("hi", 1024), ("hg", 1536), ("cq", 2048)):
        J[name] = job(w_in[:, c:c + 512])
    J["kr"] = job(w_in[:, 2560:2624])
    J["q_up"] = job(t["w_q_up"][:, 0:512], Q_RANK), job(t["w_q_up"][:, 512:768], Q_RANK)
    J["kv_up"] = job(t["w_kv_up"][:, 0:512], KV_RANK), job(t["w_kv_up"][:, 512:1024], KV_RANK)
    J["out"] = job(t["w_out"][:, 0:512]), job(t["w_out"][:, 512:1024])
    J["mlp0"] = mlp_jobs(t["w_mlp_up"][0])
    J["pool"] = job(t["pool_w"].rearrange("g c e -> (g c) e"))
    J["mlp1"] = mlp_jobs(t["w_mlp_up"][1])
    for name, c, n in (("idx", O_IQ, 296), ("qkb", O_QB, 512), ("lr", O_LR, GATE_RANK), ("vb", O_VB, 512), ("rg", O_RG, 512),
                       ("qa", O_QA, 512), ("ka", O_KA, 512), ("va", O_VA, 512)):
        J[name] = job(w2[:, c:c + n])
    J["out2"] = job(t["w_out_2"][:, 0:512]), job(t["w_out_2"][:, 512:1024])

    with root:
        open_late()
        load_input()
        norm("mix0", HALVES)
        output = ExitStack()
        oT = sb(output, "oT", [P, KT, TOK])
        mixer0 = ExitStack()
        q = sb(mixer0, "q", [P, HEADS, TOK])
        k_ = sb(mixer0, "k", [P, HEADS, TOK])
        sg = sb(mixer0, "sg", [P, HEADS, TOK])
        cT = sb(mixer0, "cT", [P, 4, TOK])
        krT = sb(mixer0, "krT", [ROPE, TOK])
        v = sb(mixer0, "v", [P, QT + 1, 512])
        within = ExitStack()
        b, qd, kd = (sb(within, n, [P, HEADS, TOK]) for n in ("hgrn_b", "hgrn_qd", "hgrn_kd"))
        att = sb(within, "hgrn_att", [P, HEADS * QT, P])
        att_meta = sb(within, "hgrn_att_meta", [META, HEADS, META])[:]
        project_in(q, k_, sg, cT, krT, v, b, qd, kd, att, att_meta, oT)
        hgrn(q, k_, sg, v, b, qd, kd, att, att_meta, oT)
        within.close()
        kr = sb(mixer0, "kr", [ROPE, HEADS, TOK])
        qr = sg[0:ROPE]
        mla_heads(q, k_, qr, kr, krT, cT, v)
        mla_attention(q, k_, qr, kr[:], v, oT)
        mixer0.close()
        project_out(oT, J["out"], HALVES, J["mlp0"] + 2)
        output.close()
        mlp(J["mlp0"], "mlp0", t["w_mlp_up"][0], t["w_mlp_down"][0], HALVES)
        norm("mix1", HALVES)
        pool_mixer(J["mlp1"] + 2)
        mlp(J["mlp1"], "mlp1", t["w_mlp_up"][1], t["w_mlp_down"][1], REAL)
        norm("norm1", [(0, SEQ)])
        mixer1 = ExitStack()
        qa, ka, va, vb, rg = (sb(mixer1, n, [P, 4, SEQ]) for n in ("qa", "ka", "va", "vb", "rg"))
        qb, kb = (sb(mixer1, n, [P, 2, SEQ]) for n in ("qb", "kb"))
        lr = sb(mixer1, "lr", [GATE_RANK, SEQ])
        mask = sb(mixer1, "mask", [P, QT - 1, SEQ])
        within = ExitStack()
        b, diff, e, qd, kd = (sb(within, "gla_" + n, [P, 2, SEQ]) for n in ("b", "diff", "e", "qd", "kd"))
        att = sb(within, "gla_att", [P, HEADS * QT, P])
        idx = ExitStack()
        iq = sb(idx, "iq", [P, 2, SEQ])
        ik = sb(idx, "ik", [P, SEQ])
        iw = sb(idx, "iw", [P, QT, IDX_HEADS])
        project_in2(qa, ka, va, iq, ik, iw, qb, kb, vb, lr, rg, mask, b, diff, e, qd, kd, att)
        idx.close()
        gla(qb, kb, vb, rg, b, diff, e, qd, kd, att, uT)
        within.close()
        sparse_attention(qa, ka, va, mask, uT)
        mixer1.close()
        project_out(uT, J["out2"], [(0, SEQ)], 0)
        mixture()
        late.close()


_NAMES = ("x", "meta_tokens", "mix_norm", "mlp_norm", "w_mlp_up", "w_mlp_down", "w_in", "hgrn_lb", "hgrn_out_norm",
          "mla_q_a_norm", "mla_kv_a_norm", "w_q_up", "w_kv_up", "q_norm", "k_norm", "w_out", "pool_w", "pool_scale",
          "norm1_g_2", "w_in_2", "q_norm_g_2", "k_norm_g_2", "rel_bias_2", "gla_gate_w2_2", "gla_gate_b_2",
          "gla_out_norm_g_2", "w_out_2", "norm2_g_2", "w_router_group_2", "b_router_group_2", "w_router_expert_2",
          "b_router_expert_2", "w_exp_gate_2", "w_exp_up_2", "w_exp_down_2")
_LEADING_ONE = ("w_in", "w_q_up", "w_kv_up", "w_out", "pool_w", "w_in_2", "gla_gate_w2_2", "w_out_2",
                "w_router_group_2", "w_router_expert_2", "w_exp_gate_2", "w_exp_up_2", "w_exp_down_2")
_KEEP_SUFFIX = ("w_in_2", "w_out_2")


def kernel(**inputs):
    import concourse.bacc as bacc
    from concourse import mybir
    from concourse.bass_utils import run_bass_kernel_spmd

    nc = bacc.Bacc("TRN2", target_bir_lowering=False, num_devices=1)
    arrays, t = {}, {}
    for name in _NAMES:
        a = np.ascontiguousarray(inputs[name])
        arrays["in_" + name] = a
        ap = nc.dram_tensor("in_" + name, a.shape, mybir.dt.from_np(a.dtype), kind="ExternalInput").ap()
        if name in _LEADING_ONE:
            ap = ap[0]
        t[name if name in _KEEP_SUFFIX else name.removesuffix("_2")] = ap
    arrays["constants"] = constant_table()
    t["constants"] = nc.dram_tensor("constants", (P, CONSTS), mybir.dt.float32, kind="ExternalInput").ap()
    arrays["level_masks"] = level_masks()
    t["level_masks"] = nc.dram_tensor("level_masks", (P, P * 8), mybir.dt.float32, kind="ExternalInput").ap()
    out = nc.dram_tensor("out", (1, SEQ, D), mybir.dt.float32, kind="ExternalOutput").ap()
    program(nc, t, out)
    r = run_bass_kernel_spmd(nc, [arrays], core_ids=[0])
    return r.results[0]["out"]
```
